# Optimizing a Trainium2 kernel written in Bass

```python
import jax
import jax.numpy as jnp
from jax import lax
import numpy as np

D_MODEL = 1024
BATCH = 1
SEQ = 512
DEPTH = 1
DEC_BATCH = 8
DEC_SEQ = 8
PAST_LEN = 512
PAGE_SIZE = 128

A_HEADS = 8
A_HEAD_DIM = 64
A_WIDTH = A_HEADS * A_HEAD_DIM
Q_BLOCK = 128
M_HEADS = 4
M_HEAD_DIM = 128
M_WIDTH = M_HEADS * M_HEAD_DIM
M_CHUNK = 64
C_WIDTH = 512
CONV_W = 3
D_FF = 2816
PLE_DIM = 256
EPS = 1e-6
SPARE_DIV = 4

IN_COLS = (
    ("a_q", A_WIDTH), ("a_k", A_WIDTH), ("a_v", A_WIDTH), ("a_f", A_HEADS),
    ("m_q", M_WIDTH), ("m_k", M_WIDTH), ("m_v", M_WIDTH), ("m_i", M_HEADS), ("m_f", M_HEADS), ("m_o", M_WIDTH),
    ("c_b", C_WIDTH), ("c_c", C_WIDTH), ("c_x", C_WIDTH),
    ("g_a", D_MODEL), ("g_m", D_MODEL), ("g_c", D_MODEL),
)
P_IN = 3 * A_WIDTH + A_HEADS + 4 * M_WIDTH + 2 * M_HEADS + 3 * C_WIDTH + 3 * D_MODEL

kernel_name = "fox_mlstm_shortconv_hybrid_step"

def _rmsnorm(x, g):
    xf = x.astype(jnp.float32)
    y = xf * lax.rsqrt(jnp.mean(xf * xf, axis=-1, keepdims=True) + EPS)
    return (y * g.astype(jnp.float32)).astype(x.dtype)

def _split_cols(z):
    bounds = np.cumsum([s for _, s in IN_COLS])[:-1].tolist()
    return jnp.split(z, bounds, axis=-1)

def _col_range(name):
    off = 0
    for n, s in IN_COLS:
        if n == name:
            return off, s
        off += s
    raise KeyError(name)

def _causal_dwconv(u, buf, w):
    t = u.shape[1]
    up = jnp.concatenate([buf.astype(u.dtype), u], axis=1)
    y = up[:, 0:t] * w[0]
    for j in range(1, CONV_W):
        y = y + up[:, j:j + t] * w[j]
    return y, up[:, up.shape[1] - (CONV_W - 1):]

def _gather_pages(pool, page_table, l):
    ps = pool.shape[1]
    g = pool[page_table[:, :, None], jnp.arange(ps)[None, None, :], l]
    return g.reshape((g.shape[0], g.shape[1] * ps) + g.shape[3:])

def _fox_prompt(q, k, v, logf):
    nb, t, h, dh = q.shape
    scale = dh ** -0.5
    cum = jnp.cumsum(logf, axis=1).transpose(0, 2, 1)
    n_blk = t // Q_BLOCK
    q_blk = q.reshape(nb, n_blk, Q_BLOCK, h, dh).swapaxes(0, 1)
    c_blk = cum.reshape(nb, h, n_blk, Q_BLOCK).transpose(2, 0, 1, 3)
    key_pos = jnp.arange(t)

    def block(args):
        i, q_i, c_i = args
        q_pos = i * Q_BLOCK + jnp.arange(Q_BLOCK)
        s = jnp.einsum("bqhd,bkhd->bhqk", q_i, k).astype(jnp.float32) * scale
        s = s + c_i[..., :, None] - cum[:, :, None, :]
        s = jnp.where(key_pos[None, :] <= q_pos[:, None], s, -jnp.inf)
        p = jax.nn.softmax(s, axis=-1).astype(v.dtype)
        return jnp.einsum("bhqk,bkhd->bqhd", p, v)

    out = lax.map(block, (jnp.arange(n_blk), q_blk, c_blk))
    return out.swapaxes(0, 1).reshape(nb, t, h * dh)

def _fox_sample(q, k_new, v_new, logf_new, k_past, v_past, logf_past):
    nb, s_len, h, dh = q.shape
    p_len = k_past.shape[1]
    scale = dh ** -0.5
    cum_past = jnp.cumsum(logf_past.astype(jnp.float32), axis=1)
    cum_new = cum_past[:, -1:] + jnp.cumsum(logf_new, axis=1)
    qc = cum_new.transpose(0, 2, 1)[..., None]
    s_past = jnp.einsum("bqhd,bkhd->bhqk", q, k_past.astype(q.dtype)).astype(jnp.float32) * scale
    s_past = s_past + qc - cum_past.transpose(0, 2, 1)[:, :, None, :]
    s_new = jnp.einsum("bqhd,bkhd->bhqk", q, k_new).astype(jnp.float32) * scale
    s_new = s_new + qc - cum_new.transpose(0, 2, 1)[:, :, None, :]
    causal = jnp.tril(jnp.ones((s_len, s_len), bool))
    s_new = jnp.where(causal, s_new, -jnp.inf)
    p = jax.nn.softmax(jnp.concatenate([s_past, s_new], axis=-1), axis=-1).astype(v_new.dtype)
    out = (jnp.einsum("bhqk,bkhd->bqhd", p[..., :p_len], v_past.astype(v_new.dtype))
           + jnp.einsum("bhqk,bkhd->bqhd", p[..., p_len:], v_new))
    return out.reshape(nb, s_len, h * dh)

def _mlstm(q, k, v, i_pre, logf, c0, n0, m0, chunk):
    f32 = jnp.float32
    nb, t, h, dk = q.shape
    dv = v.shape[-1]
    nc = t // chunk
    q = q.astype(f32)
    k = k.astype(f32) * (dk ** -0.5)
    v = v.astype(f32)

    def to_chunks(a):
        return a.reshape((nb, nc, chunk) + a.shape[2:]).swapaxes(0, 1)

    causal = jnp.tril(jnp.ones((chunk, chunk), bool))

    def step(carry, xs):
        c, n, m = carry
        q_c, k_c, v_c, i_c, f_c = xs
        big_f = jnp.cumsum(f_c, axis=1).transpose(0, 2, 1)
        it = i_c.transpose(0, 2, 1)
        d = big_f[..., :, None] - big_f[..., None, :] + it[..., None, :]
        d = jnp.where(causal, d, -jnp.inf)
        inter = m[..., None] + big_f
        m_t = jnp.maximum(inter, jnp.max(d, axis=-1))
        w = jnp.exp(d - m_t[..., None])
        a = jnp.exp(inter - m_t)
        wqk = w * jnp.einsum("blhd,bshd->bhls", q_c, k_c)
        num = (a[..., None] * jnp.einsum("bhvd,blhd->bhlv", c, q_c)
               + jnp.einsum("bhls,bshv->bhlv", wqk, v_c))
        den = a * jnp.einsum("bhd,blhd->bhl", n, q_c) + jnp.sum(wqk, axis=-1)
        h_t = num / jnp.maximum(jnp.abs(den), jnp.exp(-m_t))[..., None]
        w_last = w[..., -1, :]
        a_last = a[..., -1]
        c_new = a_last[..., None, None] * c + jnp.einsum("bhs,bshv,bshd->bhvd", w_last, v_c, k_c)
        n_new = a_last[..., None] * n + jnp.einsum("bhs,bshd->bhd", w_last, k_c)
        return (c_new, n_new, m_t[..., -1]), h_t.transpose(0, 2, 1, 3)

    xs = (to_chunks(q), to_chunks(k), to_chunks(v), to_chunks(i_pre), to_chunks(logf))
    (c1, n1, m1), hs = lax.scan(step, (c0.astype(f32), n0.astype(f32), m0.astype(f32)), xs)
    return hs.swapaxes(0, 1).reshape(nb, t, h, dv), c1, n1, m1

def _layer(x, pe, prm, past):
    (w_in, b_in, g_mix, g_mhead, w_sconv, w_oa, w_om, w_oc, w_o,
     g_ffn, w_up, w_fconv, b_fconv, w_down, g_ple, w_ple_gate, w_ple) = prm
    f32 = jnp.float32
    nb, t, _ = x.shape
    h = _rmsnorm(x, g_mix)
    z = h @ w_in + b_in
    (aq, ak, av, af, mq, mk, mv, mi, mf, mo, cb, cc, cx, ga, gm, gc) = _split_cols(z)
    aq = aq.reshape(nb, t, A_HEADS, A_HEAD_DIM)
    ak = ak.reshape(nb, t, A_HEADS, A_HEAD_DIM)
    av = av.reshape(nb, t, A_HEADS, A_HEAD_DIM)
    a_logf = jax.nn.log_sigmoid(af.astype(f32))
    mq = mq.reshape(nb, t, M_HEADS, M_HEAD_DIM)
    mk = mk.reshape(nb, t, M_HEADS, M_HEAD_DIM)
    mv = mv.reshape(nb, t, M_HEADS, M_HEAD_DIM)
    m_logf = jax.nn.log_sigmoid(mf.astype(f32))
    if past is None:
        ya = _fox_prompt(aq, ak, av, a_logf)
        c0 = jnp.zeros((nb, M_HEADS, M_HEAD_DIM, M_HEAD_DIM), f32)
        n0 = jnp.zeros((nb, M_HEADS, M_HEAD_DIM), f32)
        m0 = jnp.zeros((nb, M_HEADS), f32)
        conv0 = jnp.zeros((nb, CONV_W - 1, C_WIDTH), x.dtype)
        ffn0 = jnp.zeros((nb, CONV_W - 1, D_FF), x.dtype)
        chunk = M_CHUNK
    else:
        k_past, v_past, logf_past, c0, n0, m0, conv0, ffn0 = past
        ya = _fox_sample(aq, ak, av, a_logf, k_past, v_past, logf_past)
        chunk = t
    hm, c1, n1, m1 = _mlstm(mq, mk, mv, mi.astype(f32), m_logf, c0, n0, m0, chunk)
    hm = _rmsnorm(hm, g_mhead.reshape(M_HEADS, M_HEAD_DIM)).reshape(nb, t, M_WIDTH).astype(x.dtype)
    ym = jax.nn.sigmoid(mo) * hm
    uc, conv1 = _causal_dwconv(cc * cx, conv0, w_sconv)
    yc = (cb * uc) @ w_oc
    merged = (jax.nn.sigmoid(ga) * (ya @ w_oa) + jax.nn.sigmoid(gm) * (ym @ w_om)
              + jax.nn.sigmoid(gc) * yc)
    x = x + merged @ w_o
    h2 = _rmsnorm(x, g_ffn)
    ua, ub = jnp.split(h2 @ w_up, 2, axis=-1)
    uac, ffn1 = _causal_dwconv(ua, ffn0, w_fconv)
    x = x + (jax.nn.silu(uac + b_fconv) * ub) @ w_down
    gate = jax.nn.sigmoid(_rmsnorm(x, g_ple) @ w_ple_gate)
    x = x + gate * (pe @ w_ple)
    return x, (ak, av, a_logf, c1, n1, m1, conv1, ffn1)

def _stack_layers(per_layer):
    rows = [jnp.stack([s[i] for s in per_layer], axis=2) for i in range(3)]
    states = [jnp.stack([s[i] for s in per_layer], axis=1) for i in range(3, 8)]
    return tuple(rows + states)

def setup_inputs(seed: int = 0) -> dict:
    key = jax.random.key(seed)
    ks = iter(jax.random.split(key, 48))
    f32 = jnp.float32

    def nrm(shape, scale):
        return scale * jax.random.normal(next(ks), shape, f32)

    n_pages = PAST_LEN // PAGE_SIZE
    n_used = DEC_BATCH * n_pages
    n_phys = n_used + (n_used + SPARE_DIV - 1) // SPARE_DIV
    page_table = jax.random.permutation(next(ks), n_phys)[:n_used].reshape(DEC_BATCH, n_pages).astype(jnp.int32)

    b_in = nrm((DEPTH, P_IN), 0.02)
    o, s = _col_range("a_f")
    b_in = b_in.at[:, o:o + s].add(jnp.linspace(1.0, 4.0, s, dtype=f32))
    o, s = _col_range("m_f")
    b_in = b_in.at[:, o:o + s].add(jnp.linspace(3.0, 6.0, s, dtype=f32))

    return {
        "x_prompt": nrm((BATCH, SEQ, D_MODEL), 1.0),
        "x_sample": nrm((DEC_BATCH, DEC_SEQ, D_MODEL), 1.0),
        "cache_k": nrm((n_phys, PAGE_SIZE, DEPTH, A_HEADS, A_HEAD_DIM), 1.0),
        "cache_v": nrm((n_phys, PAGE_SIZE, DEPTH, A_HEADS, A_HEAD_DIM), 1.0),
        "cache_logf": jax.nn.log_sigmoid(2.5 + nrm((n_phys, PAGE_SIZE, DEPTH, A_HEADS), 1.0)),
        "state_mlstm_C": nrm((DEC_BATCH, DEPTH, M_HEADS, M_HEAD_DIM, M_HEAD_DIM), 0.3),
        "state_mlstm_n": nrm((DEC_BATCH, DEPTH, M_HEADS, M_HEAD_DIM), 0.3),
        "state_mlstm_m": nrm((DEC_BATCH, DEPTH, M_HEADS), 1.0),
        "state_conv": nrm((DEC_BATCH, DEPTH, CONV_W - 1, C_WIDTH), 1.0),
        "state_ffn_conv": nrm((DEC_BATCH, DEPTH, CONV_W - 1, D_FF), 1.0),
        "page_table": page_table,
        "p_prompt": nrm((DEPTH, BATCH, SEQ, PLE_DIM), 1.0),
        "p_sample": nrm((DEPTH, DEC_BATCH, DEC_SEQ, PLE_DIM), 1.0),
        "w_in": nrm((DEPTH, D_MODEL, P_IN), D_MODEL ** -0.5),
        "b_in": b_in,
        "g_mix": 1.0 + nrm((DEPTH, D_MODEL), 0.05),
        "g_mhead": 1.0 + nrm((DEPTH, M_WIDTH), 0.05),
        "w_sconv": nrm((DEPTH, CONV_W, C_WIDTH), CONV_W ** -0.5),
        "w_oa": nrm((DEPTH, A_WIDTH, D_MODEL), A_WIDTH ** -0.5),
        "w_om": nrm((DEPTH, M_WIDTH, D_MODEL), M_WIDTH ** -0.5),
        "w_oc": nrm((DEPTH, C_WIDTH, D_MODEL), C_WIDTH ** -0.5),
        "w_o": nrm((DEPTH, D_MODEL, D_MODEL), D_MODEL ** -0.5),
        "g_ffn": 1.0 + nrm((DEPTH, D_MODEL), 0.05),
        "w_up": nrm((DEPTH, D_MODEL, 2 * D_FF), D_MODEL ** -0.5),
        "w_fconv": nrm((DEPTH, CONV_W, D_FF), CONV_W ** -0.5),
        "b_fconv": nrm((DEPTH, D_FF), 0.02),
        "w_down": nrm((DEPTH, D_FF, D_MODEL), D_FF ** -0.5),
        "g_ple": 1.0 + nrm((DEPTH, D_MODEL), 0.05),
        "w_ple_gate": nrm((DEPTH, D_MODEL, D_MODEL), D_MODEL ** -0.5),
        "w_ple": nrm((DEPTH, PLE_DIM, D_MODEL), PLE_DIM ** -0.5),
        "g_final": 1.0 + nrm((D_MODEL,), 0.05),
    }

def reference(x_prompt, x_sample, cache_k, cache_v, cache_logf, state_mlstm_C, state_mlstm_n,
              state_mlstm_m, state_conv, state_ffn_conv, page_table, p_prompt, p_sample,
              w_in, b_in, g_mix, g_mhead, w_sconv, w_oa, w_om, w_oc, w_o, g_ffn, w_up,
              w_fconv, b_fconv, w_down, g_ple, w_ple_gate, w_ple, g_final):
    xp = x_prompt
    xs = x_sample
    new_p = []
    new_s = []
    for l in range(DEPTH):
        prm = (w_in[l], b_in[l], g_mix[l], g_mhead[l], w_sconv[l], w_oa[l], w_om[l], w_oc[l], w_o[l],
               g_ffn[l], w_up[l], w_fconv[l], b_fconv[l], w_down[l], g_ple[l], w_ple_gate[l], w_ple[l])
        xp, st_p = _layer(xp, p_prompt[l], prm, None)
        past = (_gather_pages(cache_k, page_table, l), _gather_pages(cache_v, page_table, l),
                _gather_pages(cache_logf, page_table, l), state_mlstm_C[:, l], state_mlstm_n[:, l],
                state_mlstm_m[:, l], state_conv[:, l], state_ffn_conv[:, l])
        xs, st_s = _layer(xs, p_sample[l], prm, past)
        new_p.append(st_p)
        new_s.append(st_s)
    y_prompt = _rmsnorm(xp, g_final)
    y_sample = _rmsnorm(xs, g_final)
    k_p, v_p, logf_p, c_p, n_p, m_p, conv_p, ffn_p = _stack_layers(new_p)
    k_s, v_s, logf_s, c_s, n_s, m_s, conv_s, ffn_s = _stack_layers(new_s)
    return (y_prompt, y_sample, k_p, v_p, logf_p, c_p, n_p, m_p, conv_p, ffn_p,
            k_s, v_s, logf_s, c_s, n_s, m_s, conv_s, ffn_s)


_drawn_inputs = setup_inputs


def setup_inputs(seed=0):
    import zlib

    import numpy as np

    out = dict(_drawn_inputs(seed))
    spreads = {}
    factors = {'g_mhead': 4.33, 'b_fconv': 6.618, 'g_ple': 26.235, 'cache_logf': 3.236}
    for name, (base, spread) in spreads.items():
        noise = np.random.default_rng([zlib.crc32(name.encode()), seed]).standard_normal(out[name].shape)
        drawn = base * np.exp(spread * noise) if base else spread * noise
        out[name] = jnp.asarray(drawn.astype(out[name].dtype))
    for name, factor in factors.items():
        out[name] = (out[name] * factor).astype(out[name].dtype)
    return out
```

```python
from contextlib import ExitStack

import numpy as np

import concourse.bass as bass
from concourse import mybir

F32 = mybir.dt.float32
F32R = mybir.dt.float32r
I32 = mybir.dt.int32
ALU = mybir.AluOpType
ACT = mybir.ActivationFunctionType
AX_X = mybir.AxisListType.X

P = 128
D = 1024
KD = D // P
TP = 512
NBATCH, NEW = 8, 8
TS = NBATCH * NEW
T = TP + TS
HALF = T // 2
QB = TP // P
TB = QB + 1
AH, AD = 8, 64
MH, MD = 4, 128
CW = 512
WT = CW // P
FF = 2816
FT = FF // P
FH = FT // 2
PLE = 256
PT = PLE // P
PAGE, PAGES = 128, 4
NPHYS = 40
EPS = 1e-6
BIG = 1e30
COL_A, COL_AF, COL_M, COL_MI, COL_MF, COL_MO, COL_C, COL_G = 0, 1536, 1544, 3080, 3084, 3088, 3600, 5136

BA, BM, BO, BC, BG = 0, 12, 24, 28, 40
GMIX, GFFN, GPLE, GFIN, GMH, WSC = 64, 72, 80, 88, 96, 100
ROWS1, ROWS2 = 112, 4 * FT

PR_A, PR_M, PR_O, PR_C, PR_MIX, PR_WO = 0, 6, 12, 14, 20, 44
PR_FFN = 48
PR_PART = FH + 4
PR_PLE = PR_FFN + 2 * PR_PART
PR_END = PR_PLE + 8


def tables():
    parts = {}
    r = np.arange(P)
    parts["ident"] = np.eye(P)
    parts["tri"] = np.concatenate([r[:, None] <= r[None, :], np.ones((P, TP - P + TS))], 1)
    parts["future_keys"] = np.where(r[None, :] <= r[:, None], 0.0, -BIG)
    parts["past_rows"] = np.where(r[:, None] <= r[None, :], 0.0, BIG)
    t = np.arange(TS)
    same = (t[:, None] // NEW == t[None, :] // NEW) & (t[:, None] <= t[None, :])
    parts["seq_tri"] = np.zeros((P, TS))
    parts["seq_tri"][:TS] = same
    parts["seq_past"] = np.zeros((P, TS))
    parts["seq_past"][:TS] = np.where(same, 0.0, BIG)
    row_b, row_q = r // 64, r % NEW
    allowed = np.zeros((P, 4, TS))
    own = np.zeros((P, 4, TS))
    for pair in range(4):
        b = 2 * pair + row_b
        allowed[:, pair] = (t[None, :] // NEW == b[:, None]) & (t[None, :] % NEW <= row_q[:, None])
        own[:, pair] = (t[None, :] // NEW == b[:, None]) & (t[None, :] % NEW == row_q[:, None])
    parts["new_keys"] = np.where(allowed > 0, 0.0, -BIG).reshape(P, 4 * TS)
    parts["own_key"] = own.reshape(P, 4 * TS)
    parts["not_seq"] = np.zeros((P, NBATCH))
    parts["not_seq"][:TS] = np.where(t[:, None] // NEW == np.arange(NBATCH)[None, :], 0.0, -BIG)
    parts["pick"] = np.zeros((P, AH * P))
    for h in range(AH):
        parts["pick"][h, h * P:(h + 1) * P] = 1.0
    starts = np.zeros(T)
    starts[0] = 1
    starts[TP::NEW] = 1
    parts["keep"] = np.broadcast_to(1.0 - starts, (P, T))
    parts["restart"] = np.broadcast_to(-BIG * starts, (P, T))
    return parts


def layout(parts):
    at, n = {}, 0
    for name, a in parts.items():
        at[name] = (n, a.shape[1])
        n += a.shape[1]
    return at, n



def build(nc, d, at, ncst):
    ctx = ExitStack()
    with ctx:
        def sem(name):
            return ctx.enter_context(nc.semaphore(name))

        base = (nc.sbuf_base + 31) // 32 * 32
        ctx.enter_context(nc.sbuf_tensor("arena", [P, (nc.sbuf_bytes_remaining - 64) // 4], F32))
        room = nc.sbuf_usable_end - base
        fixed = [0]

        def place(name, shape, dt, off):
            size = 4 * int(np.prod(shape[1:]))
            assert off % 32 == 0 and off + size <= room, (name, off, size, room)
            return nc.alloc_sbuf_tensor_at(name, shape, dt, offset=base + off)

        def keep(name, shape, dt=F32):
            size = (4 * int(np.prod(shape[1:])) + 31) // 32 * 32
            t = place(name, shape, dt, fixed[0])
            fixed[0] += size
            return t

        xT = keep("xT", [P, KD, T])
        a_hi = keep("a_hi", [P, KD, T], F32R)
        a_lo = keep("a_lo", [P, KD, T], F32R)
        raw = keep("raw", [P, 2, FH, P])
        w_hi = keep("w_hi", [P, 2, FH, P], F32R)
        w_lo = keep("w_lo", [P, 2, FH, P], F32R)
        CR = 4
        c_st = place("c_st", [P, CR, MH, MD], F32, fixed[0] - 2 * 8 * FH * P)
        cst = keep("cst", [P, ncst])
        ones = keep("ones", [P, P])
        mean_d = keep("mean_d", [P, P])
        mean_h = keep("mean_h", [P, P])
        cols1 = keep("cols1", [P, ROWS1])
        cols2 = keep("cols2", [P, ROWS2])
        gbias = keep("gbias", [P, 1])
        eps_c = keep("eps_c", [P, 1])
        rstd = keep("rstd", [P, T])
        pages = keep("pages", [P, NBATCH * PAGES], I32)
        L = fixed[0]

        def local(name, shape, dt, off):
            return place(name, shape, dt, L + off)

        def c(name, rows=P):
            o, n = at[name]
            return cst[0:rows, o:o + n]

        ident = c("ident")
        tri = c("tri")
        pick = c("pick", AH).rearrange("p (h m) -> p h m", h=AH)
        YB = 4 * WT * T
        ya_hi, ya_lo = (local(n, [P, WT, T], F32R, i * YB) for i, n in enumerate(("ya_hi", "ya_lo")))

        xs = local("xs", [P, TB, D], F32, 0)
        rows1 = local("rows1", [P, P], F32, 20480)
        rows2 = local("rows2", [P, P], F32, 20992)
        ws = local("ws", [P, KD, 96], F32, 21504)
        ws_hi = local("ws_hi", [P, KD, 96], F32R, 24576)
        ws_lo = local("ws_lo", [P, KD, 96], F32R, 27648)
        sq = local("sq", [P, 2, T], F32, 30720)
        hn = local("hn", [P, 2, T], F32, 30720 + 8 * T)

        SM = 81152
        q_a = local("q_a", [P, 3 * WT, T], F32, 2 * YB)
        v_tok = local("v_tok", [P, TB, CW], F32, 46080)
        cumb = local("cumb", [P, 2, TP], F32, 56320)
        NPK = P * (1 + 2 + 3 + 4)
        probs = local("probs", [P, 2, NPK], F32, 60416)
        kstage = local("kstage", [P, 2, CW], F32, 60416)
        logits = local("logits", [P, 2, TP], F32, 70656)
        pt = local("pt", [P, 2, TP], F32, 74752)
        gs = local("gs", [96, T], F32, SM)
        ge = local("ge", [96, T], F32, SM + 2304)
        lsg = local("lsg", [96, T], F32, SM + 4608)
        cum = local("cum", [AH, T], F32, SM + 6912)
        cq = local("cq", [P, QB, AH], F32, SM + 9216)
        lf_tok = local("lf_tok", [P, TB, AH], F32, SM + 9344)
        nmax = local("nmax", [P, 2], F32, SM + 9504)
        rsum = local("rsum", [P, 2], F32, SM + 9536)
        rinv = local("rinv", [P, 2], F32, SM + 9568)
        SS = SM + 9600
        q_blk = local("q_blk", [P, WT, NBATCH, 64], F32, SS)
        k_new = local("k_new", [P, WT, TS], F32, SS + 8192)

        kp = [local("kp0", [P, PAGES, CW], F32, 37376), local("kp1", [P, PAGES, CW], F32, 2 * YB)]
        kt_s = local("kt_s", [P, WT, TP], F32, 2 * YB + 8192)
        cums = local("cums", [P, T], F32, 2 * YB + 16384)
        vp = local("vp", [P, 2, PAGES, CW], F32, 56320)
        lrep = local("lrep", [P, PAGES, P], F32, 72704)
        lnew = local("lnew", [TS, P], F32, 74752)
        lpast = local("lpast", [P, NBATCH, PAGES, AH], F32, SM + 2304)
        pts = local("pts", [P, TB, P], F32, 76288)
        ls = local("ls", [P, T], F32, 78848)
        tmp64 = local("tmp64", [P, TS], F32, SS + 9216)

        q_m = local("q_m", [P, 3 * WT, T], F32, 2 * YB)
        k_tok = local("k_tok", [P, TB, CW], F32, 46080)
        vm_tok = local("vm_tok", [P, TB, CW], F32, 56320)
        sig_o = local("sig_o", [P, WT, T], F32, 56320)
        m_all = local("m_all", [P, MH, T], F32, 66560)
        decay = local("decay", [P, 3, TP], F32, 75776)
        e_m = local("e_m", [P, 2, TP], F32, 81920)
        n0 = local("n0", [NBATCH, CW], F32, 86016)
        rows_m = local("rows_m", [MH, 5, T], F32, 88064)
        e_ms = local("e_ms", [P, MH, TS], F32, 99584)
        a_s = local("a_s", [P, MH, TS], F32, 100608)
        w_s = local("w_s", [TS, MH, TS], F32, 101632)
        g_col = local("g_col", [P, TB, MH], F32, 102656)
        wl_p = local("wl_p", [P, QB, MH], F32, 102752)
        wl_s = local("wl_s", [TS, MH, NBATCH], F32, 102816)
        n_t = local("n_t", [P, MH, NBATCH], F32, 102944)
        m0 = local("m0", [MH, NBATCH], F32, 103072)
        a_last = local("a_last", [MH, NBATCH], F32, 103104)
        a_last_t = local("a_last_t", [NBATCH, MH], F32, 103136)
        c_t = local("c_t", [P, MH, MD], F32, 79872)
        k_own = local("k_own", [TS, 2, MH, MD], F32, 81920)
        h_t = local("h_t", [P, MH, T], F32, 4 * YB)
        h_sq = local("h_sq", [P, MH, T], F32, 46080)
        ym_hi, ym_lo = (local(n, [P, WT, T], F32R, (2 + i) * YB) for i, n in enumerate(("ym_hi", "ym_lo")))

        UW = 2 + TP + NBATCH * (2 + NEW)
        yc_hi, yc_lo = (local(n, [P, WT, T], F32R, (4 + i) * YB) for i, n in enumerate(("yc_hi", "yc_lo")))
        c_buf = local("c_buf", [P, 3 * WT, T], F32, 6 * YB)
        u_c = local("u_c", [P, WT, UW], F32, 82944)
        c_last = raw[:, 0, FH - 1, 0:18 * WT].rearrange("p (f c) -> p f c", f=WT)
        c_rows = local("c_rows", [16, CW], F32, 92800)
        c_out = rstd[0:18, 0:CW]

        mg_hi, mg_lo = (local(n, [P, KD, T], F32R, 6 * YB + i * 2 * YB) for i, n in enumerate(("mg_hi", "mg_lo")))
        gate = local("gate", [P, 3, T], F32, 92160)
        mix = local("mix", [P, 2, T], F32, 99072)

        hid_hi, hid_lo = (local(n, [P, FH, T], F32R, 40960 + i * 25344) for i, n in enumerate(("hid_hi", "hid_lo")))
        u_f = local("u_f", [P, UW], F32, 91648)
        y_f = local("y_f", [P, T], F32, 94048)
        s_f = local("s_f", [P, T], F32, 96352)
        f_last = local("f_last", [P, FT, 18], F32, 98656)
        f_cols = local("f_cols", [P, FT, 16], F32, 100256)
        f_rows = local("f_rows", [16, FF], F32, 0)
        f_out = local("f_out", [18, FF], F32, 11264)
        p_rows = local("p_rows", [P, TB, PLE], F32, 22528)
        p_hi, p_lo = (local(n, [P, PT, T], F32R, i * 4608) for i, n in enumerate(("p_hi", "p_lo")))

        gate_p = local("gate_p", [P, 2, T], F32, 55296)
        emb = local("emb", [P, T], F32, 59904)
        y_t = local("y_t", [P, KD, T], F32, 62208)
        y_rows = local("y_rows", [P, 2, D], F32, 80640)

        psum = ctx.enter_context(nc.psum_tensor("psum", [P, 8, 512], F32))

        def acc(slot):
            return psum[:, 2 * slot:2 * slot + 2, 0:HALF]

        cst_in, rows_in, ws_in = sem("cst_in"), sem("rows_in"), sem("ws_in")
        x_in = sem("x_in")
        bias_in, pages_in, gzero = sem("bias_in"), sem("pages_in"), sem("gzero")
        w_landed = [sem("w_landed0"), sem("w_landed1")]
        hi_ready, lo_ready, gemm_done = sem("hi_ready"), sem("lo_ready"), sem("gemm_done")
        psum_free = [sem("psum_free0"), sem("psum_free1")]
        dve_step, act_step, pool_step = sem("dve_step"), sem("act_step"), sem("pool_step")
        consts_ready, ws_zero, cols_done, cols_ready = sem("consts_ready"), sem("ws_zero"), sem("cols_done"), sem("cols_ready")
        xt_done, x_ready, sq_ready, sum_done, std_ready, hn_ready, ahi_ready, a_ready = (
            sem(n) for n in ("xt_done", "x_ready", "sq_ready", "sum_done", "std_ready", "hn_ready", "ahi_ready", "a_ready"))
        wshi_ready, ws_ready, gates_done = sem("wshi_ready"), sem("ws_ready"), sem("gates_done")
        gln_ready, cum_ready, small_done, small_ready = (
            sem(n) for n in ("gln_ready", "cum_ready", "small_done", "small_ready"))
        tok_done, tok_copied, q_scaled = sem("tok_done"), sem("tok_copied"), sem("q_scaled")
        out_k = [sem("out_k0"), sem("out_k1")]
        outs = sem("outs")
        cumb_done, cumb_ready, scores_done, logits_ready, nmax_ready, exp_done, probs_ready = (
            sem(n) for n in ("cumb_done", "cumb_ready", "scores_done", "logits_ready", "nmax_ready", "exp_done", "probs_ready"))
        pt_done, pt_copied, pv_done, o_hi, o_lo = (sem(n) for n in ("pt_done", "pt_copied", "pv_done", "o_hi", "o_lo"))
        qblk_ready, lpast_in = sem("qblk_ready"), sem("lpast_in")
        kp_in, vp_in = [sem("kp_in0"), sem("kp_in1")], [sem("vp_in0"), sem("vp_in1")]
        ktr_done, ktr_copied, lrep_ready, cums_done, cums_ready, s_done, s_free, snmax, sexp, sprobs, spt_done, spt_copied, spv_done, so_hi, so_lo = (
            sem(n) for n in ("ktr_done", "ktr_copied", "lrep_ready", "cums_done", "cums_ready", "s_done", "s_free", "snmax", "sexp", "sprobs", "spt_done", "spt_copied", "spv_done", "so_hi", "so_lo"))
        rows_ready, m0_in, mrow_ready, mb_done, mb_copied, mside_done, mside_copied, kscaled, mtok_done, mtok_copied, wl_sub, wl_ready = (
            sem(n) for n in ("rows_ready", "m0_in", "mrow_ready", "mb_done", "mb_copied", "mside_done", "mside_copied", "kscaled", "mtok_done", "mtok_copied", "wl_sub", "wl_ready"))
        em_done, em_ready, mqk_done, mdec_ready, mexp_done, mw_ready, mpv_done, h_ready = (
            sem(n) for n in ("em_done", "em_ready", "mqk_done", "mdec_ready", "mexp_done", "mw_ready", "mpv_done", "h_ready"))
        kw_ready, cp_done, cp_copied, n_in, nt_done, nt_copied, qn_ready, sqk_done, sdec_ready, sdexp_done, sw_ready, ssum_done = (
            sem(n) for n in ("kw_ready", "cp_done", "cp_copied", "n_in", "nt_done", "nt_copied", "qn_ready", "sqk_done", "sdec_ready", "sdexp_done", "sw_ready", "ssum_done"))
        c_in = [sem(f"c_in{s}") for s in range(CR)]
        c_store = [sem(f"c_store{s}") for s in range(CR)]
        ctr_done, ctr_copied, inter_done, kown_ready, cadd_done, cnew_ready, n_new_ready = (
            sem(n) for n in ("ctr_done", "ctr_copied", "inter_done", "kown_ready", "cadd_done", "cnew_ready", "n_new_ready"))
        hsq_ready, hmean_done, hstd_ready, ym_full, ymhi_ready, ym_ready = (
            sem(n) for n in ("hsq_ready", "hmean_done", "hstd_ready", "ym_full", "ymhi_ready", "ym_ready"))
        conv_rows_in, ctr2_done, yc_full, ychi_ready, yc_ready, clast_done, clast_copied = (
            sem(n) for n in ("conv_rows_in", "ctr2_done", "yc_full", "ychi_ready", "yc_ready", "clast_done", "clast_copied"))
        mix_step, f_rows_in, p_rows_in, fcols_done, fcols_ready, p_done, phi_ready, p_ready = (
            sem(n) for n in ("mix_step", "f_rows_in", "p_rows_in", "fcols_done", "fcols_ready", "p_done", "phi_ready", "p_ready"))
        fconv_done, fstep, fsig_done, hid_ready, flast_done, flast_copied, xple_ready, yt_ready, ytr_done, ytr_copied = (
            sem(n) for n in ("fconv_done", "fstep", "fsig_done", "hid_ready", "flast_done", "flast_copied", "xple_ready", "yt_ready", "ytr_done", "ytr_copied"))
        conv_out = sem("conv_out")
        y_store = [sem("y_store0"), sem("y_store1")]

        w_in = d["w_in"][0].rearrange("(k p) n -> p k n", p=P)

        ctx.enter_context(nc.allow_non_contiguous_dma(reason="a few numbers for each head"))
        block = ctx.enter_context(nc.Block())
        @block.sync
        def _(sp):
            for b in range(QB):
                sp.dma_start(xs[:, b, :], d["x_prompt"][0, b * P:(b + 1) * P, :]).then_inc(x_in, 16)
            sp.dma_start(xs[0:TS, QB, :], d["x_sample"].rearrange("b t n -> (b t) n")).then_inc(x_in, 16)

            def load(first, start, pairs, sources, kts):
                def one(i):
                    for slot in (0, 1):
                        if not (first == 0 and isinstance(i, int) and i == 0):
                            sp.wait_ge(lo_ready, (i + first) * 2 + (slot - 1))
                        sp.dma_start(raw[:, slot, 0:kts[slot], :], sources[slot](i)).then_inc(w_landed[slot], 16)

                if pairs - start == 1:
                    one(start)
                else:
                    with sp.Fori(start, pairs) as i:
                        one(i)

            def two(mat, col):
                return [lambda i, s=s: mat[:, :, bass.ds(i * 256 + (col + s * P), P)] for s in (0, 1)]

            load(PR_A, 0, 1, two(w_in, COL_A), (KD, KD))
            load(PR_A, 1, 6, two(w_in, COL_A), (KD, KD))
            load(PR_M, 0, 1, two(w_in, COL_M), (KD, KD))

            sp.wait_ge(small_ready, 2)
            for b in range(TB):
                n = 2 * b + 1
                rows = TS if b == QB else P
                k_rows = d["k_s"].rearrange("b t l h e -> (b t) (l h e)") if b == QB else d["k_p"][0, b * P:(b + 1) * P].rearrange("t l h e -> t (l h e)")
                v_rows = d["v_s"].rearrange("b t l h e -> (b t) (l h e)") if b == QB else d["v_p"][0, b * P:(b + 1) * P].rearrange("t l h e -> t (l h e)")
                lf_rows = d["logf_s"].rearrange("b t l h -> (b t) (l h)") if b == QB else d["logf_p"][0, b * P:(b + 1) * P].rearrange("t l h -> t (l h)")
                sp.wait_ge(tok_copied, n)
                sp.dma_start(v_rows, v_tok[0:rows, b, :]).then_inc(outs, 16)
                sp.wait_ge(tok_copied, n + 1)
                sp.dma_start(k_rows, kstage[0:rows, b % 2, :]).then_inc(out_k[b % 2], 16)
                sp.dma_start(lf_rows, lf_tok[0:rows, b, :]).then_inc(outs, 16)

            sp.wait_ge(pages_in, 16)
            page = [[sp.value_load(pages[0:1, b * PAGES + j:b * PAGES + j + 1], min_val=0, max_val=NPHYS - 1) for j in range(PAGES)]
                    for b in range(NBATCH)]
            for b in range(NBATCH):
                for j in range(PAGES):
                    sp.dma_start(lpast[:, b, j, :], d["cache_logf"][bass.ds(page[b][j], 1), :, 0, :].rearrange("a s h -> (a s) h")).then_inc(lpast_in, 16)

            def page_rows(name, ring, landed, b):
                for j in range(PAGES):
                    sp.dma_start(ring[:, j, :], d[name][bass.ds(page[b][j], 1), :, 0].rearrange("a s h e -> (a s) (h e)")).then_inc(landed, 16)

            page_rows("cache_k", kp[0], kp_in[0], 0)
            sp.wait_ge(pv_done, 4 * AH)
            sp.wait_ge(qblk_ready, AH + 1)
            page_rows("cache_k", kp[1], kp_in[1], 1)
            for kind, p in (("v", 0), ("k", 1), ("k", 2), ("v", 1), ("k", 3), ("v", 2), ("v", 3)):
                for b2 in range(2):
                    if kind == "k":
                        sp.wait_ge(ktr_done, 4 * (2 * p + b2 - 1))
                        page_rows("cache_k", kp[b2], kp_in[b2], 2 * p + b2)
                    else:
                        if p:
                            sp.wait_ge(spv_done, p)
                        page_rows("cache_v", vp[:, b2], vp_in[b2], 2 * p + b2)
            load(PR_M, 1, 6, two(w_in, COL_M), (KD, KD))
            load(PR_O, 0, 1, two(w_in, COL_MO), (KD, KD))
            sp.wait_ge(gemm_done, 2 * (PR_M + 6))

            def state_in(b):
                sp.dma_start(c_st[:, b % CR, :, :], d["state_mlstm_C"][b, 0].rearrange("h v k -> v h k")).then_inc(c_in[b % CR], 16)

            for b in range(CR):
                state_in(b)
            sp.wait_ge(rows_ready, 1)
            sp.dma_start(n0[:], d["state_mlstm_n"].rearrange("b l h e -> b (l h e)")).then_inc(n_in, 16)
            sp.wait_ge(mrow_ready, 1)
            sp.dma_start(d["m_p"].rearrange("a l h -> h (a l)"), rows_m[:, 0, TP - 1:TP]).then_inc(outs, 16)
            sp.dma_start(d["m_s"].rearrange("b l h -> h (l b)"), rows_m[:, 0, TP + NEW - 1:T:NEW]).then_inc(outs, 16)
            sp.wait_ge(cp_copied, 2)
            sp.dma_start(d["C_p"][0, 0].rearrange("h v k -> v h k"), m_all[:, :, 0:MD]).then_inc(outs, 16)
            sp.dma_start(d["n_p"][0, 0].rearrange("h k -> (h k)").rearrange("(o n) -> o n", o=1), rows_m[0:1, 2, 0:CW]).then_inc(outs, 16)
            for b in range(NBATCH):
                sp.wait_ge(cnew_ready, b + 1)
                sp.dma_start(d["C_s"][b, 0].rearrange("h v k -> v h k"), c_st[:, b % CR, :, :]).then_inc(c_store[b % CR], 16)
                if b >= 1 and b - 1 + CR < NBATCH:
                    sp.wait_ge(c_store[(b - 1) % CR], 16)
                    state_in(b - 1 + CR)
            sp.wait_ge(n_new_ready, 1)
            sp.dma_start(d["n_s"].rearrange("b l h e -> b (l h e)"), n0[:]).then_inc(outs, 16)
            load(PR_O, 1, 2, two(w_in, COL_MO), (KD, KD))
            load(PR_C, 0, 1, two(w_in, COL_C), (KD, KD))
            sp.wait_ge(ym_ready, 1)
            sp.dma_start(c_rows[:], d["state_conv"].rearrange("b l r c -> (b l r) c")).then_inc(conv_rows_in, 16)
            load(PR_C, 1, 6, two(w_in, COL_C), (KD, KD))

            w_out = [d[name][0].rearrange("(k p) n -> p k n", p=P) for name in ("w_oa", "w_om", "w_oc")]
            for i in range(KD):
                for b in range(3):
                    n = 2 * (PR_MIX + 3 * i + b)
                    sp.wait_ge(lo_ready, n - 1)
                    sp.dma_start(raw[:, 0, 0:KD, :], w_in[:, :, COL_G + b * D + i * P:COL_G + b * D + (i + 1) * P]).then_inc(w_landed[0], 16)
                    sp.wait_ge(lo_ready, n)
                    sp.dma_start(raw[:, 1, 0:WT, :], w_out[b][:, :, i * P:(i + 1) * P]).then_inc(w_landed[1], 16)

            def kt_view(mat):
                return mat.rearrange("(k p) n -> p k n", p=P)

            load(PR_WO, 0, 4, two(kt_view(d["w_o"][0]), 0), (KD, KD))
            sp.wait_ge(clast_copied, 1)
            sp.dma_start(d["conv_p"][0, 0], c_out[0:2, :]).then_inc(conv_out, 16)
            sp.dma_start(d["conv_s"].rearrange("b l r c -> (b l r) c"), c_out[2:18, :]).then_inc(conv_out, 16)
            up = kt_view(d["w_up"][0])
            ups = [[lambda i, f=f, s=s: up[:, :, bass.ds(i * P + (f * FH * P + s * FF), P)] for s in (0, 1)] for f in range(2)]
            load(PR_FFN, 0, 1, ups[0], (KD, KD))
            sp.wait_ge(mix_step, 4 * KD)
            sp.dma_start(f_rows[:], d["state_ffn_conv"].rearrange("b l r c -> (b l r) c")).then_inc(f_rows_in, 16)
            for b in range(QB):
                sp.dma_start(p_rows[:, b, :], d["p_prompt"][0, 0, b * P:(b + 1) * P, :]).then_inc(p_rows_in, 16)
            sp.dma_start(p_rows[0:TS, QB, :], d["p_sample"][0].rearrange("b t n -> (b t) n")).then_inc(p_rows_in, 16)
            for f in range(2):
                load(PR_FFN + f * PR_PART, 1 - f, FH, ups[f], (KD, KD))
                down = d["w_down"][0][f * FH * P:(f + 1) * FH * P, :].rearrange("(k p) n -> p k n", p=P)
                load(PR_FFN + f * PR_PART + FH, 0, 4, two(down, 0), (FH, FH))
            tail = [kt_view(d["w_ple_gate"][0]), kt_view(d["w_ple"][0])]
            load(PR_PLE, 0, 8, [lambda i, s=s: tail[s][:, :, bass.ds(i * P, P)] for s in (0, 1)], (KD, PT))
            sp.wait_ge(flast_copied, 6)
            sp.dma_start(d["ffn_p"][0, 0], f_out[0:2, :]).then_inc(outs, 16)
            sp.dma_start(d["ffn_s"].rearrange("b l r c -> (b l r) c"), f_out[2:18, :]).then_inc(outs, 16)
            for b in range(TB):
                sp.wait_ge(ytr_copied, 2 * b + 2)
                dst = d["y_sample"].rearrange("b t n -> (b t) n") if b == QB else d["y_prompt"][0, b * P:(b + 1) * P, :]
                sp.dma_start(dst, y_rows[0:TS if b == QB else P, b % 2, :]).then_inc(y_store[b % 2], 16)
            sp.wait_ge(y_store[0], 16 * 3)
            sp.wait_ge(y_store[1], 16 * 2)
            sp.wait_ge(outs, 16 * (2 * TB + 7))
            sp.wait_ge(conv_out, 32)
            for s in range(CR):
                sp.wait_ge(c_store[s], 16 * (NBATCH // CR))
            sp.wait_ge(out_k[0], 16 * 3)
            sp.wait_ge(out_k[1], 16 * 2)

        @block.gpsimd
        def _(pool):
            pool.memset(ws[:], 0.0).then_inc(ws_zero, 1)
            pool.memset(ones[:], 1.0).then_inc(consts_ready, 1)
            pool.memset(mean_d[:], 1.0 / D).then_inc(consts_ready, 1)
            pool.memset(mean_h[:], 1.0 / MD).then_inc(consts_ready, 1)
            pool.memset(eps_c[:], EPS).then_inc(consts_ready, 1)
            pool.wait_ge(wshi_ready, 1)
            pool.tensor_tensor(ws_lo[:], ws[:], ws_hi[:].bitcast(F32), ALU.subtract).then_inc(ws_ready, 1)

            def split_lo(first, start, pairs, kts):
                def one(i):
                    for slot in (0, 1):
                        pool.wait_ge(hi_ready, (i + first) * 2 + (slot + 1))
                        pool.tensor_tensor(w_lo[:, slot, 0:kts[slot], :], raw[:, slot, 0:kts[slot], :],
                                           w_hi[:, slot, 0:kts[slot], :].bitcast(F32), ALU.subtract).then_inc(lo_ready, 1)

                if pairs - start == 1:
                    one(start)
                else:
                    with pool.Fori(start, pairs) as i:
                        one(i)

            split_lo(PR_A, 0, 6, (KD, KD))
            split_lo(PR_M, 0, 1, (KD, KD))

            pool.wait_ge(q_scaled, 1)
            pool.memset(q_blk[:], 0.0).then_inc(pool_step, 1)
            pool.wait_ge(pool_step, 1)
            for h in range(AH):
                r = slice(64 * (h % 2), 64 * (h % 2) + 64)
                pool.tensor_copy(q_blk[r, h // 2, :, 8 * h:8 * h + 8],
                                 q_a[r, h // 2, TP:T].rearrange("p (b q) -> p b q", b=NBATCH)).then_inc(qblk_ready, 1)
                pool.wait_ge(qblk_ready, h + 1)
            pool.tensor_copy(k_new[:], q_a[:, WT:2 * WT, TP:T]).then_inc(qblk_ready, 1)
            pool.wait_ge(qblk_ready, AH + 1)
            pool.wait_ge(pv_done, 4 * AH)
            for b2 in range(2):
                pool.tensor_copy(lnew[:, 64 * b2:64 * b2 + 64].rearrange("p (h q) -> p h q", h=AH),
                                 lf_tok[0:TS, QB, :].unsqueeze(2).broadcast_to([TS, AH, NEW])).then_inc(lrep_ready, 1)
                pool.wait_ge(lrep_ready, b2 + 1)
            pool.wait_ge(lpast_in, 16 * NBATCH * PAGES)
            for p in range(NBATCH // 2):
                if p:
                    pool.wait_ge(cums_done, p)
                for b2 in range(2):
                    pool.tensor_copy(lrep[:].rearrange("p j (b h q) -> p j b h q", b=2, h=AH)[:, :, b2],
                                     lpast[:, 2 * p + b2].unsqueeze(3).broadcast_to([P, PAGES, AH, NEW])).then_inc(lrep_ready, 1)
                    pool.wait_ge(lrep_ready, 2 * p + b2 + 3)
            split_lo(PR_M, 1, 6, (KD, KD))
            pool.wait_ge(wl_ready, 2)
            pool.wait_ge(mtok_copied, 2 * TB)
            for b in range(QB):
                kb = k_tok[:, b, :].rearrange("p (h e) -> p h e", h=MH)
                pool.tensor_tensor(kb, kb, wl_p[:, b, :].unsqueeze(2).broadcast_to([P, MH, MD]), ALU.mult).then_inc(kw_ready, 1)
            pool.wait_ge(h_ready, MH)
            for b in range(NBATCH):
                if b >= 2:
                    pool.wait_ge(cadd_done, b - 1)
                pool.tensor_tensor(k_own[:, b % 2], k_tok[0:TS, QB, :].rearrange("p (h e) -> p h e", h=MH),
                                   wl_s[:, :, b:b + 1].broadcast_to([TS, MH, MD]), ALU.mult).then_inc(kown_ready, 1)
            split_lo(PR_O, 0, 2, (KD, KD))
            split_lo(PR_C, 0, 6, (KD, KD))
            with pool.Fori(0, KD) as i:
                for b in range(3):
                    for slot, kt in ((0, KD), (1, WT)):
                        pool.wait_ge(hi_ready, i * 6 + ((PR_MIX + b) * 2 + slot + 1))
                        pool.tensor_tensor(w_lo[:, slot, 0:kt, :], raw[:, slot, 0:kt, :],
                                           w_hi[:, slot, 0:kt, :].bitcast(F32), ALU.subtract).then_inc(lo_ready, 1)
            split_lo(PR_WO, 0, 4, (KD, KD))
            for f in range(2):
                split_lo(PR_FFN + f * PR_PART, 0, FH, (KD, KD))
                split_lo(PR_FFN + f * PR_PART + FH, 0, 4, (FH, FH))
            split_lo(PR_PLE, 0, 8, (KD, PT))

        @block.scalar
        def _(act):
            act.dma_start(cst[:], d["cst"]).then_inc(cst_in, 16)
            brows = d["b_in"][0]
            for r0, c0, n in ((BA, COL_A, 12), (BM, COL_M, 12), (BO, COL_MO, 4), (BC, COL_C, 12), (BG, COL_G, 24)):
                act.dma_start(rows1[r0:r0 + n, :], brows[c0:c0 + n * P].rearrange("(t p) -> t p", p=P)).then_inc(rows_in, 16)
            for r0, name in ((GMIX, "g_mix"), (GFFN, "g_ffn"), (GPLE, "g_ple"), (GMH, "g_mhead")):
                n = KD if r0 != GMH else WT
                act.dma_start(rows1[r0:r0 + n, :], d[name][0].rearrange("(t p) -> t p", p=P)).then_inc(rows_in, 16)
            act.dma_start(rows1[GFIN:GFIN + KD, :], d["g_final"].rearrange("(t p) -> t p", p=P)).then_inc(rows_in, 16)
            act.dma_start(rows1[WSC:WSC + 3 * WT, :], d["w_sconv"][0].rearrange("j (t p) -> (j t) p", p=P)).then_inc(rows_in, 16)
            act.dma_start(rows2[0:3 * FT, :], d["w_fconv"][0].rearrange("j (t p) -> (j t) p", p=P)).then_inc(rows_in, 16)
            act.dma_start(rows2[3 * FT:4 * FT, :], d["b_fconv"][0].rearrange("(t p) -> t p", p=P)).then_inc(rows_in, 16)
            act.wait_ge(ws_zero, 1)
            for r0, c0, n in ((0, COL_AF, 8), (32, COL_MI, 4), (64, COL_MF, 4)):
                act.dma_start(ws[:, :, r0:r0 + n], w_in[:, :, c0:c0 + n]).then_inc(ws_in, 16)
            act.wait_ge(gzero, 1)
            for r0, c0, n in ((0, COL_AF, 8), (32, COL_MI, 4), (64, COL_MF, 4)):
                act.dma_start(gbias[r0:r0 + n, :], brows[c0:c0 + n].rearrange("(p o) -> p o", o=1)).then_inc(bias_in, 16)
            act.dma_start(pages[0:1, :], d["page_table"].rearrange("b j -> (b j)").rearrange("(o n) -> o n", o=1)).then_inc(pages_in, 16)

            steps = [0]

            def link(ins):
                steps[0] += 1
                ins.then_inc(act_step, 1)
                act.wait_ge(act_step, steps[0])

            for k in range(KD):
                act.wait_ge(xt_done, k + 1)
                act.activation(xT[:, k, 0:TP], psum[:, 2 * (k % 2), :], ACT.Copy)
                act.activation(xT[:, k, TP:T], psum[:, 2 * (k % 2) + 1, 0:TS], ACT.Copy).then_inc(x_ready, 1)
            act.wait_ge(ws_in, 48)
            act.activation(ws_hi[:], ws[:], ACT.Copy).then_inc(wshi_ready, 1)

            def norm_split(number):
                act.wait_ge(sum_done, number + 1)
                act.activation(rstd[:].rearrange("p (a t) -> p a t", a=2), psum[:, 6:8, 0:HALF], ACT.Sqrt, bias=eps_c[:]).then_inc(std_ready, 1)
                for k in range(KD):
                    act.wait_ge(hn_ready, KD * number + k + 1)
                    act.activation(a_hi[:, k, :], hn[:, k % 2, :], ACT.Copy).then_inc(ahi_ready, 1)

            def hi(first, i, slot, kt):
                act.wait_ge(w_landed[slot], (i + (first + 1)) * 16)
                if not (isinstance(i, int) and first + i == 0):
                    act.wait_ge(gemm_done, (i + first) * 2 + (slot - 1))
                act.activation(w_hi[:, slot, 0:kt, :], raw[:, slot, 0:kt, :], ACT.Copy).then_inc(hi_ready, 1)

            def biased(first, pairs, kt_next, dst, col, func=ACT.Identity):
                def one(i, kt):
                    for slot in (0, 1):
                        if kt:
                            hi(first, i + 1, slot, kt[slot])
                        act.wait_ge(gemm_done, (i + first) * 2 + (slot + 1))
                        act.activation(dst[:, bass.ds(i * 2 + slot, 1), :].rearrange("p o (a t) -> p (o a) t", a=2), acc(slot), func,
                                       bias=cols1[:, bass.ds(i * 2 + (col + slot), 1)]).then_inc(psum_free[slot], 1)

                if pairs > 1:
                    with act.Fori(0, pairs - 1) as i:
                        one(i, (KD, KD))
                one(pairs - 1, kt_next)

            hi(PR_A, 0, 0, KD)
            hi(PR_A, 0, 1, KD)
            act.wait_ge(consts_ready, 4)
            norm_split(0)
            act.wait_ge(cols_ready, 2)
            act.wait_ge(gates_done, 1)
            act.wait_ge(bias_in, 48)
            link(act.activation(gs[:].rearrange("p (a t) -> p a t", a=2), psum[0:96, 4:6, 0:HALF], ACT.Identity, bias=gbias[0:96]))
            link(act.activation(ge[:], gs[:], ACT.Abs))
            link(act.activation(ge[:], ge[:], ACT.Exp, scale=-1.0))
            act.activation(ge[:], ge[:], ACT.Ln, bias=1.0).then_inc(gln_ready, 1)

            biased(PR_A, 6, (KD, KD), q_a, BA)
            act.wait_ge(small_done, 1)
            act.activation(lf_tok[:, 0:QB, :], psum[:, 4, 0:QB * AH].rearrange("p (b h) -> p b h", b=QB), ACT.Copy)
            act.activation(lf_tok[0:TS, QB, :], psum[0:TS, 4, QB * AH:TB * AH], ACT.Copy).then_inc(small_ready, 1)
            act.activation(cq[:], psum[:, 4, 64:64 + QB * AH].rearrange("p (b h) -> p b h", b=QB), ACT.Copy).then_inc(small_ready, 1)
            for b in range(TB):
                rows = TS if b == QB else P
                for which in range(2):
                    n = 2 * b + which
                    act.wait_ge(tok_done, n + 1)
                    if which and b >= 2:
                        act.wait_ge(out_k[b % 2], 16 * (b // 2))
                    act.activation(kstage[0:rows, b % 2, :] if which else v_tok[0:rows, b, :], psum[0:rows, 4 + n % 4, :], ACT.Copy).then_inc(tok_copied, 1)

            act.wait_ge(out_k[0], 16 * 3)
            act.wait_ge(out_k[1], 16 * 2)
            for h in range(AH + 1):
                if h < AH:
                    act.wait_ge(cumb_done, h + 1)
                    if h >= 2:
                        act.wait_ge(logits_ready, 4 * (h - 1))
                    act.activation(cumb[:, h % 2, :], psum[:, h % 2, :], ACT.Copy).then_inc(cumb_ready, 1)
                for i in range(QB):
                    if h < AH:
                        n = 4 * h + i
                        act.wait_ge(nmax_ready, n + 1)
                        if h >= 2 and i == 0:
                            act.wait_ge(pt_done, 4 * (h - 1))
                        o = P * (i * (i + 1) // 2)
                        act.activation(probs[:, h % 2, o:o + P * (i + 1)], logits[:, n % 2, 0:P * (i + 1)], ACT.Exp,
                                       bias=nmax[:, n % 2:n % 2 + 1], accum_out=rsum[:, n % 2:n % 2 + 1]).then_inc(exp_done, 1)
                    if h >= 1:
                        m = 4 * (h - 1) + i
                        act.wait_ge(pt_done, m + 1)
                        if m >= 2:
                            act.wait_ge(pv_done, m - 1)
                        act.activation(pt[:, m % 2, 0:TP - P * i], psum[:, (6, 2)[m % 2], 0:TP - P * i], ACT.Copy).then_inc(pt_copied, 1)
                if h >= 1 and (h - 1) % 2:
                    f = (h - 1) // 2
                    act.wait_ge(pv_done, 4 * h)
                    act.activation(ya_hi[:, f, 0:TP], psum[:, (7, 3)[f % 2], :], ACT.Copy).then_inc(o_hi, 1)

            for p in range(NBATCH // 2 + 1):
                if p < NBATCH // 2:
                    if p == 0:
                        act.wait_ge(pv_done, 4 * AH)
                        act.wait_ge(qblk_ready, AH + 1)
                    for b2 in range(2):
                        for f in range(WT):
                            m = 4 * (2 * p + b2) + f
                            act.wait_ge(ktr_done, m + 1)
                            if m >= 4:
                                act.wait_ge(s_done, (2 * p + b2 - 1) * 4 + f + 1)
                            act.activation(kt_s[:, f, :], psum[:, 4 + m % 2, :], ACT.Copy).then_inc(ktr_copied, 1)
                    act.wait_ge(cums_done, p + 1)
                    if p:
                        act.wait_ge(s_free, p)
                    act.activation(cums[:, 0:TP], psum[:, 0, :], ACT.Copy)
                    act.activation(cums[:, TP:T], psum[:, 1, 0:TS], ACT.Copy).then_inc(cums_ready, 1)
                if p:
                    y = p - 1
                    act.wait_ge(snmax, y + 1)
                    act.activation(ls[:], ls[:], ACT.Exp, bias=nmax[:, 0:1], accum_out=rsum[:, 0:1]).then_inc(sexp, 1)
                    act.wait_ge(spt_done, y + 1)
                    act.activation(pts[:, 0:QB, :], psum[:, 6, :].rearrange("p (j r) -> p j r", j=QB), ACT.Copy)
                    act.activation(pts[0:TS, QB, :], psum[0:TS, 0, 0:P], ACT.Copy).then_inc(spt_copied, 1)
                    act.wait_ge(spv_done, y + 1)
                    for hh in range(2):
                        r = slice(64 * hh, 64 * hh + 64)
                        act.activation(ya_hi[r, :, TP + 16 * y:TP + 16 * y + 16].rearrange("p f (b q) -> p b f q", b=2),
                                       psum[r, 7, 0:128].rearrange("p (b f r) -> p b f r", b=2, f=WT)[:, :, :, 8 * hh:8 * hh + 8], ACT.Copy).then_inc(so_hi, 1)
            act.dma_start(m0[:], d["state_mlstm_m"].rearrange("b l h -> h (l b)")).then_inc(m0_in, 16)
            biased(PR_M, 6, None, q_m, BM)
            for h in range(MH):
                act.wait_ge(mb_done, h + 1)
                act.activation(m_all[:, h, 0:TP], psum[:, 4 + h % 2, :], ACT.Copy).then_inc(mb_copied, 1)
            act.wait_ge(mside_done, 1)
            act.activation(m_all[:, :, TP:T], psum[:, 6, 0:MH * TS].rearrange("p (h t) -> p h t", h=MH), ACT.Copy)
            act.activation(e_ms[:], psum[:, 6, MH * TS:2 * MH * TS].rearrange("p (h t) -> p h t", h=MH), ACT.Exp, scale=-1.0)
            act.activation(a_s[:], psum[:, 7, 0:MH * TS].rearrange("p (h t) -> p h t", h=MH), ACT.Exp)
            act.activation(a_last[:], rows_m[:, 4, NEW - 1:TS:NEW], ACT.Exp)
            act.activation(g_col[:, 0:QB, :], psum[:, 7, 256:256 + QB * MH].rearrange("p (b h) -> p b h", b=QB), ACT.Copy)
            act.activation(g_col[0:TS, QB, :], psum[0:TS, 7, 256 + QB * MH:256 + TB * MH], ACT.Copy).then_inc(mside_copied, 1)
            for b in range(TB):
                rows = TS if b == QB else P
                for which in range(2):
                    n = 2 * b + which
                    act.wait_ge(mtok_done, n + 1)
                    act.activation((k_tok if which else vm_tok)[0:rows, b, :], psum[0:rows, n % 4, :], ACT.Copy).then_inc(mtok_copied, 1)
            act.wait_ge(wl_sub, 2)
            act.activation(wl_p[:], wl_p[:], ACT.Exp).then_inc(wl_ready, 1)
            act.activation(wl_s[:], wl_s[:], ACT.Exp).then_inc(wl_ready, 1)

            for n in range(4 * MH):
                h = n // 4
                if n % 4 == 0:
                    act.wait_ge(em_done, h + 1)
                    if h >= 2:
                        act.wait_ge(h_ready, h - 1)
                    act.activation(e_m[:, h % 2, :], psum[:, 2, :], ACT.Exp, scale=-1.0).then_inc(em_ready, 1)
                act.wait_ge(mdec_ready, n + 1)
                w = TP - P * (n % 4)
                act.activation(decay[:, n % 3, 0:w], decay[:, n % 3, 0:w], ACT.Exp, scale=-1.0).then_inc(mexp_done, 1)
            act.wait_ge(cp_done, 1)
            act.activation(m_all[:, :, 0:MD], psum[:, 3, :].rearrange("p (h e) -> p h e", h=MH), ACT.Copy).then_inc(cp_copied, 1)
            act.wait_ge(cp_done, 2)
            act.activation(rows_m[0:1, 2, 0:CW], psum[0:1, 4, :], ACT.Copy).then_inc(cp_copied, 1)
            act.wait_ge(nt_done, 1)
            act.activation(n_t[:], psum[:, 5, 0:MH * NBATCH].rearrange("p (h b) -> p h b", h=MH), ACT.Copy)
            act.activation(a_last_t[:], psum[0:NBATCH, 5, 64:64 + MH], ACT.Copy).then_inc(nt_copied, 1)
            act.wait_ge(sdec_ready, 1)
            act.activation(w_s[:], w_s[:], ACT.Exp, scale=-1.0).then_inc(sdexp_done, 1)
            for b in range(NBATCH):
                act.wait_ge(ctr_done, b + 1)
                if b:
                    act.wait_ge(inter_done, b)
                act.activation(c_t[:], psum[:, b % 2, :].rearrange("p (h e) -> p h e", h=MH), ACT.Copy).then_inc(ctr_copied, 1)
            for s in range(CR):
                act.wait_ge(c_store[s], 16 * (NBATCH // CR))
            hi(PR_O, 0, 0, KD)
            hi(PR_O, 0, 1, KD)
            for pair in range(2):
                biased(PR_O + pair, 1, (KD, KD), sig_o[:, 2 * pair:2 * pair + 2, :], BO + 2 * pair, ACT.Sigmoid)
                act.wait_ge(hmean_done, pair + 1)
                act.activation(h_sq[:, 2 * pair:2 * pair + 2, :].rearrange("p h (a t) -> p (h a) t", a=2), psum[:, 4:8, 0:HALF],
                               ACT.Sqrt, bias=eps_c[:]).then_inc(hstd_ready, 1)
            act.wait_ge(ym_full, 1)
            act.activation(ym_hi[:], h_t[:], ACT.Copy).then_inc(ymhi_ready, 1)
            biased(PR_C, 6, (KD, WT), c_buf, BC)
            for g in range(2):
                act.wait_ge(yc_full, g + 1)
                act.activation(yc_hi[:, 2 * g:2 * g + 2, :], c_buf[:, WT + 2 * g:WT + 2 * g + 2, :], ACT.Copy).then_inc(ychi_ready, 1)

            def mixing(i, last):
                for b in range(3):
                    kts = (KD, KD) if last and b == 2 else (KD, WT)
                    hi(PR_MIX + b + 1, i * 3, 0, kts[0])
                    act.wait_ge(gemm_done, i * 6 + ((PR_MIX + b) * 2 + 1))
                    act.wait_ge(psum_free[1], i * 3 + (PR_MIX + b - 2))
                    act.activation(gate[:, b, :].rearrange("p (a t) -> p a t", a=2), acc(0), ACT.Sigmoid,
                                   bias=cols1[:, bass.ds(i + (BG + KD * b), 1)]).then_inc(psum_free[0], 1)
                    hi(PR_MIX + b + 1, i * 3, 1, kts[1])

            with act.Fori(0, KD - 1) as i:
                mixing(i, False)
            mixing(KD - 1, True)
            act.wait_ge(clast_done, 1)
            act.activation(c_out, psum[0:18, 5, :], ACT.Copy).then_inc(clast_copied, 1)

            def split_only(first, pairs, kts, kt_next):
                with act.Fori(0, pairs - 1) as i:
                    for slot in (0, 1):
                        hi(first, i + 1, slot, kts[slot])
                if kt_next:
                    for slot in (0, 1):
                        hi(first, pairs, slot, kt_next[slot])

            split_only(PR_WO, 4, (KD, KD), (KD, KD))
            act.wait_ge(conv_out, 32)
            norm_split(1)

            def up(f, i, kts):
                first = PR_FFN + f * PR_PART
                hi(first, i + 1, 0, kts[0])
                act.wait_ge(gemm_done, i * 2 + (first * 2 + 1))
                act.wait_ge(fconv_done, i + (f * FH + 1))
                act.activation(u_f[:, 2:2 + HALF], psum[:, 0, 0:HALF], ACT.Copy)
                act.activation(u_f[:, 2 + HALF:2 + TP], psum[:, 1, 0:TP - HALF], ACT.Copy)
                seqs = u_f[:, 2 + TP:UW].rearrange("p (b t) -> p b t", b=NBATCH)
                act.activation(seqs[:, :, 0:2], f_cols[:, bass.ds(i + f * FH, 1), :].rearrange("p o (b r) -> p (o b) r", b=NBATCH), ACT.Copy)
                act.activation(seqs[:, :, 2:2 + NEW], psum[:, 1, TP - HALF:HALF].rearrange("p (b t) -> p b t", b=NBATCH), ACT.Copy).then_inc(psum_free[0], 1)
                hi(first, i + 1, 1, kts[1])
                act.wait_ge(fconv_done, i + (f * FH + 2))
                act.activation(s_f[:], y_f[:], ACT.Sigmoid).then_inc(fsig_done, 1)

            act.wait_ge(fcols_ready, 1)
            for f in range(2):
                with act.Fori(0, FH - 1) as i:
                    up(f, i, (KD, KD))
                up(f, FH - 1, (FH, FH))
                split_only(PR_FFN + f * PR_PART + FH, 4, (FH, FH), (KD, PT) if f else (KD, KD))
            norm_split(2)
            for k in range(PT):
                act.wait_ge(p_done, k + 1)
                act.activation(p_hi[:, k, 0:TP], psum[:, 5 + 2 * k, :], ACT.Copy)
                act.activation(p_hi[:, k, TP:T], psum[:, 4 + 2 * k, 0:TS], ACT.Copy).then_inc(phi_ready, 1)
            for g in range(6):
                n = min(4, FT - 4 * g)
                act.wait_ge(flast_done, g + 1)
                last = act.activation(f_out[:, 4 * g * P:(4 * g + n) * P], psum[0:18, 4 + g % 2, 0:n * P], ACT.Copy)
                last.then_inc(flast_copied, 1)

            def ple(i, last):
                if not last:
                    hi(PR_PLE, i + 1, 0, KD)
                act.wait_ge(gemm_done, i * 2 + (PR_PLE * 2 + 1))
                act.wait_ge(psum_free[1], i + PR_PLE)
                act.activation(gate_p[:, 0, :].rearrange("p (a t) -> p a t", a=2), acc(0), ACT.Sigmoid).then_inc(psum_free[0], 1)
                if not last:
                    hi(PR_PLE, i + 1, 1, PT)

            with act.Fori(0, KD - 1) as i:
                ple(i, False)
            ple(KD - 1, True)
            act.wait_ge(sum_done, 4)
            act.activation(rstd[:].rearrange("p (a t) -> p a t", a=2), psum[:, 6:8, 0:HALF], ACT.Sqrt, bias=eps_c[:]).then_inc(std_ready, 1)
            for n in range(2 * TB):
                b, half = n // 2, n % 2
                rows = TS if b == QB else P
                act.wait_ge(ytr_done, n + 1)
                if b >= 2:
                    act.wait_ge(y_store[b % 2], 16 * (b // 2))
                act.activation(y_rows[0:rows, b % 2, half * 512:half * 512 + 512], psum[0:rows, n % 4, :], ACT.Copy).then_inc(ytr_copied, 1)

        @block.tensor
        def _(pe):
            pe.wait_ge(cst_in, 16)
            pe.wait_ge(x_in, 16 * TB)
            for k in range(KD):
                s = k % 2
                if k >= 2:
                    pe.wait_ge(x_ready, k - 1)
                for b in range(QB):
                    pe.transpose(psum[:, 2 * s, b * P:(b + 1) * P], xs[:, b, k * P:(k + 1) * P], ident)
                pe.transpose(psum[:, 2 * s + 1, 0:TS], xs[0:TS, QB, k * P:(k + 1) * P], ident[0:TS, 0:TS]).then_inc(xt_done, 1)
            pe.wait_ge(rows_in, 16 * 13)
            pe.transpose(psum[:, 4, 0:ROWS1], rows1[0:ROWS1, :], ident[0:ROWS1, 0:ROWS1]).then_inc(cols_done, 1)
            pe.transpose(psum[:, 5, 0:ROWS2], rows2[0:ROWS2, :], ident[0:ROWS2, 0:ROWS2]).then_inc(cols_done, 1)

            def mean_square(number):
                pe.wait_ge(sq_ready, 2 * KD * (number + 1))
                for a in range(2):
                    last = pe.matmul(psum[:, 6 + a, 0:HALF], mean_d[:], sq[:, 1, a * HALF:(a + 1) * HALF], start=True, stop=True)
                last.then_inc(sum_done, 1)

            pe.wait_ge(consts_ready, 4)
            mean_square(0)

            def chunk(first, i, slot, xhi, xlo, kt):
                pe.wait_ge(hi_ready, (i + first) * 2 + (slot + 1))
                pe.wait_ge(psum_free[slot], i + first)
                for a in range(2):
                    dst, cols = acc(slot)[:, a, :], slice(a * HALF, (a + 1) * HALF)
                    for k in range(kt):
                        pe.matmul(dst, w_hi[:, slot, k, :], xhi[:, k, cols], start=(k == 0), stop=False)
                        pe.matmul(dst, w_hi[:, slot, k, :], xlo[:, k, cols], start=False, stop=False)
                    if a == 0:
                        pe.wait_ge(lo_ready, (i + first) * 2 + (slot + 1))
                    for k in range(kt):
                        last = pe.matmul(dst, w_lo[:, slot, k, :], xhi[:, k, cols], start=False, stop=(k == kt - 1))
                last.then_inc(gemm_done, 1)

            def first_chunks(first, slots, kt, xhi, xlo, arrived, each):
                for slot in slots:
                    pe.wait_ge(lo_ready, first * 2 + slot + 1)
                    if first:
                        pe.wait_ge(psum_free[slot], first)
                for k in range(kt):
                    pe.wait_ge(arrived, each(k))
                    for slot in slots:
                        for a in range(2):
                            dst, cols = acc(slot)[:, a, :], slice(a * HALF, (a + 1) * HALF)
                            pe.matmul(dst, w_hi[:, slot, k, :], xhi[:, k, cols], start=(k == 0), stop=False)
                            pe.matmul(dst, w_hi[:, slot, k, :], xlo[:, k, cols], start=False, stop=False)
                            last = pe.matmul(dst, w_lo[:, slot, k, :], xhi[:, k, cols], start=False, stop=(k == kt - 1))
                        if k == kt - 1:
                            last.then_inc(gemm_done, 1)

            def chunks(first, start, pairs, xs2, kts):
                def one(i):
                    for slot in (0, 1):
                        chunk(first, i, slot, *xs2[slot], kts[slot])

                if pairs - start == 1:
                    one(start)
                else:
                    with pe.Fori(start, pairs) as i:
                        one(i)

            first_chunks(PR_A, (0, 1), KD, a_hi, a_lo, a_ready, lambda k: k + 1)
            pe.wait_ge(ws_ready, 1)
            pe.wait_ge(cols_ready, 2)
            for a in range(2):
                dst, cols = psum[0:96, 4 + a, 0:HALF], slice(a * HALF, (a + 1) * HALF)
                for k in range(KD):
                    pe.matmul(dst, ws_hi[:, k, :], a_hi[:, k, cols], start=(k == 0), stop=False)
                    pe.matmul(dst, ws_hi[:, k, :], a_lo[:, k, cols], start=False, stop=False)
                    last = pe.matmul(dst, ws_lo[:, k, :], a_hi[:, k, cols], start=False, stop=(k == KD - 1))
            last.then_inc(gates_done, 1)
            normed = (a_hi, a_lo)
            chunks(PR_A, 1, 6, (normed, normed), (KD, KD))

            pe.wait_ge(cum_ready, 1)
            for b in range(QB):
                pe.transpose(psum[:, 4, AH * b:AH * b + AH], lsg[0:AH, b * P:(b + 1) * P], ident[0:AH, 0:AH])
                pe.transpose(psum[:, 4, 64 + AH * b:64 + AH * b + AH], cum[:, b * P:(b + 1) * P], ident[0:AH, 0:AH])
            pe.transpose(psum[0:TS, 4, AH * QB:AH * TB], lsg[0:AH, TP:T], ident[0:AH, 0:AH]).then_inc(small_done, 1)
            pe.wait_ge(small_ready, 2)
            pe.wait_ge(psum_free[0], 6)
            pe.wait_ge(psum_free[1], 6)
            for b in range(TB):
                rows = TS if b == QB else P
                for which in range(2):
                    n = 2 * b + which
                    if n >= 4:
                        pe.wait_ge(tok_copied, n - 3)
                    for f in range(WT):
                        last = pe.transpose(psum[0:rows, 4 + n % 4, f * P:(f + 1) * P],
                                            q_a[:, (2 - which) * WT + f, b * P:b * P + rows], ident)
                    last.then_inc(tok_done, 1)
            pe.wait_ge(tok_copied, 2 * TB)

            pe.wait_ge(q_scaled, 1)
            for h in range(AH + 1):
                f, r = h // 2, slice(64 * (h % 2), 64 * (h % 2) + 64)
                if h < AH:
                    if h >= 2:
                        pe.wait_ge(cumb_ready, h - 1)
                    pe.matmul(psum[:, h % 2, :], pick[:, h, :], cum[:, 0:TP], start=True, stop=True).then_inc(cumb_done, 1)
                for i in range(QB + 1):
                    if h < AH and i < QB:
                        n = 4 * h + i
                        if n >= 2:
                            pe.wait_ge(logits_ready, n - 1)
                        pe.matmul(psum[:, 4 + n % 2, 0:P * (i + 1)], q_a[r, f, i * P:(i + 1) * P],
                                  q_a[r, WT + f, 0:P * (i + 1)], start=True, stop=True).then_inc(scores_done, 1)
                    g = h - 1
                    if g < 0:
                        continue
                    gf, gr = g // 2, slice(64 * (g % 2), 64 * (g % 2) + 64)
                    if i < QB:
                        m = 4 * g + i
                        pe.wait_ge(probs_ready, 4 * (g + 1))
                        if m >= 2:
                            pe.wait_ge(pt_copied, m - 1)
                        for b in range(i, QB):
                            o = P * (b * (b + 1) // 2 + i)
                            last = pe.transpose(psum[:, (6, 2)[m % 2], (b - i) * P:(b - i + 1) * P],
                                                probs[:, g % 2, o:o + P], ident)
                        last.then_inc(pt_done, 1)
                    if i >= 1:
                        m = 4 * g + i - 1
                        pe.wait_ge(pt_copied, m + 1)
                        if gf >= 2 and g % 2 == 0 and i == 1:
                            pe.wait_ge(o_lo, gf - 1)
                        pe.matmul(psum[gr, (7, 3)[gf % 2], P * (i - 1):TP], v_tok[:, i - 1, AD * g:AD * g + AD],
                                  pt[:, m % 2, 0:TP - P * (i - 1)], start=(i == 1), stop=(i == QB)).then_inc(pv_done, 1)
            pe.wait_ge(o_lo, 4)

            pe.wait_ge(qblk_ready, AH + 1)
            for p in range(NBATCH // 2 + 1):
                if p < NBATCH // 2:
                    if p >= 2:
                        pe.wait_ge(s_free, p - 1)
                    for b2 in range(2):
                        b = 2 * p + b2
                        pe.wait_ge(kp_in[b2], 64 * (p + 1))
                        rr = slice(64 * b2, 64 * b2 + 64)
                        for f in range(WT + 1):
                            if f < WT:
                                m = 4 * b + f
                                if m >= 2:
                                    pe.wait_ge(ktr_copied, m - 1)
                                for j in range(PAGES):
                                    last = pe.transpose(psum[:, 4 + m % 2, j * P:(j + 1) * P], kp[b2][:, j, f * P:(f + 1) * P], ident)
                                last.then_inc(ktr_done, 1)
                            if f:
                                g = f - 1
                                pe.wait_ge(ktr_copied, 4 * b + g + 1)
                                pe.matmul(psum[rr, 2 + p % 2, :], q_blk[:, g, b, :], kt_s[:, g, :], start=(g == 0), stop=(g == WT - 1)).then_inc(s_done, 1)
                    pe.wait_ge(lrep_ready, 2 * p + 4)
                    for j in range(PAGES):
                        pe.matmul(psum[:, 0, P * j:TP], lrep[:, j, :], tri[:, 0:TP - P * j], start=(j == 0), stop=(j == PAGES - 1))
                    if p:
                        pe.wait_ge(s_free, p)
                    for j in range(PAGES):
                        pe.matmul(psum[:, 1, 0:TS], lrep[:, j, :], ones[:, 0:TS], start=(j == 0), stop=False)
                    pe.matmul(psum[:, 1, 0:TS], lnew[:], c("seq_tri", TS), start=False, stop=True)
                    for b2 in range(2):
                        for g in range(WT):
                            last = pe.matmul(psum[64 * b2:64 * b2 + 64, 1, 64:64 + TS], q_blk[:, g, 2 * p + b2, :], k_new[:, g, :],
                                             start=(g == 0), stop=(g == WT - 1))
                    last.then_inc(cums_done, 1)
                if p:
                    y = p - 1
                    pe.wait_ge(sprobs, y + 1)
                    pe.wait_ge(cums_ready, min(y + 2, NBATCH // 2))
                    for j in range(QB):
                        pe.transpose(psum[:, 6, j * P:(j + 1) * P], ls[:, j * P:(j + 1) * P], ident)
                    pe.transpose(psum[0:TS, 0, 0:P], ls[:, TP:T], ident).then_inc(spt_done, 1)
                    pe.wait_ge(spt_copied, y + 1)
                    for b2 in range(2):
                        pe.wait_ge(vp_in[b2], 64 * (y + 1))
                    if y:
                        pe.wait_ge(so_lo, 2 * y)
                    for b2 in range(2):
                        for f in range(WT):
                            o = 64 * b2 + 16 * f
                            for j in range(PAGES):
                                pe.matmul(psum[:, 7, o:o + 16], vp[:, b2, j, f * P:(f + 1) * P], pts[:, j, o:o + 16], start=(j == 0), stop=False)
                            last = pe.matmul(psum[:, 7, o:o + 16], v_tok[0:TS, QB, f * P:(f + 1) * P], pts[0:TS, QB, o:o + 16], start=False, stop=True)
                    last.then_inc(spv_done, 1)
            pe.wait_ge(s_free, NBATCH // 2)
            pe.wait_ge(spt_copied, NBATCH // 2)
            pe.wait_ge(so_lo, NBATCH)
            chunks(PR_M, 0, 1, (normed, normed), (KD, KD))
            chunks(PR_M, 1, 6, (normed, normed), (KD, KD))
            pe.wait_ge(mrow_ready, 1)
            for h in range(MH):
                if h >= 2:
                    pe.wait_ge(mb_copied, h - 1)
                pe.matmul(psum[:, 4 + h % 2, :], pick[0:MH, h, :], rows_m[:, 3, 0:TP], start=True, stop=True).then_inc(mb_done, 1)
            for h in range(MH):
                pe.matmul(psum[:, 6, TS * h:TS * h + TS], pick[0:MH, h, :], rows_m[:, 3, TP:T], start=True, stop=True)
                pe.matmul(psum[:, 6, TS * (MH + h):TS * (MH + h) + TS], pick[0:MH, h, :], rows_m[:, 0, TP:T], start=True, stop=True)
                pe.matmul(psum[:, 7, TS * h:TS * h + TS], pick[0:MH, h, :], rows_m[:, 4, 0:TS], start=True, stop=True)
            for b in range(TB):
                rows = TS if b == QB else P
                last = pe.transpose(psum[0:rows, 7, 256 + MH * b:256 + MH * b + MH], rows_m[:, 1, b * P:b * P + rows], ident[0:MH, 0:MH])
            last.then_inc(mside_done, 1)
            pe.wait_ge(psum_free[0], PR_M + 6)
            pe.wait_ge(psum_free[1], PR_M + 6)
            pe.wait_ge(kscaled, 1)
            for b in range(TB):
                rows = TS if b == QB else P
                for which in range(2):
                    n = 2 * b + which
                    if n >= 4:
                        pe.wait_ge(mtok_copied, n - 3)
                    for f in range(WT):
                        last = pe.transpose(psum[0:rows, n % 4, f * P:(f + 1) * P], q_m[:, (2 - which) * WT + f, b * P:b * P + rows], ident)
                    last.then_inc(mtok_done, 1)
            pe.wait_ge(mtok_copied, 2 * TB)
            pe.wait_ge(mside_copied, 1)
            pe.wait_ge(mb_copied, MH)
            for n in range(4 * MH + 1):
                if n < 4 * MH:
                    h, j = n // 4, n % 4
                    if j == 0:
                        if h:
                            pe.wait_ge(em_ready, h)
                        pe.matmul(psum[:, 2, :], pick[0:MH, h, :], rows_m[:, 0, 0:TP], start=True, stop=True).then_inc(em_done, 1)
                    if n >= 2:
                        pe.wait_ge(mw_ready, n - 1)
                    pe.matmul(psum[:, 4 + n % 2, 0:TP - P * j], q_m[:, WT + h, P * j:P * j + P], q_m[:, h, P * j:TP],
                              start=True, stop=True).then_inc(mqk_done, 1)
                if n:
                    m = n - 1
                    h, j = m // 4, m % 4
                    pe.wait_ge(mw_ready, m + 1)
                    if h >= 2 and j == 0:
                        pe.wait_ge(h_ready, h - 1)
                    pe.matmul(psum[:, (6, 0)[h % 2], P * j:TP], vm_tok[:, j, h * MD:(h + 1) * MD], decay[:, m % 3, 0:TP - P * j], start=(j == 0), stop=(j == QB - 1))
                    pe.matmul(psum[:, (7, 1)[h % 2], P * j:TP], ones[:], decay[:, m % 3, 0:TP - P * j], start=(j == 0), stop=(j == QB - 1)).then_inc(mpv_done, 1)
            pe.wait_ge(kw_ready, QB)
            for h in range(MH):
                for b in range(QB):
                    last = pe.matmul(psum[:, 3, h * MD:(h + 1) * MD], vm_tok[:, b, h * MD:(h + 1) * MD], k_tok[:, b, h * MD:(h + 1) * MD],
                                     start=(b == 0), stop=(b == QB - 1))
            last.then_inc(cp_done, 1)
            for b in range(QB):
                last = pe.matmul(psum[0:1, 4, :], ones[:, 0:1], k_tok[:, b, :], start=(b == 0), stop=(b == QB - 1))
            last.then_inc(cp_done, 1)
            pe.wait_ge(n_in, 16)
            for h in range(MH):
                pe.transpose(psum[:, 5, NBATCH * h:NBATCH * h + NBATCH], n0[:, h * MD:(h + 1) * MD], ident[0:NBATCH, 0:NBATCH])
            pe.transpose(psum[0:NBATCH, 5, 64:64 + MH], a_last[:], ident[0:MH, 0:MH]).then_inc(nt_done, 1)
            pe.wait_ge(h_ready, MH)
            for h in range(MH):
                last = pe.matmul(psum[0:TS, 2, TS * h:TS * h + TS], q_m[:, WT + h, TP:T], q_m[:, h, TP:T], start=True, stop=True)
            last.then_inc(sqk_done, 1)
            pe.wait_ge(cp_copied, 2)
            for b in range(NBATCH + 1):
                if b < NBATCH:
                    pe.wait_ge(c_in[b % CR], 16 * (b // CR + 1))
                    if b >= 2:
                        pe.wait_ge(ctr_copied, b - 1)
                    for h in range(MH):
                        last = pe.transpose(psum[:, b % 2, h * MD:(h + 1) * MD], c_st[:, b % CR, h, :], ident)
                    last.then_inc(ctr_done, 1)
                    pe.wait_ge(kown_ready, b + 1)
                    if b >= 2:
                        pe.wait_ge(cnew_ready, b - 1)
                    for h in range(MH):
                        last = pe.matmul(psum[:, 3 + b % 2, h * MD:(h + 1) * MD], vm_tok[0:TS, QB, h * MD:(h + 1) * MD], k_own[:, b % 2, h, :], start=True, stop=True)
                    last.then_inc(cadd_done, 1)
                if b:
                    y = b - 1
                    pe.wait_ge(ctr_copied, y + 1)
                    for h in range(MH):
                        last = pe.matmul(psum[:, 6, TS * h + NEW * y:TS * h + NEW * y + NEW], c_t[:, h, :], q_m[:, h, TP + NEW * y:TP + NEW * y + NEW], start=True, stop=True)
                    last.then_inc(inter_done, 1)
            pe.wait_ge(qn_ready, 1)
            pe.wait_ge(sw_ready, 1)
            pe.matmul(psum[:, 7, 0:MH * TS], ones[:], q_m[:, 0:MH, 0:TS], start=True, stop=True)
            for h in range(MH):
                pe.matmul(psum[:, 7, 256 + TS * h:256 + TS * h + TS], ones[0:TS, :], w_s[:, h, :], start=True, stop=True)
                pe.matmul(psum[:, 6, 256 + TS * h:256 + TS * h + TS], vm_tok[0:TS, QB, h * MD:(h + 1) * MD], w_s[:, h, :], start=True, stop=True)
            for h in range(MH):
                last = pe.matmul(psum[0:NBATCH, 5, h * MD:(h + 1) * MD], wl_s[:, h, :], k_tok[0:TS, QB, h * MD:(h + 1) * MD], start=True, stop=True)
            last.then_inc(ssum_done, 1)
            pe.wait_ge(cnew_ready, NBATCH)
            for pair in range(2):
                chunks(PR_O, pair, pair + 1, (normed, normed), (KD, KD))
                pe.wait_ge(hsq_ready, 1)
                if pair:
                    pe.wait_ge(hstd_ready, 1)
                for n in range(4):
                    h, a = 2 * pair + n // 2, n % 2
                    last = pe.matmul(psum[:, 4 + n, 0:HALF], mean_h[:], h_sq[:, h, a * HALF:(a + 1) * HALF], start=True, stop=True)
                last.then_inc(hmean_done, 1)
            chunks(PR_C, 0, 1, (normed, normed), (KD, KD))
            pe.wait_ge(hstd_ready, 2)
            pe.wait_ge(conv_rows_in, 16)
            for f in range(WT):
                last = pe.transpose(psum[:, 4, 16 * f:16 * f + 16], c_rows[:, f * P:(f + 1) * P], ident[0:16, 0:16])
            last.then_inc(ctr2_done, 1)
            chunks(PR_C, 1, 6, (normed, normed), (KD, KD))
            pe.wait_ge(ym_ready, 1)
            with pe.Fori(0, KD) as i:
                for b, branch in enumerate(((ya_hi, ya_lo), (ym_hi, ym_lo), (yc_hi, yc_lo))):
                    chunk(PR_MIX + b, i * 3, 0, *normed, KD)
                    if b == 2:
                        pe.wait_ge(yc_ready, 1)
                    chunk(PR_MIX + b, i * 3, 1, *branch, WT)
            for f in range(WT):
                last = pe.transpose(psum[0:18, 5, f * P:(f + 1) * P], c_last[:, f, :], ident)
            last.then_inc(clast_done, 1)
            mixed = (mg_hi, mg_lo)
            first_chunks(PR_WO, (0, 1), KD, mg_hi, mg_lo, mix_step, lambda k: 4 * (k + 1))
            chunks(PR_WO, 1, 4, (mixed, mixed), (KD, KD))
            mean_square(1)

            pe.wait_ge(f_rows_in, 16)
            for t in range(FT):
                last = pe.transpose(psum[:, 4, 16 * t:16 * t + 16], f_rows[:, t * P:(t + 1) * P], ident[0:16, 0:16])
            last.then_inc(fcols_done, 1)
            first_chunks(PR_FFN, (0, 1), KD, a_hi, a_lo, a_ready, lambda k: KD + k + 1)
            hidden = (hid_hi, hid_lo)
            for f in range(2):
                chunks(PR_FFN + f * PR_PART, 1 - f, FH, (normed, normed), (KD, KD))
                first_chunks(PR_FFN + f * PR_PART + FH, (0, 1), FH, hid_hi, hid_lo, hid_ready, lambda k: f * FH + k + 1)
                chunks(PR_FFN + f * PR_PART + FH, 1, 4, (hidden, hidden), (FH, FH))
            mean_square(2)
            pe.wait_ge(p_rows_in, 16 * TB)
            pe.wait_ge(std_ready, 3)
            for k in range(PT):
                for b in range(QB):
                    pe.transpose(psum[:, 5 + 2 * k, b * P:(b + 1) * P], p_rows[:, b, k * P:(k + 1) * P], ident)
                pe.transpose(psum[:, 4 + 2 * k, 0:TS], p_rows[0:TS, QB, k * P:(k + 1) * P], ident[0:TS, 0:TS]).then_inc(p_done, 1)
            first_chunks(PR_PLE, (0,), KD, a_hi, a_lo, a_ready, lambda k: 2 * KD + k + 1)
            pe.wait_ge(p_ready, PT)
            chunk(PR_PLE, 0, 1, p_hi, p_lo, PT)
            for g in range(6):
                if g >= 2:
                    pe.wait_ge(flast_copied, g - 1)
                for t in range(4 * g, min(4 * g + 4, FT)):
                    last = pe.transpose(psum[0:18, 4 + g % 2, (t - 4 * g) * P:(t - 4 * g + 1) * P], f_last[:, t, :], ident)
                last.then_inc(flast_done, 1)
            chunks(PR_PLE, 1, 8, (normed, (p_hi, p_lo)), (KD, PT))
            mean_square(3)
            pe.wait_ge(psum_free[0], PR_END)
            pe.wait_ge(psum_free[1], PR_END)
            for n in range(2 * TB):
                b, half = n // 2, n % 2
                rows = TS if b == QB else P
                pe.wait_ge(yt_ready, 4 * half + 4)
                if n >= 4:
                    pe.wait_ge(ytr_copied, n - 3)
                for f in range(4):
                    last = pe.transpose(psum[0:rows, n % 4, f * P:(f + 1) * P], y_t[:, 4 * half + f, b * P:b * P + rows], ident)
                last.then_inc(ytr_done, 1)

        @block.vector
        def _(dve):
            steps = [0]

            def link(ins):
                steps[0] += 1
                ins.then_inc(dve_step, 1)
                dve.wait_ge(dve_step, steps[0])

            dve.memset(gbias[:], 0.0).then_inc(gzero, 1)
            dve.wait_ge(cols_done, 1)
            dve.tensor_copy(cols1[:], psum[:, 4, 0:ROWS1]).then_inc(cols_ready, 1)
            dve.wait_ge(cols_done, 2)
            dve.tensor_copy(cols2[:], psum[:, 5, 0:ROWS2]).then_inc(cols_ready, 1)
            dve.wait_ge(cols_ready, 2)

            def add_square(number, k, xk):
                dve.tensor_tensor(sq[:, 0:1, :], xk, xk, ALU.mult).then_inc(sq_ready, 1)
                dve.wait_ge(sq_ready, k * 2 + (2 * KD * number + 1))
                dve.tensor_tensor(sq[:, 1, :], sq[:, 1, :], sq[:, 0, :], ALU.add).then_inc(sq_ready, 1)
                dve.wait_ge(sq_ready, k * 2 + (2 * KD * number + 2))

            def norm(number, gain, last=False):
                dve.wait_ge(std_ready, number + 1)
                link(dve.reciprocal(rstd[:], rstd[:]))
                if last:
                    for k in range(KD):
                        dve.scalar_tensor_tensor(y_t[:, k, :], xT[:, k, :], cols1[:, gain + k:gain + k + 1], rstd[:],
                                                 ALU.mult, ALU.mult).then_inc(yt_ready, 1)
                    return
                for k in range(KD + 1):
                    if k < KD:
                        if k >= 2 or number:
                            dve.wait_ge(ahi_ready, KD * number + k - 1)
                            dve.wait_ge(a_ready, KD * number + k - 1)
                        dve.scalar_tensor_tensor(hn[:, k % 2, :], xT[:, k, :], cols1[:, gain + k:gain + k + 1], rstd[:],
                                                 ALU.mult, ALU.mult).then_inc(hn_ready, 1)
                    if k:
                        dve.wait_ge(ahi_ready, KD * number + k)
                        dve.tensor_tensor(a_lo[:, k - 1, :], hn[:, (k - 1) % 2, :], a_hi[:, k - 1, :].bitcast(F32), ALU.subtract).then_inc(a_ready, 1)

            link(dve.memset(sq[:, 1, :], 0.0))
            for k in range(KD):
                dve.wait_ge(x_ready, k + 1)
                add_square(0, k, xT[:, k:k + 1, :])
            norm(0, GMIX)
            dve.wait_ge(gln_ready, 1)
            link(dve.scalar_tensor_tensor(lsg[:], gs[:], 0.0, ge[:], ALU.min, ALU.subtract))
            dve.tensor_tensor_scan(cum[:], c("keep", AH), lsg[0:AH, :], 0.0, ALU.mult, ALU.add).then_inc(cum_ready, 1)
            dve.wait_ge(psum_free[0], 6)
            dve.wait_ge(psum_free[1], 6)
            dve.tensor_scalar(q_a[:, 0:WT, :], q_a[:, 0:WT, :], AD ** -0.5, None, ALU.mult).then_inc(q_scaled, 1)
            dve.wait_ge(small_ready, 2)

            def scale_rows(n):
                i = n % 4
                g = n // 4
                o = P * (i * (i + 1) // 2)
                dve.wait_ge(exp_done, n + 1)
                link(dve.reciprocal(rinv[:, n % 2:n % 2 + 1], rsum[:, n % 2:n % 2 + 1]))
                dve.tensor_scalar(probs[:, g % 2, o:o + P * (i + 1)], probs[:, g % 2, o:o + P * (i + 1)], rinv[:, n % 2:n % 2 + 1], None,
                                  ALU.mult).then_inc(probs_ready, 1)

            for n in range(4 * AH + 1):
                if n < 4 * AH:
                    h, i = n // 4, n % 4
                    w = P * (i + 1)
                    if i == 0:
                        dve.wait_ge(cumb_ready, h + 1)
                    dve.wait_ge(scores_done, n + 1)
                    if n >= 2:
                        dve.wait_ge(exp_done, n - 1)
                    dve.scalar_tensor_tensor(logits[:, n % 2, 0:w], psum[:, 4 + n % 2, 0:w], cq[:, i, h:h + 1], cumb[:, h % 2, 0:w],
                                             ALU.add, ALU.subtract).then_inc(logits_ready, 1)
                    dve.wait_ge(logits_ready, n + 1)
                    diag = logits[:, n % 2, w - P:w]
                    link(dve.tensor_tensor(diag, diag, c("future_keys"), ALU.add))
                    dve.tensor_reduce(nmax[:, n % 2:n % 2 + 1], logits[:, n % 2, 0:w], AX_X, ALU.max, negate=True).then_inc(nmax_ready, 1)
                if n:
                    scale_rows(n - 1)
                if n >= 12 and (n - 12) % 8 == 0 or n == 4 * AH:
                    f = (n - 12) // 8 if n < 4 * AH else 3
                    if n < 4 * AH or True:
                        dve.wait_ge(o_hi, f + 1)
                        dve.tensor_tensor(ya_lo[:, f, 0:TP], psum[:, (7, 3)[f % 2], :], ya_hi[:, f, 0:TP].bitcast(F32), ALU.subtract).then_inc(o_lo, 1)

            for y in range(NBATCH // 2):
                dve.wait_ge(cums_ready, y + 1)
                dve.wait_ge(s_done, 8 * (y + 1))
                link(dve.tensor_tensor(tmp64[:], cums[:, TP:T], c("own_key")[:, TS * y:TS * (y + 1)], ALU.mult))
                link(dve.tensor_reduce(rinv[:, 1:2], tmp64[:], AX_X, ALU.add))
                if y:
                    dve.wait_ge(spt_done, y)
                dve.scalar_tensor_tensor(ls[:, 0:TP], psum[:, 2 + y % 2, :], rinv[:, 1:2], cums[:, 0:TP], ALU.add, ALU.subtract)
                link(dve.scalar_tensor_tensor(ls[:, TP:T], psum[:, 1, 64:64 + TS], rinv[:, 1:2], cums[:, TP:T],
                                              ALU.add, ALU.subtract))
                dve.tensor_tensor(ls[:, TP:T], ls[:, TP:T], c("new_keys")[:, TS * y:TS * (y + 1)], ALU.add).then_inc(s_free, 1)
                dve.wait_ge(s_free, y + 1)
                dve.tensor_reduce(nmax[:, 0:1], ls[:], AX_X, ALU.max, negate=True).then_inc(snmax, 1)
                dve.wait_ge(sexp, y + 1)
                link(dve.reciprocal(rinv[:, 0:1], rsum[:, 0:1]))
                dve.tensor_scalar(ls[:], ls[:], rinv[:, 0:1], None, ALU.mult).then_inc(sprobs, 1)
                for hh in range(2):
                    r = slice(64 * hh, 64 * hh + 64)
                    dve.wait_ge(so_hi, 2 * y + hh + 1)
                    dve.tensor_tensor(ya_lo[r, :, TP + 16 * y:TP + 16 * y + 16].rearrange("p f (b q) -> p b f q", b=2),
                                      psum[r, 7, 0:128].rearrange("p (b f r) -> p b f r", b=2, f=WT)[:, :, :, 8 * hh:8 * hh + 8],
                                      ya_hi[r, :, TP + 16 * y:TP + 16 * y + 16].rearrange("p f (b q) -> p b f q", b=2).bitcast(F32),
                                      ALU.subtract).then_inc(so_lo, 1)
            link(dve.tensor_copy(rows_m[:, 0, :], lsg[64:64 + MH, :]))
            link(dve.tensor_copy(rows_m[:, 1, :], gs[32:32 + MH, :]))
            dve.engine_nop().then_inc(rows_ready, 1)
            link(dve.tensor_tensor_scan(rows_m[:, 2, :], c("keep", MH), rows_m[:, 0, :], 0.0, ALU.mult, ALU.add))
            link(dve.tensor_tensor(rows_m[:, 1, :], rows_m[:, 1, :], rows_m[:, 2, :], ALU.subtract))
            link(dve.tensor_copy(rows_m[:, 4, :], rows_m[:, 1, :]))
            dve.wait_ge(m0_in, 16)
            link(dve.tensor_scalar(rows_m[:, 4, 0:1], rows_m[:, 4, 0:1], 0.0, None, ALU.max))
            link(dve.tensor_tensor(rows_m[:, 4, TP:T:NEW], rows_m[:, 4, TP:T:NEW], m0[:], ALU.max))
            link(dve.tensor_tensor_scan(rows_m[:, 3, :], c("restart", MH), rows_m[:, 4, :], -BIG, ALU.add, ALU.max))
            link(dve.tensor_tensor(rows_m[:, 0, :], rows_m[:, 2, :], rows_m[:, 3, :], ALU.add))
            dve.tensor_tensor(rows_m[:, 4, 0:TS].rearrange("p (b t) -> p b t", b=NBATCH), m0[:].unsqueeze(2).broadcast_to([MH, NBATCH, NEW]),
                              rows_m[:, 3, TP:T].rearrange("p (b t) -> p b t", b=NBATCH), ALU.subtract).then_inc(mrow_ready, 1)
            dve.wait_ge(psum_free[0], PR_M + 6)
            dve.wait_ge(psum_free[1], PR_M + 6)
            dve.tensor_scalar(q_m[:, WT:2 * WT, :], q_m[:, WT:2 * WT, :], MD ** -0.5, None, ALU.mult).then_inc(kscaled, 1)
            dve.wait_ge(mside_copied, 1)
            dve.tensor_tensor(wl_p[:], g_col[:, 0:QB, :], m_all[:, :, TP - 1].unsqueeze(1).broadcast_to([P, QB, MH]), ALU.subtract).then_inc(wl_sub, 1)
            link(dve.tensor_tensor(wl_s[:], g_col[0:TS, QB, :].unsqueeze(2).broadcast_to([TS, MH, NBATCH]), m_all[0:TS, :, TP + NEW - 1:T:NEW], ALU.subtract))
            link(dve.tensor_scalar(wl_s[:], wl_s[:], 0.0, None, ALU.min))
            dve.tensor_tensor(wl_s[:], wl_s[:], c("not_seq", TS).unsqueeze(1).broadcast_to([TS, MH, NBATCH]), ALU.add).then_inc(wl_sub, 1)

            def decays(n):
                h, j = n // 4, n % 4
                w = TP - P * j
                if n >= 3:
                    dve.wait_ge(mpv_done, n - 2)
                link(dve.tensor_scalar(decay[:, n % 3, 0:w], m_all[:, h, P * j:TP], g_col[:, j, h:h + 1], 0.0, ALU.subtract, ALU.max))
                dve.tensor_tensor(decay[:, n % 3, 0:P], decay[:, n % 3, 0:P], c("past_rows"), ALU.add).then_inc(mdec_ready, 1)

            def finish_head(h):
                dve.wait_ge(mpv_done, 4 * (h + 1))
                dve.wait_ge(em_ready, h + 1)
                e = e_m[:, h % 2, :]
                link(dve.scalar_tensor_tensor(e, psum[:, (7, 1)[h % 2], :], -1.0, e, ALU.mult, ALU.max))
                link(dve.tensor_tensor(e, psum[:, (7, 1)[h % 2], :], e, ALU.max))
                link(dve.reciprocal(e, e))
                dve.tensor_tensor(h_t[:, h, 0:TP], psum[:, (6, 0)[h % 2], :], e, ALU.mult).then_inc(h_ready, 1)

            dve.wait_ge(mtok_done, 2 * TB)
            decays(0)
            for n in range(4 * MH):
                if n + 1 < 4 * MH:
                    decays(n + 1)
                w = TP - P * (n % 4)
                dve.wait_ge(mexp_done, n + 1)
                dve.wait_ge(mqk_done, n + 1)
                dve.tensor_tensor(decay[:, n % 3, 0:w], psum[:, 4 + n % 2, 0:w], decay[:, n % 3, 0:w], ALU.mult).then_inc(mw_ready, 1)
                if n % 4 == 1 and n > 4:
                    finish_head(n // 4 - 1)
            finish_head(MH - 1)

            gc_s = g_col[0:TS, QB, :].unsqueeze(2).broadcast_to([TS, MH, TS])
            link(dve.tensor_tensor(w_s[:], m_all[0:TS, :, TP:T], gc_s, ALU.subtract))
            link(dve.tensor_scalar(w_s[:], w_s[:], 0.0, None, ALU.max))
            dve.tensor_tensor(w_s[:], w_s[:], c("seq_past", TS).unsqueeze(1).broadcast_to([TS, MH, TS]), ALU.add).then_inc(sdec_ready, 1)
            dve.wait_ge(nt_copied, 1)
            q_s = q_m[:, 0:MH, TP:T].rearrange("p h (b t) -> p h b t", b=NBATCH)
            for h in range(MH):
                last = dve.tensor_tensor(q_m[:, h, 0:TS].rearrange("p (b t) -> p b t", b=NBATCH), q_s[:, h],
                                         n_t[:, h, :].unsqueeze(2).broadcast_to([P, NBATCH, NEW]), ALU.mult)
            last.then_inc(qn_ready, 1)
            dve.wait_ge(sdexp_done, 1)
            dve.wait_ge(sqk_done, 1)
            dve.tensor_tensor(w_s[:], psum[0:TS, 2, 0:MH * TS].rearrange("p (h t) -> p h t", h=MH), w_s[:], ALU.mult).then_inc(sw_ready, 1)
            for b in range(NBATCH):
                dve.wait_ge(ctr_done, b + 1)
                cb = c_st[:, b % CR]
                link(dve.tensor_tensor(cb, cb, a_s[:, :, NEW * b + NEW - 1:NEW * b + NEW].broadcast_to([P, MH, MD]), ALU.mult))
                dve.wait_ge(cadd_done, b + 1)
                dve.tensor_tensor(cb, psum[:, 3 + b % 2, :].rearrange("p (h e) -> p h e", h=MH), cb, ALU.add).then_inc(cnew_ready, 1)
            n_v = n0[:].rearrange("p (h e) -> p h e", h=MH)
            link(dve.tensor_tensor(n_v, n_v, a_last_t[:].unsqueeze(2).broadcast_to([NBATCH, MH, MD]), ALU.mult))
            dve.wait_ge(ssum_done, 1)
            dve.tensor_tensor(n0[:], psum[0:NBATCH, 5, :], n0[:], ALU.add).then_inc(n_new_ready, 1)
            dve.wait_ge(inter_done, NBATCH)

            def quad(bank, o):
                return psum[:, bank, o:o + MH * TS].rearrange("p (h t) -> p h t", h=MH)

            num, den = q_m[:, 0:MH, TS:2 * TS], q_m[:, 0:MH, 2 * TS:3 * TS]
            link(dve.tensor_tensor(num, quad(6, 0), a_s[:], ALU.mult))
            link(dve.tensor_tensor(num, quad(6, 256), num, ALU.add))
            link(dve.tensor_tensor(den, quad(7, 0), a_s[:], ALU.mult))
            link(dve.tensor_tensor(den, quad(7, 256), den, ALU.add))
            link(dve.scalar_tensor_tensor(e_ms[:], den, -1.0, e_ms[:], ALU.mult, ALU.max))
            link(dve.tensor_tensor(den, den, e_ms[:], ALU.max))
            link(dve.reciprocal(den, den))
            link(dve.tensor_tensor(h_t[:, :, TP:T], num, den, ALU.mult))
            dve.tensor_tensor(h_sq[:], h_t[:], h_t[:], ALU.mult).then_inc(hsq_ready, 1)
            dve.wait_ge(hstd_ready, 2)
            link(dve.reciprocal(h_sq[:], h_sq[:]))
            link(dve.tensor_tensor(h_t[:], h_t[:], h_sq[:], ALU.mult))
            dve.wait_ge(psum_free[0], PR_O + 2)
            dve.wait_ge(psum_free[1], PR_O + 2)
            for h in range(MH):
                last = dve.scalar_tensor_tensor(h_t[:, h, :], h_t[:, h, :], cols1[:, GMH + h:GMH + h + 1], sig_o[:, h, :], ALU.mult, ALU.mult)
            last.then_inc(ym_full, 1)
            dve.wait_ge(ymhi_ready, 1)
            dve.tensor_tensor(ym_lo[:], h_t[:], ym_hi[:].bitcast(F32), ALU.subtract).then_inc(ym_ready, 1)
            link(dve.memset(u_c[:, :, 0:2], 0.0))
            dve.wait_ge(ctr2_done, 1)

            def seqs(x):
                return x.rearrange("p (b t) -> p b t", b=NBATCH)

            def seqs4(x):
                return x.rearrange("p f (b t) -> p f b t", b=NBATCH)

            us = seqs4(u_c[:, :, 2 + TP:UW])
            dve.tensor_copy(us[:, :, :, 0:2], psum[:, 4, 0:16 * WT].rearrange("p (f b r) -> p f b r", f=WT, b=NBATCH))
            for g in range(2):
                for slot in (0, 1):
                    dve.wait_ge(psum_free[slot], PR_C + 5 + g)
                fs2 = slice(2 * g, 2 * g + 2)
                b_in, c_in2, x_in2 = (c_buf[:, WT * n + 2 * g:WT * n + 2 * g + 2, :] for n in range(3))
                dve.tensor_tensor(u_c[:, fs2, 2:2 + TP], c_in2[:, :, 0:TP], x_in2[:, :, 0:TP], ALU.mult)
                link(dve.tensor_tensor(us[:, fs2, :, 2:2 + NEW], seqs4(c_in2[:, :, TP:T]), seqs4(x_in2[:, :, TP:T]), ALU.mult))
                dve.tensor_copy(c_last[:, fs2, 0:2], u_c[:, fs2, TP:TP + 2])
                dve.tensor_copy(c_last[:, fs2, 2:18].rearrange("p f (b r) -> p f b r", b=NBATCH), us[:, fs2, :, NEW:NEW + 2])
                for j in (2, 1, 0):
                    for f in (2 * g, 2 * g + 1):
                        w = cols1[:, WSC + WT * j + f:WSC + WT * j + f + 1]
                        y = c_buf[:, WT + f, :]
                        if j == 2:
                            dve.tensor_scalar(y[:, 0:TP], u_c[:, f, 2:2 + TP], w, None, ALU.mult)
                            last = dve.tensor_scalar(seqs(y[:, TP:T]), us[:, f, :, 2:2 + NEW], w, None, ALU.mult)
                        else:
                            dve.scalar_tensor_tensor(y[:, 0:TP], u_c[:, f, j:j + TP], w, y[:, 0:TP], ALU.mult, ALU.add)
                            last = dve.scalar_tensor_tensor(seqs(y[:, TP:T]), us[:, f, :, j:j + NEW], w, seqs(y[:, TP:T]), ALU.mult, ALU.add)
                    link(last)
                dve.tensor_tensor(c_in2, c_in2, b_in, ALU.mult).then_inc(yc_full, 1)
            for g in range(2):
                fs2 = slice(2 * g, 2 * g + 2)
                dve.wait_ge(ychi_ready, g + 1)
                last = dve.tensor_tensor(yc_lo[:, fs2, :], c_buf[:, WT + 2 * g:WT + 2 * g + 2, :], yc_hi[:, fs2, :].bitcast(F32), ALU.subtract)
            last.then_inc(yc_ready, 1)

            def halves(x):
                return x.rearrange("p (a t) -> p a t", a=2)

            with dve.Fori(0, KD) as i:
                for b in range(3):
                    dve.wait_ge(gemm_done, i * 6 + ((PR_MIX + b) * 2 + 2))
                    dve.wait_ge(psum_free[0], i * 3 + (PR_MIX + b + 1))
                    dve.tensor_tensor(halves(mix[:, min(b, 1), :]), acc(1), halves(gate[:, b, :]), ALU.mult).then_inc(psum_free[1], 1)
                    dve.wait_ge(psum_free[1], i * 3 + (PR_MIX + b + 1))
                    if b:
                        dve.tensor_tensor(mix[:, 0, :], mix[:, 0, :], mix[:, 1, :], ALU.add).then_inc(mix_step, 1)
                        dve.wait_ge(mix_step, i * 4 + b)
                whole = mix[:, 0:1, :]
                dve.tensor_copy(mg_hi[:, bass.ds(i, 1), :], whole).then_inc(mix_step, 1)
                dve.wait_ge(mix_step, i * 4 + 3)
                dve.tensor_tensor(mg_lo[:, bass.ds(i, 1), :], whole, mg_hi[:, bass.ds(i, 1), :].bitcast(F32), ALU.subtract).then_inc(mix_step, 1)
                dve.wait_ge(mix_step, i * 4 + 4)

            def add_to_stream(first, pairs, number):
                if number:
                    link(dve.memset(sq[:, 1, :], 0.0))
                with dve.Fori(0, pairs) as i:
                    for slot in (0, 1):
                        dve.wait_ge(gemm_done, i * 2 + (first * 2 + slot + 1))
                        xk = xT[:, bass.ds(i * 2 + slot, 1), :].rearrange("p o (a t) -> p (o a) t", a=2)
                        dve.tensor_tensor(xk, acc(slot), xk, ALU.add).then_inc(psum_free[slot], 1)
                        if number:
                            dve.wait_ge(psum_free[slot], i + (first + 1))
                            add_square(number, i * 2 + slot, xT[:, bass.ds(i * 2 + slot, 1), :])

            add_to_stream(PR_WO, 4, 1)
            norm(1, GFFN)
            dve.wait_ge(fcols_done, 1)
            dve.tensor_copy(f_cols[:], psum[:, 4, 0:16 * FT].rearrange("p (t r) -> p t r", t=FT)).then_inc(fcols_ready, 1)

            dve.memset(u_f[:, 0:2], 0.0).then_inc(fconv_done, 1)
            fs = seqs(u_f[:, 2 + TP:UW])
            for f in range(2):
                first = PR_FFN + f * PR_PART
                with dve.Fori(0, FH) as i:
                    t0 = f * FH

                    def col(j):
                        return cols2[:, bass.ds(i + (j * FT + t0), 1)]

                    dve.wait_ge(psum_free[0], i + (first + 1))
                    lt = f_last[:, bass.ds(i + t0, 1), :]
                    dve.tensor_copy(lt[:, :, 0:2], u_f[:, TP:TP + 2].unsqueeze(1))
                    dve.tensor_copy(lt[:, :, 2:18].rearrange("p o (b r) -> p (o b) r", b=NBATCH), fs[:, :, NEW:NEW + 2])
                    dve.tensor_scalar(y_f[:, 0:TP], u_f[:, 2:2 + TP], col(2), col(3), ALU.mult, ALU.add)
                    dve.tensor_scalar(seqs(y_f[:, TP:T]), fs[:, :, 2:2 + NEW], col(2), col(3), ALU.mult, ALU.add).then_inc(fstep, 1)
                    dve.wait_ge(fstep, i * 4 + (4 * t0 + 1))
                    for j in (1, 0):
                        dve.scalar_tensor_tensor(y_f[:, 0:TP], u_f[:, j:j + TP], col(j), y_f[:, 0:TP], ALU.mult, ALU.add)
                        last = dve.scalar_tensor_tensor(seqs(y_f[:, TP:T]), fs[:, :, j:j + NEW], col(j), seqs(y_f[:, TP:T]), ALU.mult, ALU.add)
                        if j:
                            last.then_inc(fstep, 1)
                            dve.wait_ge(fstep, i * 4 + (4 * t0 + 2))
                        else:
                            last.then_inc(fconv_done, 1)
                    dve.wait_ge(fsig_done, i + (t0 + 1))
                    dve.tensor_tensor(y_f[:], y_f[:], s_f[:], ALU.mult).then_inc(fstep, 1)
                    dve.wait_ge(fstep, i * 4 + (4 * t0 + 3))
                    dve.wait_ge(gemm_done, i * 2 + (first * 2 + 2))
                    dve.tensor_tensor(halves(y_f[:]), acc(1), halves(y_f[:]), ALU.mult).then_inc(psum_free[1], 1)
                    dve.wait_ge(psum_free[1], i + (first + 1))
                    dve.tensor_copy(hid_hi[:, bass.ds(i, 1), :], y_f[:].unsqueeze(1)).then_inc(fstep, 1)
                    dve.wait_ge(fstep, i * 4 + (4 * t0 + 4))
                    dve.tensor_tensor(hid_lo[:, bass.ds(i, 1), :], y_f[:].unsqueeze(1), hid_hi[:, bass.ds(i, 1), :].bitcast(F32), ALU.subtract).then_inc(hid_ready, 1)
                    dve.wait_ge(hid_ready, i + (t0 + 1))
                add_to_stream(first + FH, 4, 2 * f)
            norm(2, GPLE)
            for k in range(PT):
                dve.wait_ge(phi_ready, k + 1)
                dve.tensor_tensor(p_lo[:, k, 0:TP], psum[:, 5 + 2 * k, :], p_hi[:, k, 0:TP].bitcast(F32), ALU.subtract)
                dve.tensor_tensor(p_lo[:, k, TP:T], psum[:, 4 + 2 * k, 0:TS], p_hi[:, k, TP:T].bitcast(F32), ALU.subtract).then_inc(p_ready, 1)
            link(dve.memset(sq[:, 1, :], 0.0))
            with dve.Fori(0, KD) as i:
                dve.wait_ge(psum_free[0], i + (PR_PLE + 1))
                dve.wait_ge(gemm_done, i * 2 + (PR_PLE * 2 + 2))
                dve.tensor_tensor(halves(emb[:]), acc(1), halves(gate_p[:, 0, :]), ALU.mult).then_inc(psum_free[1], 1)
                dve.wait_ge(psum_free[1], i + (PR_PLE + 1))
                xk = xT[:, bass.ds(i, 1), :]
                dve.tensor_tensor(xk, xk, emb[:].unsqueeze(1), ALU.add).then_inc(xple_ready, 1)
                dve.wait_ge(xple_ready, i + 1)
                add_square(3, i, xk)
            norm(3, GFIN, last=True)



_INS = ["x_prompt", "x_sample", "cache_k", "cache_v", "cache_logf", "state_mlstm_C", "state_mlstm_n", "state_mlstm_m",
        "state_conv", "state_ffn_conv", "page_table", "p_prompt", "p_sample", "w_in", "b_in", "g_mix", "g_mhead",
        "w_sconv", "w_oa", "w_om", "w_oc", "w_o", "g_ffn", "w_up", "w_fconv", "b_fconv", "w_down", "g_ple",
        "w_ple_gate", "w_ple", "g_final"]
_OUTS = [("y_prompt", (1, 512, 1024)), ("y_sample", (8, 8, 1024)),
         ("k_p", (1, 512, 1, 8, 64)), ("v_p", (1, 512, 1, 8, 64)), ("logf_p", (1, 512, 1, 8)),
         ("C_p", (1, 1, 4, 128, 128)), ("n_p", (1, 1, 4, 128)), ("m_p", (1, 1, 4)),
         ("conv_p", (1, 1, 2, 512)), ("ffn_p", (1, 1, 2, 2816)),
         ("k_s", (8, 8, 1, 8, 64)), ("v_s", (8, 8, 1, 8, 64)), ("logf_s", (8, 8, 1, 8)),
         ("C_s", (8, 1, 4, 128, 128)), ("n_s", (8, 1, 4, 128)), ("m_s", (8, 1, 4)),
         ("conv_s", (8, 1, 2, 512)), ("ffn_s", (8, 1, 2, 2816))]


def kernel(**inputs):
    import numpy as _np
    import concourse.bacc as _bacc
    from concourse import mybir as _mybir
    from concourse.bass_utils import run_bass_kernel_spmd as _run

    nc = _bacc.Bacc("TRN2", target_bir_lowering=False, num_devices=1)
    arrays, d = {}, {}
    for name in _INS:
        a = _np.ascontiguousarray(inputs[name])
        arrays[f"in_{name}"] = a
        d[name] = nc.dram_tensor(f"in_{name}", a.shape, _mybir.dt.from_np(a.dtype), kind="ExternalInput").ap()
    parts = tables()
    at, ncst = layout(parts)
    arrays["in_cst"] = _np.concatenate([_np.asarray(a, _np.float32) for a in parts.values()], 1)
    d["cst"] = nc.dram_tensor("in_cst", (P, ncst), F32, kind="ExternalInput").ap()
    for name, shape in _OUTS:
        d[name] = nc.dram_tensor(f"out_{name}", shape, F32, kind="ExternalOutput").ap()
    build(nc, d, at, ncst)
    r = _run(nc, [arrays], core_ids=[0])
    return tuple(r.results[0][f"out_{name}"] for name, _ in _OUTS)
```

```python
from contextlib import ExitStack

import numpy as np

import concourse.bass as bass
from concourse import mybir

F32 = mybir.dt.float32
F32R = mybir.dt.float32r
I32 = mybir.dt.int32
ALU = mybir.AluOpType
ACT = mybir.ActivationFunctionType
AX_X = mybir.AxisListType.X

P = 128
D = 1024
KD = D // P
TP = 512
NBATCH, NEW = 8, 8
TS = NBATCH * NEW
T = TP + TS
HALF = T // 2
QB = TP // P
TB = QB + 1
AH, AD = 8, 64
MH, MD = 4, 128
CW = 512
WT = CW // P
FF = 2816
FT = FF // P
FH = FT // 2
PLE = 256
PT = PLE // P
PAGE, PAGES = 128, 4
NPHYS = 40
EPS = 1e-6
BIG = 1e30
COL_A, COL_AF, COL_M, COL_MI, COL_MF, COL_MO, COL_C, COL_G = 0, 1536, 1544, 3080, 3084, 3088, 3600, 5136

BA, BM, BO, BC, BG = 0, 12, 24, 28, 40
GMIX, GFFN, GPLE, GFIN, GMH, WSC = 64, 72, 80, 88, 96, 100
ROWS1, ROWS2 = 112, 4 * FT

PR_A, PR_M, PR_O, PR_C, PR_MIX, PR_WO = 0, 6, 12, 14, 20, 44
PR_FFN = 48
PR_PART = FH + 4
PR_PLE = PR_FFN + 2 * PR_PART
PR_END = PR_PLE + 8


def tables():
    parts = {}
    r = np.arange(P)
    parts["ident"] = np.eye(P)
    parts["tri"] = np.concatenate([r[:, None] <= r[None, :], np.ones((P, TP - P + TS))], 1)
    parts["future_keys"] = np.where(r[None, :] <= r[:, None], 0.0, -BIG)
    parts["past_rows"] = np.where(r[:, None] <= r[None, :], 0.0, BIG)
    t = np.arange(TS)
    same = (t[:, None] // NEW == t[None, :] // NEW) & (t[:, None] <= t[None, :])
    parts["seq_tri"] = np.zeros((P, TS))
    parts["seq_tri"][:TS] = same
    parts["seq_past"] = np.zeros((P, TS))
    parts["seq_past"][:TS] = np.where(same, 0.0, BIG)
    row_b, row_q = r // 64, r % NEW
    allowed = np.zeros((P, 4, TS))
    own = np.zeros((P, 4, TS))
    for pair in range(4):
        b = 2 * pair + row_b
        allowed[:, pair] = (t[None, :] // NEW == b[:, None]) & (t[None, :] % NEW <= row_q[:, None])
        own[:, pair] = (t[None, :] // NEW == b[:, None]) & (t[None, :] % NEW == row_q[:, None])
    parts["new_keys"] = np.where(allowed > 0, 0.0, -BIG).reshape(P, 4 * TS)
    parts["own_key"] = own.reshape(P, 4 * TS)
    parts["not_seq"] = np.zeros((P, NBATCH))
    parts["not_seq"][:TS] = np.where(t[:, None] // NEW == np.arange(NBATCH)[None, :], 0.0, -BIG)
    parts["pick"] = np.zeros((P, AH * P))
    for h in range(AH):
        parts["pick"][h, h * P:(h + 1) * P] = 1.0
    starts = np.zeros(T)
    starts[0] = 1
    starts[TP::NEW] = 1
    parts["keep"] = np.broadcast_to(1.0 - starts, (P, T))
    parts["restart"] = np.broadcast_to(-BIG * starts, (P, T))
    return parts


def layout(parts):
    at, n = {}, 0
    for name, a in parts.items():
        at[name] = (n, a.shape[1])
        n += a.shape[1]
    return at, n



def build(nc, d, at, ncst):
    ctx = ExitStack()
    with ctx:
        def sem(name):
            return ctx.enter_context(nc.semaphore(name))

        base = (nc.sbuf_base + 31) // 32 * 32
        ctx.enter_context(nc.sbuf_tensor("arena", [P, (nc.sbuf_bytes_remaining - 64) // 4], F32))
        room = nc.sbuf_usable_end - base
        fixed = [0]

        def place(name, shape, dt, off):
            size = 4 * int(np.prod(shape[1:]))
            assert off % 32 == 0 and off + size <= room, (name, off, size, room)
            return nc.alloc_sbuf_tensor_at(name, shape, dt, offset=base + off)

        def keep(name, shape, dt=F32):
            size = (4 * int(np.prod(shape[1:])) + 31) // 32 * 32
            t = place(name, shape, dt, fixed[0])
            fixed[0] += size
            return t

        xT = keep("xT", [P, KD, T])
        a_hi = keep("a_hi", [P, KD, T], F32R)
        a_lo = keep("a_lo", [P, KD, T], F32R)
        raw = keep("raw", [P, 2, FH, P])
        w_hi = keep("w_hi", [P, 2, FH, P], F32R)
        w_lo = keep("w_lo", [P, 2, FH, P], F32R)
        IN_W, EARLY = 5, 6
        c_st = [place(f"c_st{b}", [P, MH, MD], F32, fixed[0] - 2 * 8 * FH * P + b * 4 * CW) for b in range(IN_W)]
        cst = keep("cst", [P, ncst])
        ones = keep("ones", [P, P])
        mean_d = keep("mean_d", [P, P])
        mean_h = keep("mean_h", [P, P])
        cols1 = keep("cols1", [P, ROWS1])
        cols2 = keep("cols2", [P, ROWS2])
        gbias = keep("gbias", [P, 1])
        eps_c = keep("eps_c", [P, 1])
        rstd = keep("rstd", [P, T])
        pages = keep("pages", [P, NBATCH * PAGES], I32)
        L = fixed[0]

        def local(name, shape, dt, off):
            return place(name, shape, dt, L + off)

        def c(name, rows=P):
            o, n = at[name]
            return cst[0:rows, o:o + n]

        ident = c("ident")
        tri = c("tri")
        pick = c("pick", AH).rearrange("p (h m) -> p h m", h=AH)
        YB = 4 * WT * T
        ya_hi, ya_lo = (local(n, [P, WT, T], F32R, i * YB) for i, n in enumerate(("ya_hi", "ya_lo")))

        xs = local("xs", [P, TB, D], F32, 0)
        rows1 = local("rows1", [P, P], F32, 20480)
        rows2 = local("rows2", [P, P], F32, 20992)
        ws = local("ws", [P, KD, 96], F32, 21504)
        ws_hi = local("ws_hi", [P, KD, 96], F32R, 24576)
        ws_lo = local("ws_lo", [P, KD, 96], F32R, 27648)
        sq = local("sq", [P, 2, T], F32, 30720)
        hn = local("hn", [P, 2, T], F32, 30720 + 8 * T)

        SM = 81152
        q_a = local("q_a", [P, 3 * WT, T], F32, 2 * YB)
        v_tok = local("v_tok", [P, TB, CW], F32, 46080)
        NPK = P * (1 + 2 + 3 + 4)
        probs = local("probs", [P, 2, NPK], F32, 60416)
        kstage = local("kstage", [P, 2, CW], F32, 60416)
        pt = local("pt", [P, 2, TP], F32, 74752)
        gs = local("gs", [96, T], F32, SM)
        ge = local("ge", [96, T], F32, SM + 2304)
        lsg = local("lsg", [96, T], F32, SM + 4608)
        ncum = local("ncum", [AH, T], F32, SM + 6912)
        lf_tok = local("lf_tok", [P, TB, AH], F32, SM + 9344)
        nmax = local("nmax", [P, 4], F32, SM + 9504)
        rsum = local("rsum", [P, 4], F32, SM + 9536)
        rinv = local("rinv", [P, 4], F32, SM + 9568)
        SS = SM + 9600
        q_blk = local("q_blk", [P, WT, NBATCH, 64], F32, SS)
        k_new = local("k_new", [P, WT, TS], F32, SS + 8192)

        kp = [local("kp0", [P, PAGES, CW], F32, 37376), local("kp1", [P, PAGES, CW], F32, 2 * YB)]
        kt_s = local("kt_s", [P, WT, TP], F32, 2 * YB + 8192)
        cums = local("cums", [P, T], F32, 2 * YB + 16384)
        vp = local("vp", [P, 2, PAGES, CW], F32, 56320)
        lrep = local("lrep", [P, PAGES, P], F32, 72704)
        lnew = local("lnew", [TS, P], F32, 74752)
        lpast = local("lpast", [P, NBATCH, PAGES, AH], F32, SM + 2304)
        pts = local("pts", [P, TB, P], F32, 76288)
        ls = local("ls", [P, T], F32, 78848)
        tmp64 = local("tmp64", [P, TS], F32, SS + 9216)
        o_tok = local("o_tok", [P, CW], F32, SS + 9472)

        q_m = local("q_m", [P, 3 * WT, T], F32, 2 * YB)
        k_tok = local("k_tok", [P, TB, CW], F32, 46080)
        vm_tok = local("vm_tok", [P, TB, CW], F32, 56320)
        sig_o = local("sig_o", [P, WT, T], F32, 3 * YB)
        m_all = local("m_all", [P, MH, T], F32, 66560)
        decay = local("decay", [P, 3, TP], F32, 75776)
        e_m = local("e_m", [P, 2, TP], F32, 81920)
        n0 = local("n0", [NBATCH, CW], F32, 86016)
        rows_m = local("rows_m", [MH, 5, T], F32, 88064)
        e_ms = local("e_ms", [P, MH, TS], F32, 99584)
        a_s = local("a_s", [P, MH, TS], F32, 100608)
        w_s = local("w_s", [TS, MH, TS], F32, 101632)
        g_col = local("g_col", [P, TB, MH], F32, 102656)
        wl_p = local("wl_p", [P, QB, MH], F32, 102752)
        wl_s = local("wl_s", [TS, MH, NBATCH], F32, 102816)
        n_t = local("n_t", [P, MH, NBATCH], F32, 102944)
        m0 = local("m0", [MH, NBATCH], F32, 103072)
        a_last = local("a_last", [MH, NBATCH], F32, 103104)
        a_last_t = local("a_last_t", [NBATCH, MH], F32, 103136)
        c_st += [rstd[:, 0:CW].rearrange("p (h e) -> p h e", h=MH)]
        c_st += [local(f"c_st{b}", [P, MH, MD], F32, 75776 + (b - EARLY) * 4 * CW) for b in range(EARLY, NBATCH)]
        c_t = local("c_t", [P, MH, MD], F32, 79872)
        k_own = local("k_own", [TS, 2, MH, MD], F32, 81920)
        h_t = local("h_t", [P, MH, T], F32, 4 * YB)
        h_sq = local("h_sq", [P, MH, T], F32, 46080)
        ym_hi, ym_lo = (local(n, [P, WT, T], F32R, (2 + i) * YB) for i, n in enumerate(("ym_hi", "ym_lo")))

        UW = 2 + TP + NBATCH * (2 + NEW)
        yc_hi, yc_lo = (local(n, [P, WT, T], F32R, (4 + i) * YB) for i, n in enumerate(("yc_hi", "yc_lo")))
        c_buf = local("c_buf", [P, 3 * WT, T], F32, 6 * YB)
        u_c = local("u_c", [P, WT, UW], F32, 82944)
        c_last = raw[:, 0, FH - 1, 0:18 * WT].rearrange("p (f c) -> p f c", f=WT)
        c_rows = local("c_rows", [16, CW], F32, 92800)
        c_out = rstd[0:18, 0:CW]

        mg_hi, mg_lo = (local(n, [P, KD, T], F32R, 6 * YB + i * 2 * YB) for i, n in enumerate(("mg_hi", "mg_lo")))
        gate = local("gate", [P, 3, T], F32, 92160)
        mix = local("mix", [P, 2, T], F32, 99072)

        hid_hi, hid_lo = (local(n, [P, FH, T], F32R, 40960 + i * 25344) for i, n in enumerate(("hid_hi", "hid_lo")))
        u_f = local("u_f", [P, UW], F32, 91648)
        y_f = local("y_f", [P, T], F32, 94048)
        s_f = local("s_f", [P, T], F32, 96352)
        f_last = local("f_last", [P, FT, 18], F32, 98656)
        f_cols = local("f_cols", [P, FT, 16], F32, 100256)
        f_rows = local("f_rows", [16, FF], F32, 0)
        f_out = local("f_out", [18, FF], F32, 11264)
        p_rows = local("p_rows", [P, TB, PLE], F32, 22528)
        p_hi, p_lo = (local(n, [P, PT, T], F32R, i * 4608) for i, n in enumerate(("p_hi", "p_lo")))

        gate_p = local("gate_p", [P, 2, T], F32, 55296)
        emb = local("emb", [P, T], F32, 59904)
        y_t = local("y_t", [P, KD, T], F32, 62208)
        y_rows = local("y_rows", [P, 2, D], F32, 80640)

        psum = ctx.enter_context(nc.psum_tensor("psum", [P, 8, 512], F32))

        S_BANKS = (0, 1, 4, 5)

        def own_heads(r, hh):
            x = psum[r, 6:8, :].rearrange("p a c -> p (a c)")[:, 0:WT * 144].rearrange("p (f x) -> p f x", x=144)
            return x[:, :, 8 * hh:8 * hh + P].rearrange("p f (b y) -> p f b y", b=2)[:, :, :, 0:NEW]

        def acc(slot):
            return psum[:, 2 * slot:2 * slot + 2, 0:HALF]

        cst_in, rows_in, ws_in = sem("cst_in"), sem("rows_in"), sem("ws_in")
        x_in = sem("x_in")
        bias_in, pages_in, gzero = sem("bias_in"), sem("pages_in"), sem("gzero")
        w_landed = [sem("w_landed0"), sem("w_landed1")]
        hi_ready, lo_ready, gemm_done = sem("hi_ready"), sem("lo_ready"), sem("gemm_done")
        psum_free = [sem("psum_free0"), sem("psum_free1")]
        dve_step, act_step, pool_step = sem("dve_step"), sem("act_step"), sem("pool_step")
        consts_ready, ws_zero, cols_done, cols_ready = sem("consts_ready"), sem("ws_zero"), sem("cols_done"), sem("cols_ready")
        xt_done, x_ready, sq_ready, sum_done, std_ready, hn_ready, ahi_ready, a_ready = (
            sem(n) for n in ("xt_done", "x_ready", "sq_ready", "sum_done", "std_ready", "hn_ready", "ahi_ready", "a_ready"))
        wshi_ready, ws_ready, gates_done = sem("wshi_ready"), sem("ws_ready"), sem("gates_done")
        gln_ready, cum_ready, small_done, small_ready = (
            sem(n) for n in ("gln_ready", "cum_ready", "small_done", "small_ready"))
        tok_done, tok_copied, q_scaled = sem("tok_done"), sem("tok_copied"), sem("q_scaled")
        out_k = [sem("out_k0"), sem("out_k1")]
        outs = sem("outs")
        scores_done, nmax_ready, exp_done, rinv_ready, probs_ready = (
            sem(n) for n in ("scores_done", "nmax_ready", "exp_done", "rinv_ready", "probs_ready"))
        pt_done, pt_copied, pv_done, o_hi, o_lo = (sem(n) for n in ("pt_done", "pt_copied", "pv_done", "o_hi", "o_lo"))
        qblk_ready, lpast_in = sem("qblk_ready"), sem("lpast_in")
        kp_in, vp_in = [sem("kp_in0"), sem("kp_in1")], [sem("vp_in0"), sem("vp_in1")]
        ktr_done, ktr_copied, lrep_ready, cums_done, cums_ready, s_done, s_free, snmax, sexp, sprobs, spt_done, spt_copied, spv_done, so_hi, so_lo = (
            sem(n) for n in ("ktr_done", "ktr_copied", "lrep_ready", "cums_done", "cums_ready", "s_done", "s_free", "snmax", "sexp", "sprobs", "spt_done", "spt_copied", "spv_done", "so_hi", "so_lo"))
        rows_ready, m0_in, mrow_ready, mb_done, mb_copied, mside_done, mside_copied, kscaled, mtok_done, mtok_copied, wl_sub, wl_ready = (
            sem(n) for n in ("rows_ready", "m0_in", "mrow_ready", "mb_done", "mb_copied", "mside_done", "mside_copied", "kscaled", "mtok_done", "mtok_copied", "wl_sub", "wl_ready"))
        em_done, em_ready, mqk_done, mdec_ready, mexp_done, mw_ready, mpv_done, h_ready = (
            sem(n) for n in ("em_done", "em_ready", "mqk_done", "mdec_ready", "mexp_done", "mw_ready", "mpv_done", "h_ready"))
        kw_ready, cp_done, cp_copied, n_in, nt_done, nt_copied, qn_ready, sqk_done, sdec_ready, sdexp_done, sw_ready, ssum_done = (
            sem(n) for n in ("kw_ready", "cp_done", "cp_copied", "n_in", "nt_done", "nt_copied", "qn_ready", "sqk_done", "sdec_ready", "sdexp_done", "sw_ready", "ssum_done"))
        c_in = [sem(f"c_in{s}") for s in range(2)]
        c_store = [sem(f"c_store{s}") for s in range(2)]
        so_rows, sot_done = sem("so_rows"), sem("sot_done")
        ctr_done, ctr_copied, inter_done, kown_ready, cadd_done, cnew_ready, n_new_ready = (
            sem(n) for n in ("ctr_done", "ctr_copied", "inter_done", "kown_ready", "cadd_done", "cnew_ready", "n_new_ready"))
        hsq_ready, hmean_done, hstd_ready, ym_full, ymhi_ready, ym_ready = (
            sem(n) for n in ("hsq_ready", "hmean_done", "hstd_ready", "ym_full", "ymhi_ready", "ym_ready"))
        conv_rows_in, ctr2_done, yc_full, ychi_ready, yc_ready, clast_done, clast_copied = (
            sem(n) for n in ("conv_rows_in", "ctr2_done", "yc_full", "ychi_ready", "yc_ready", "clast_done", "clast_copied"))
        mix_step, f_rows_in, p_rows_in, fcols_done, fcols_ready, p_done, phi_ready, p_ready = (
            sem(n) for n in ("mix_step", "f_rows_in", "p_rows_in", "fcols_done", "fcols_ready", "p_done", "phi_ready", "p_ready"))
        fconv_done, fstep, fsig_done, hid_ready, flast_done, flast_copied, xple_ready, yt_ready, ytr_done = (
            sem(n) for n in ("fconv_done", "fstep", "fsig_done", "hid_ready", "flast_done", "flast_copied", "xple_ready", "yt_ready", "ytr_done"))
        ytr_copied = [sem("ytr_copied0"), sem("ytr_copied1")]
        conv_out = sem("conv_out")
        y_store = [sem("y_store0"), sem("y_store1")]

        w_in = d["w_in"][0].rearrange("(k p) n -> p k n", p=P)

        ctx.enter_context(nc.allow_non_contiguous_dma(reason="a few numbers for each head"))
        block = ctx.enter_context(nc.Block())
        @block.sync
        def _(sp):
            for b in range(QB):
                sp.dma_start(xs[:, b, :], d["x_prompt"][0, b * P:(b + 1) * P, :]).then_inc(x_in, 16)
            sp.dma_start(xs[0:TS, QB, :], d["x_sample"].rearrange("b t n -> (b t) n")).then_inc(x_in, 16)

            def load(first, start, pairs, sources, kts):
                def one(i):
                    for slot in (0, 1):
                        if not (first == 0 and isinstance(i, int) and i == 0):
                            sp.wait_ge(lo_ready, (i + first) * 2 + (slot - 1))
                        sp.dma_start(raw[:, slot, 0:kts[slot], :], sources[slot](i)).then_inc(w_landed[slot], 16)

                if pairs - start == 1:
                    one(start)
                else:
                    with sp.Fori(start, pairs) as i:
                        one(i)

            def two(mat, col):
                return [lambda i, s=s: mat[:, :, bass.ds(i * 256 + (col + s * P), P)] for s in (0, 1)]

            load(PR_A, 0, 1, two(w_in, COL_A), (KD, KD))
            load(PR_A, 1, 6, two(w_in, COL_A), (KD, KD))
            load(PR_M, 0, 1, two(w_in, COL_M), (KD, KD))

            sp.wait_ge(small_ready, 1)
            for b in range(TB):
                n = 2 * b + 1
                rows = TS if b == QB else P
                k_rows = d["k_s"].rearrange("b t l h e -> (b t) (l h e)") if b == QB else d["k_p"][0, b * P:(b + 1) * P].rearrange("t l h e -> t (l h e)")
                v_rows = d["v_s"].rearrange("b t l h e -> (b t) (l h e)") if b == QB else d["v_p"][0, b * P:(b + 1) * P].rearrange("t l h e -> t (l h e)")
                lf_rows = d["logf_s"].rearrange("b t l h -> (b t) (l h)") if b == QB else d["logf_p"][0, b * P:(b + 1) * P].rearrange("t l h -> t (l h)")
                sp.wait_ge(tok_copied, n)
                sp.dma_start(v_rows, v_tok[0:rows, b, :]).then_inc(outs, 16)
                sp.wait_ge(tok_copied, n + 1)
                sp.dma_start(k_rows, kstage[0:rows, b % 2, :]).then_inc(out_k[b % 2], 16)
                sp.dma_start(lf_rows, lf_tok[0:rows, b, :]).then_inc(outs, 16)

            sp.wait_ge(pages_in, 16)
            page = [[sp.value_load(pages[0:1, b * PAGES + j:b * PAGES + j + 1], min_val=0, max_val=NPHYS - 1) for j in range(PAGES)]
                    for b in range(NBATCH)]
            for b in range(NBATCH):
                for j in range(PAGES):
                    sp.dma_start(lpast[:, b, j, :], d["cache_logf"][bass.ds(page[b][j], 1), :, 0, :].rearrange("a s h -> (a s) h")).then_inc(lpast_in, 16)

            def page_rows(name, ring, landed, b):
                for j in range(PAGES):
                    sp.dma_start(ring[:, j, :], d[name][bass.ds(page[b][j], 1), :, 0].rearrange("a s h e -> (a s) (h e)")).then_inc(landed, 16)

            page_rows("cache_k", kp[0], kp_in[0], 0)
            sp.wait_ge(pv_done, 4 * AH)
            sp.wait_ge(qblk_ready, AH + 1)
            page_rows("cache_k", kp[1], kp_in[1], 1)
            for kind, p in (("v", 0), ("k", 1), ("k", 2), ("v", 1), ("k", 3), ("v", 2), ("v", 3)):
                for b2 in range(2):
                    if kind == "k":
                        sp.wait_ge(ktr_done, 4 * (2 * p + b2 - 1))
                        page_rows("cache_k", kp[b2], kp_in[b2], 2 * p + b2)
                    else:
                        if p:
                            sp.wait_ge(spv_done, p)
                        page_rows("cache_v", vp[:, b2], vp_in[b2], 2 * p + b2)
            load(PR_M, 1, 6, two(w_in, COL_M), (KD, KD))
            load(PR_O, 0, 1, two(w_in, COL_MO), (KD, KD))
            sp.wait_ge(gemm_done, 2 * (PR_M + 6))
            for b in range(EARLY):
                sp.dma_start(c_st[b][:], d["state_mlstm_C"][b, 0].rearrange("h v k -> v h k")).then_inc(c_in[0], 16)
            sp.wait_ge(rows_ready, 1)
            sp.dma_start(n0[:], d["state_mlstm_n"].rearrange("b l h e -> b (l h e)")).then_inc(n_in, 16)
            sp.wait_ge(mrow_ready, 1)
            sp.dma_start(d["m_p"].rearrange("a l h -> h (a l)"), rows_m[:, 0, TP - 1:TP]).then_inc(outs, 16)
            sp.dma_start(d["m_s"].rearrange("b l h -> h (l b)"), rows_m[:, 0, TP + NEW - 1:T:NEW]).then_inc(outs, 16)
            sp.wait_ge(cp_copied, 2)
            sp.dma_start(d["C_p"][0, 0].rearrange("h v k -> v h k"), m_all[:, :, 0:MD]).then_inc(outs, 16)
            sp.dma_start(d["n_p"][0, 0].rearrange("h k -> (h k)").rearrange("(o n) -> o n", o=1), rows_m[0:1, 2, 0:CW]).then_inc(outs, 16)
            sp.wait_ge(h_ready, MH)
            for b in range(EARLY, NBATCH):
                sp.dma_start(c_st[b][:], d["state_mlstm_C"][b, 0].rearrange("h v k -> v h k")).then_inc(c_in[1], 16)
            for b in range(NBATCH):
                sp.wait_ge(cnew_ready, b + 1)
                sp.dma_start(d["C_s"][b, 0].rearrange("h v k -> v h k"), c_st[b][:]).then_inc(c_store[b >= IN_W], 16)
            sp.wait_ge(n_new_ready, 1)
            sp.dma_start(d["n_s"].rearrange("b l h e -> b (l h e)"), n0[:]).then_inc(outs, 16)
            load(PR_O, 1, 2, two(w_in, COL_MO), (KD, KD))
            load(PR_C, 0, 1, two(w_in, COL_C), (KD, KD))
            load(PR_C, 1, 3, two(w_in, COL_C), (KD, KD))
            sp.wait_ge(ym_ready, 1)
            sp.dma_start(c_rows[:], d["state_conv"].rearrange("b l r c -> (b l r) c")).then_inc(conv_rows_in, 16)
            load(PR_C, 3, 6, two(w_in, COL_C), (KD, KD))

            w_out = [d[name][0].rearrange("(k p) n -> p k n", p=P) for name in ("w_oa", "w_om", "w_oc")]
            for i in range(KD):
                for b in range(3):
                    n = 2 * (PR_MIX + 3 * i + b)
                    sp.wait_ge(lo_ready, n - 1)
                    sp.dma_start(raw[:, 0, 0:KD, :], w_in[:, :, COL_G + b * D + i * P:COL_G + b * D + (i + 1) * P]).then_inc(w_landed[0], 16)
                    sp.wait_ge(lo_ready, n)
                    sp.dma_start(raw[:, 1, 0:WT, :], w_out[b][:, :, i * P:(i + 1) * P]).then_inc(w_landed[1], 16)

            def kt_view(mat):
                return mat.rearrange("(k p) n -> p k n", p=P)

            load(PR_WO, 0, 4, two(kt_view(d["w_o"][0]), 0), (KD, KD))
            sp.wait_ge(clast_copied, 1)
            sp.dma_start(d["conv_p"][0, 0], c_out[0:2, :]).then_inc(conv_out, 16)
            sp.dma_start(d["conv_s"].rearrange("b l r c -> (b l r) c"), c_out[2:18, :]).then_inc(conv_out, 16)
            up = kt_view(d["w_up"][0])
            ups = [[lambda i, f=f, s=s: up[:, :, bass.ds(i * P + (f * FH * P + s * FF), P)] for s in (0, 1)] for f in range(2)]
            load(PR_FFN, 0, 1, ups[0], (KD, KD))
            sp.wait_ge(mix_step, 4 * KD)
            sp.dma_start(f_rows[:], d["state_ffn_conv"].rearrange("b l r c -> (b l r) c")).then_inc(f_rows_in, 16)
            for b in range(QB):
                sp.dma_start(p_rows[:, b, :], d["p_prompt"][0, 0, b * P:(b + 1) * P, :]).then_inc(p_rows_in, 16)
            sp.dma_start(p_rows[0:TS, QB, :], d["p_sample"][0].rearrange("b t n -> (b t) n")).then_inc(p_rows_in, 16)
            for f in range(2):
                load(PR_FFN + f * PR_PART, 1 - f, FH, ups[f], (KD, KD))
                down = d["w_down"][0][f * FH * P:(f + 1) * FH * P, :].rearrange("(k p) n -> p k n", p=P)
                load(PR_FFN + f * PR_PART + FH, 0, 4, two(down, 0), (FH, FH))
            tail = [kt_view(d["w_ple_gate"][0]), kt_view(d["w_ple"][0])]
            load(PR_PLE, 0, 8, [lambda i, s=s: tail[s][:, :, bass.ds(i * P, P)] for s in (0, 1)], (KD, PT))
            sp.wait_ge(flast_copied, 6)
            sp.dma_start(d["ffn_p"][0, 0], f_out[0:2, :]).then_inc(outs, 16)
            sp.dma_start(d["ffn_s"].rearrange("b l r c -> (b l r) c"), f_out[2:18, :]).then_inc(outs, 16)
            for b in range(TB):
                sp.wait_ge(ytr_copied[0], b + 1)
                sp.wait_ge(ytr_copied[1], b + 1)
                dst = d["y_sample"].rearrange("b t n -> (b t) n") if b == QB else d["y_prompt"][0, b * P:(b + 1) * P, :]
                sp.dma_start(dst, y_rows[0:TS if b == QB else P, b % 2, :]).then_inc(y_store[b % 2], 16)
            sp.wait_ge(y_store[0], 16 * 3)
            sp.wait_ge(y_store[1], 16 * 2)
            sp.wait_ge(outs, 16 * (2 * TB + 7))
            sp.wait_ge(conv_out, 32)
            sp.wait_ge(c_store[0], 16 * IN_W)
            sp.wait_ge(c_store[1], 16 * (NBATCH - IN_W))
            sp.wait_ge(out_k[0], 16 * 3)
            sp.wait_ge(out_k[1], 16 * 2)

        @block.gpsimd
        def _(pool):
            pool.memset(ws[:], 0.0).then_inc(ws_zero, 1)
            pool.memset(ones[:], 1.0).then_inc(consts_ready, 1)
            pool.memset(mean_d[:], 1.0 / D).then_inc(consts_ready, 1)
            pool.memset(mean_h[:], 1.0 / MD).then_inc(consts_ready, 1)
            pool.memset(eps_c[:], EPS).then_inc(consts_ready, 1)
            pool.wait_ge(wshi_ready, 1)
            pool.tensor_tensor(ws_lo[:], ws[:], ws_hi[:].bitcast(F32), ALU.subtract).then_inc(ws_ready, 1)

            def split_lo(first, start, pairs, kts):
                def one(i):
                    for slot in (0, 1):
                        pool.wait_ge(hi_ready, (i + first) * 2 + (slot + 1))
                        pool.tensor_tensor(w_lo[:, slot, 0:kts[slot], :], raw[:, slot, 0:kts[slot], :],
                                           w_hi[:, slot, 0:kts[slot], :].bitcast(F32), ALU.subtract).then_inc(lo_ready, 1)

                if pairs - start == 1:
                    one(start)
                else:
                    with pool.Fori(start, pairs) as i:
                        one(i)

            def norm_lo(number):
                for k in range(KD):
                    pool.wait_ge(ahi_ready, KD * number + k + 1)
                    pool.tensor_tensor(a_lo[:, k, :], hn[:, k % 2, :], a_hi[:, k, :].bitcast(F32), ALU.subtract).then_inc(a_ready, 1)

            split_lo(PR_A, 0, 1, (KD, KD))
            norm_lo(0)
            split_lo(PR_A, 1, 6, (KD, KD))
            split_lo(PR_M, 0, 1, (KD, KD))

            pool.wait_ge(q_scaled, 1)
            pool.memset(q_blk[:], 0.0).then_inc(pool_step, 1)
            pool.wait_ge(pool_step, 1)
            for h in range(AH):
                r = slice(64 * (h % 2), 64 * (h % 2) + 64)
                pool.tensor_copy(q_blk[r, h // 2, :, 8 * h:8 * h + 8],
                                 q_a[r, h // 2, TP:T].rearrange("p (b q) -> p b q", b=NBATCH)).then_inc(qblk_ready, 1)
                pool.wait_ge(qblk_ready, h + 1)
            pool.tensor_copy(k_new[:], q_a[:, WT:2 * WT, TP:T]).then_inc(qblk_ready, 1)
            pool.wait_ge(qblk_ready, AH + 1)
            for n in range(4 * AH):
                b = QB - 1 - n % 4
                o = P * (b * (b + 1) // 2)
                row = probs[:, (n // 4) % 2, o:o + P * (b + 1)]
                pool.wait_ge(rinv_ready, n + 1)
                pool.tensor_scalar(row, row, rinv[:, n % 4:n % 4 + 1], None, ALU.mult).then_inc(probs_ready, 1)
            pool.wait_ge(pv_done, 4 * AH)
            for b2 in range(2):
                pool.tensor_copy(lnew[:, 64 * b2:64 * b2 + 64].rearrange("p (h q) -> p h q", h=AH),
                                 lf_tok[0:TS, QB, :].unsqueeze(2).broadcast_to([TS, AH, NEW])).then_inc(lrep_ready, 1)
                pool.wait_ge(lrep_ready, b2 + 1)
            pool.wait_ge(lpast_in, 16 * NBATCH * PAGES)
            for p in range(NBATCH // 2):
                if p:
                    pool.wait_ge(cums_done, p)
                for b2 in range(2):
                    pool.tensor_copy(lrep[:].rearrange("p j (b h q) -> p j b h q", b=2, h=AH)[:, :, b2],
                                     lpast[:, 2 * p + b2].unsqueeze(3).broadcast_to([P, PAGES, AH, NEW])).then_inc(lrep_ready, 1)
                    pool.wait_ge(lrep_ready, 2 * p + b2 + 3)
            split_lo(PR_M, 1, 6, (KD, KD))
            pool.wait_ge(wl_ready, 2)
            pool.wait_ge(mtok_copied, 2 * TB)
            for b in range(QB):
                kb = k_tok[:, b, :].rearrange("p (h e) -> p h e", h=MH)
                pool.tensor_tensor(kb, kb, wl_p[:, b, :].unsqueeze(2).broadcast_to([P, MH, MD]), ALU.mult).then_inc(kw_ready, 1)
            pool.wait_ge(h_ready, MH)
            for b in range(NBATCH):
                if b >= 2:
                    pool.wait_ge(cadd_done, b - 1)
                pool.tensor_tensor(k_own[:, b % 2], k_tok[0:TS, QB, :].rearrange("p (h e) -> p h e", h=MH),
                                   wl_s[:, :, b:b + 1].broadcast_to([TS, MH, MD]), ALU.mult).then_inc(kown_ready, 1)
            split_lo(PR_O, 0, 2, (KD, KD))
            split_lo(PR_C, 0, 6, (KD, KD))
            with pool.Fori(0, KD) as i:
                for b in range(3):
                    for slot, kt in ((0, KD), (1, WT)):
                        pool.wait_ge(hi_ready, i * 6 + ((PR_MIX + b) * 2 + slot + 1))
                        pool.tensor_tensor(w_lo[:, slot, 0:kt, :], raw[:, slot, 0:kt, :],
                                           w_hi[:, slot, 0:kt, :].bitcast(F32), ALU.subtract).then_inc(lo_ready, 1)
            split_lo(PR_WO, 0, 4, (KD, KD))
            for f in range(2):
                if f == 0:
                    split_lo(PR_FFN, 0, 1, (KD, KD))
                    norm_lo(1)
                split_lo(PR_FFN + f * PR_PART, 1 - f, FH, (KD, KD))
                split_lo(PR_FFN + f * PR_PART + FH, 0, 4, (FH, FH))
            split_lo(PR_PLE, 0, 1, (KD, PT))
            norm_lo(2)
            split_lo(PR_PLE, 1, 8, (KD, PT))

        @block.scalar
        def _(act):
            act.dma_start(cst[:], d["cst"]).then_inc(cst_in, 16)
            brows = d["b_in"][0]
            for r0, c0, n in ((BA, COL_A, 12), (BM, COL_M, 12), (BO, COL_MO, 4), (BC, COL_C, 12), (BG, COL_G, 24)):
                act.dma_start(rows1[r0:r0 + n, :], brows[c0:c0 + n * P].rearrange("(t p) -> t p", p=P)).then_inc(rows_in, 16)
            for r0, name in ((GMIX, "g_mix"), (GFFN, "g_ffn"), (GPLE, "g_ple"), (GMH, "g_mhead")):
                n = KD if r0 != GMH else WT
                act.dma_start(rows1[r0:r0 + n, :], d[name][0].rearrange("(t p) -> t p", p=P)).then_inc(rows_in, 16)
            act.dma_start(rows1[GFIN:GFIN + KD, :], d["g_final"].rearrange("(t p) -> t p", p=P)).then_inc(rows_in, 16)
            act.dma_start(rows1[WSC:WSC + 3 * WT, :], d["w_sconv"][0].rearrange("j (t p) -> (j t) p", p=P)).then_inc(rows_in, 16)
            act.dma_start(rows2[0:3 * FT, :], d["w_fconv"][0].rearrange("j (t p) -> (j t) p", p=P)).then_inc(rows_in, 16)
            act.dma_start(rows2[3 * FT:4 * FT, :], d["b_fconv"][0].rearrange("(t p) -> t p", p=P)).then_inc(rows_in, 16)
            act.wait_ge(ws_zero, 1)
            for r0, c0, n in ((0, COL_AF, 8), (32, COL_MI, 4), (64, COL_MF, 4)):
                act.dma_start(ws[:, :, r0:r0 + n], w_in[:, :, c0:c0 + n]).then_inc(ws_in, 16)
            act.wait_ge(gzero, 1)
            for r0, c0, n in ((0, COL_AF, 8), (32, COL_MI, 4), (64, COL_MF, 4)):
                act.dma_start(gbias[r0:r0 + n, :], brows[c0:c0 + n].rearrange("(p o) -> p o", o=1)).then_inc(bias_in, 16)
            act.dma_start(pages[0:1, :], d["page_table"].rearrange("b j -> (b j)").rearrange("(o n) -> o n", o=1)).then_inc(pages_in, 16)

            for k in range(KD):
                act.wait_ge(xt_done, k + 1)
                act.activation(xT[:, k, 0:TP], psum[:, 2 * (k % 2), :], ACT.Copy)
                act.activation(xT[:, k, TP:T], psum[:, 2 * (k % 2) + 1, 0:TS], ACT.Copy).then_inc(x_ready, 1)
            act.wait_ge(ws_in, 48)
            act.activation(ws_hi[:], ws[:], ACT.Copy).then_inc(wshi_ready, 1)

            def norm_split(number):
                act.wait_ge(sum_done, KD + number)
                act.activation(rstd[:].rearrange("p (a t) -> p a t", a=2), psum[:, 6:8, 0:HALF], ACT.Sqrt, bias=eps_c[:]).then_inc(std_ready, 1)
                for k in range(KD):
                    act.wait_ge(hn_ready, KD * number + k + 1)
                    act.activation(a_hi[:, k, :], hn[:, k % 2, :], ACT.Copy).then_inc(ahi_ready, 1)

            def hi(first, i, slot, kt):
                act.wait_ge(w_landed[slot], (i + (first + 1)) * 16)
                if not (isinstance(i, int) and first + i == 0):
                    act.wait_ge(gemm_done, (i + first) * 2 + (slot - 1))
                act.activation(w_hi[:, slot, 0:kt, :], raw[:, slot, 0:kt, :], ACT.Copy).then_inc(hi_ready, 1)

            def biased(first, pairs, kt_next, dst, col, func=ACT.Identity):
                def one(i, kt):
                    for slot in (0, 1):
                        if kt:
                            hi(first, i + 1, slot, kt[slot])
                        act.wait_ge(gemm_done, (i + first) * 2 + (slot + 1))
                        act.activation(dst[:, bass.ds(i * 2 + slot, 1), :].rearrange("p o (a t) -> p (o a) t", a=2), acc(slot), func,
                                       bias=cols1[:, bass.ds(i * 2 + (col + slot), 1)]).then_inc(psum_free[slot], 1)

                if pairs > 1:
                    with act.Fori(0, pairs - 1) as i:
                        one(i, (KD, KD))
                one(pairs - 1, kt_next)

            hi(PR_A, 0, 0, KD)
            hi(PR_A, 0, 1, KD)
            act.wait_ge(consts_ready, 4)
            norm_split(0)
            biased(PR_A, 2, (KD, KD), q_a, BA)
            act.wait_ge(cols_ready, 2)
            act.wait_ge(gates_done, 1)
            act.wait_ge(bias_in, 48)
            act.activation(gs[:].rearrange("p (a t) -> p a t", a=2), psum[0:96, 4:6, 0:HALF], ACT.Identity, bias=gbias[0:96]).then_inc(act_step, 1)
            biased(PR_A + 2, 1, (KD, KD), q_a[:, 4:6, :], BA + 4)
            act.wait_ge(act_step, 1)
            act.activation(ge[:], gs[:], ACT.Abs).then_inc(act_step, 1)
            biased(PR_A + 3, 1, (KD, KD), q_a[:, 6:8, :], BA + 6)
            act.wait_ge(act_step, 2)
            act.activation(ge[:], ge[:], ACT.Exp, scale=-1.0).then_inc(act_step, 1)
            biased(PR_A + 4, 1, (KD, KD), q_a[:, 8:10, :], BA + 8)
            act.wait_ge(act_step, 3)
            act.activation(ge[:], ge[:], ACT.Ln, bias=1.0).then_inc(gln_ready, 1)
            biased(PR_A + 5, 1, (KD, KD), q_a[:, 10:12, :], BA + 10)
            act.wait_ge(small_done, 1)
            act.activation(lf_tok[:, 0:QB, :], psum[:, 4, 0:QB * AH].rearrange("p (b h) -> p b h", b=QB), ACT.Copy)
            act.activation(lf_tok[0:TS, QB, :], psum[0:TS, 4, QB * AH:TB * AH], ACT.Copy).then_inc(small_ready, 1)
            for b in range(TB):
                rows = TS if b == QB else P
                for which in range(2):
                    n = 2 * b + which
                    act.wait_ge(tok_done, n + 1)
                    if which and b >= 2:
                        act.wait_ge(out_k[b % 2], 16 * (b // 2))
                    act.activation(kstage[0:rows, b % 2, :] if which else v_tok[0:rows, b, :], psum[0:rows, 4 + n % 4, :], ACT.Copy).then_inc(tok_copied, 1)

            act.wait_ge(out_k[0], 16 * 3)
            act.wait_ge(out_k[1], 16 * 2)
            for h in range(AH + 1):
                for i in range(QB):
                    if h < AH:
                        n = 4 * h + i
                        act.wait_ge(nmax_ready, n + 1)
                        if h >= 2 and i == 0:
                            act.wait_ge(pt_done, 4 * (h - 1))
                        if n >= 4:
                            act.wait_ge(rinv_ready, n - 3)
                        b = QB - 1 - i
                        o = P * (b * (b + 1) // 2)
                        act.activation(probs[:, h % 2, o:o + P * (b + 1)], psum[:, S_BANKS[i], 0:P * (b + 1)], ACT.Exp,
                                       bias=nmax[:, i:i + 1], accum_out=rsum[:, i:i + 1]).then_inc(exp_done, 1)
                    if h >= 1:
                        m = 4 * (h - 1) + i
                        act.wait_ge(pt_done, m + 1)
                        if m >= 2:
                            act.wait_ge(pv_done, m - 1)
                        act.activation(pt[:, m % 2, 0:TP - P * i], psum[:, (6, 2)[m % 2], 0:TP - P * i], ACT.Copy).then_inc(pt_copied, 1)
                if h >= 1 and (h - 1) % 2:
                    f = (h - 1) // 2
                    act.wait_ge(pv_done, 4 * h)
                    act.activation(ya_hi[:, f, 0:TP], psum[:, (7, 3)[f % 2], :], ACT.Copy).then_inc(o_hi, 1)

            for p in range(NBATCH // 2 + 1):
                if p < NBATCH // 2:
                    if p == 0:
                        act.wait_ge(pv_done, 4 * AH)
                        act.wait_ge(qblk_ready, AH + 1)
                    for b2 in range(2):
                        for f in range(WT):
                            m = 4 * (2 * p + b2) + f
                            act.wait_ge(ktr_done, m + 1)
                            if m >= 4:
                                act.wait_ge(s_done, (2 * p + b2 - 1) * 4 + f + 1)
                            act.activation(kt_s[:, f, :], psum[:, 4 + m % 2, :], ACT.Copy).then_inc(ktr_copied, 1)
                    act.wait_ge(cums_done, p + 1)
                    if p:
                        act.wait_ge(s_free, p)
                    act.activation(cums[:, 0:TP], psum[:, 0, :], ACT.Copy)
                    act.activation(cums[:, TP:T], psum[:, 1, 0:TS], ACT.Copy).then_inc(cums_ready, 1)
                if p:
                    y = p - 1
                    act.wait_ge(snmax, y + 1)
                    act.activation(ls[:], ls[:], ACT.Exp, bias=nmax[:, 0:1], accum_out=rsum[:, 0:1]).then_inc(sexp, 1)
                    act.wait_ge(spt_done, y + 1)
                    act.activation(pts[:, 0:QB, :], psum[:, 6, :].rearrange("p (j r) -> p j r", j=QB), ACT.Copy)
                    act.activation(pts[0:TS, QB, :], psum[0:TS, 0, 0:P], ACT.Copy).then_inc(spt_copied, 1)
                    act.wait_ge(spv_done, y + 1)
                    act.activation(o_tok[:], psum[:, 7, :], ACT.Copy).then_inc(so_rows, 1)
                    act.wait_ge(sot_done, y + 1)
                    for hh in range(2):
                        r = slice(64 * hh, 64 * hh + 64)
                        act.activation(ya_hi[r, :, TP + 16 * y:TP + 16 * y + 16].rearrange("p f (b q) -> p f b q", b=2),
                                       own_heads(r, hh), ACT.Copy).then_inc(so_hi, 1)
            act.dma_start(m0[:], d["state_mlstm_m"].rearrange("b l h -> h (l b)")).then_inc(m0_in, 16)
            act.wait_ge(outs, 16 * 2 * TB)
            biased(PR_M, 6, None, q_m, BM)
            for h in range(MH):
                act.wait_ge(mb_done, h + 1)
                act.activation(m_all[:, h, 0:TP], psum[:, 4 + h % 2, :], ACT.Copy).then_inc(mb_copied, 1)
            act.wait_ge(mside_done, 1)
            act.activation(m_all[:, :, TP:T], psum[:, 6, 0:MH * TS].rearrange("p (h t) -> p h t", h=MH), ACT.Copy)
            act.activation(e_ms[:], psum[:, 6, MH * TS:2 * MH * TS].rearrange("p (h t) -> p h t", h=MH), ACT.Exp, scale=-1.0)
            act.activation(a_s[:], psum[:, 7, 0:MH * TS].rearrange("p (h t) -> p h t", h=MH), ACT.Exp)
            act.activation(a_last[:], rows_m[:, 4, NEW - 1:TS:NEW], ACT.Exp)
            act.activation(g_col[:, 0:QB, :], psum[:, 7, 256:256 + QB * MH].rearrange("p (b h) -> p b h", b=QB), ACT.Copy)
            act.activation(g_col[0:TS, QB, :], psum[0:TS, 7, 256 + QB * MH:256 + TB * MH], ACT.Copy).then_inc(mside_copied, 1)
            for b in range(TB):
                rows = TS if b == QB else P
                for which in range(2):
                    n = 2 * b + which
                    act.wait_ge(mtok_done, n + 1)
                    act.activation((k_tok if which else vm_tok)[0:rows, b, :], psum[0:rows, n % 4, :], ACT.Copy).then_inc(mtok_copied, 1)
            act.wait_ge(wl_sub, 2)
            act.activation(wl_p[:], wl_p[:], ACT.Exp).then_inc(wl_ready, 1)
            act.activation(wl_s[:], wl_s[:], ACT.Exp).then_inc(wl_ready, 1)

            for n in range(4 * MH):
                h = n // 4
                if n % 4 == 0:
                    act.wait_ge(em_done, h + 1)
                    if h >= 2:
                        act.wait_ge(h_ready, h - 1)
                    act.activation(e_m[:, h % 2, :], psum[:, 2, :], ACT.Exp, scale=-1.0).then_inc(em_ready, 1)
                act.wait_ge(mdec_ready, n + 1)
                w = TP - P * (n % 4)
                act.activation(decay[:, n % 3, 0:w], decay[:, n % 3, 0:w], ACT.Exp, scale=-1.0).then_inc(mexp_done, 1)
            act.wait_ge(cp_done, 1)
            act.activation(m_all[:, :, 0:MD], psum[:, 3, :].rearrange("p (h e) -> p h e", h=MH), ACT.Copy).then_inc(cp_copied, 1)
            act.wait_ge(cp_done, 2)
            act.activation(rows_m[0:1, 2, 0:CW], psum[0:1, 4, :], ACT.Copy).then_inc(cp_copied, 1)
            act.wait_ge(nt_done, 1)
            act.activation(n_t[:], psum[:, 5, 0:MH * NBATCH].rearrange("p (h b) -> p h b", h=MH), ACT.Copy)
            act.activation(a_last_t[:], psum[0:NBATCH, 5, 64:64 + MH], ACT.Copy).then_inc(nt_copied, 1)
            act.wait_ge(sdec_ready, 1)
            act.activation(w_s[:], w_s[:], ACT.Exp, scale=-1.0).then_inc(sdexp_done, 1)
            for b in range(NBATCH):
                act.wait_ge(ctr_done, b + 1)
                if b:
                    act.wait_ge(inter_done, b)
                act.activation(c_t[:], psum[:, b % 2, :].rearrange("p (h e) -> p h e", h=MH), ACT.Copy).then_inc(ctr_copied, 1)
            act.wait_ge(c_store[0], 16 * IN_W)
            hi(PR_O, 0, 0, KD)
            hi(PR_O, 0, 1, KD)
            for pair in range(2):
                biased(PR_O + pair, 1, (KD, KD), sig_o[:, 2 * pair:2 * pair + 2, :], BO + 2 * pair, ACT.Sigmoid)
                act.wait_ge(hmean_done, pair + 1)
                act.activation(h_sq[:, 2 * pair:2 * pair + 2, :].rearrange("p h (a t) -> p (h a) t", a=2), psum[:, 4:8, 0:HALF],
                               ACT.Sqrt, bias=eps_c[:]).then_inc(hstd_ready, 1)
            act.wait_ge(c_store[1], 16 * (NBATCH - IN_W))
            act.wait_ge(outs, 16 * (2 * TB + 5))
            biased(PR_C, 2, (KD, KD), c_buf, BC)
            act.wait_ge(ym_full, 1)
            act.activation(ym_hi[:], h_t[:], ACT.Copy).then_inc(ymhi_ready, 1)
            biased(PR_C + 2, 4, (KD, WT), c_buf[:, 4:3 * WT, :], BC + 4)
            for g in range(2):
                if g:
                    hi(PR_MIX, 1, 0, KD)
                act.wait_ge(yc_full, g + 1)
                act.activation(yc_hi[:, 2 * g:2 * g + 2, :], c_buf[:, WT + 2 * g:WT + 2 * g + 2, :], ACT.Copy).then_inc(ychi_ready, 1)

            def mixing(i, last):
                for b in range(3):
                    act.wait_ge(gemm_done, i * 6 + ((PR_MIX + b) * 2 + 1))
                    act.wait_ge(psum_free[1], i * 3 + (PR_MIX + b - 2))
                    act.activation(gate[:, b, :].rearrange("p (a t) -> p a t", a=2), acc(0), ACT.Sigmoid,
                                   bias=cols1[:, bass.ds(i + (BG + KD * b), 1)]).then_inc(psum_free[0], 1)
                    hi(PR_MIX + b + 1, i * 3, 1, KD if last and b == 2 else WT)
                    if not (last and b == 2):
                        hi(PR_MIX + b + 2, i * 3, 0, KD)

            with act.Fori(0, KD - 1) as i:
                mixing(i, False)
            mixing(KD - 1, True)
            act.wait_ge(clast_done, 1)
            act.activation(c_out, psum[0:18, 5, :], ACT.Copy).then_inc(clast_copied, 1)

            def split_only(first, pairs, kts, kt_next):
                with act.Fori(0, pairs - 1) as i:
                    for slot in (0, 1):
                        hi(first, i + 1, slot, kts[slot])
                if kt_next:
                    for slot in (0, 1):
                        hi(first, pairs, slot, kt_next[slot])

            split_only(PR_WO, 4, (KD, KD), (KD, KD))
            act.wait_ge(conv_out, 32)
            norm_split(1)

            def up(f, i, kts):
                first = PR_FFN + f * PR_PART
                hi(first, i + 1, 0, kts[0])
                act.wait_ge(gemm_done, i * 2 + (first * 2 + 1))
                act.wait_ge(fconv_done, i + (f * FH + 1))
                act.activation(u_f[:, 2:2 + HALF], psum[:, 0, 0:HALF], ACT.Copy)
                act.activation(u_f[:, 2 + HALF:2 + TP], psum[:, 1, 0:TP - HALF], ACT.Copy)
                seqs = u_f[:, 2 + TP:UW].rearrange("p (b t) -> p b t", b=NBATCH)
                act.activation(seqs[:, :, 0:2], f_cols[:, bass.ds(i + f * FH, 1), :].rearrange("p o (b r) -> p (o b) r", b=NBATCH), ACT.Copy)
                act.activation(seqs[:, :, 2:2 + NEW], psum[:, 1, TP - HALF:HALF].rearrange("p (b t) -> p b t", b=NBATCH), ACT.Copy).then_inc(psum_free[0], 1)
                hi(first, i + 1, 1, kts[1])
                act.wait_ge(fconv_done, i + (f * FH + 2))
                act.activation(s_f[:], y_f[:], ACT.Sigmoid).then_inc(fsig_done, 1)

            act.wait_ge(fcols_ready, 1)
            for f in range(2):
                with act.Fori(0, FH - 1) as i:
                    up(f, i, (KD, KD))
                up(f, FH - 1, (FH, FH))
                split_only(PR_FFN + f * PR_PART + FH, 4, (FH, FH), (KD, PT) if f else (KD, KD))
            norm_split(2)
            for k in range(PT):
                act.wait_ge(p_done, k + 1)
                act.activation(p_hi[:, k, 0:TP], psum[:, 5 + 2 * k, :], ACT.Copy)
                act.activation(p_hi[:, k, TP:T], psum[:, 4 + 2 * k, 0:TS], ACT.Copy).then_inc(phi_ready, 1)
            hi(PR_PLE, 1, 0, KD)
            for g in range(6):
                n = min(4, FT - 4 * g)
                act.wait_ge(flast_done, g + 1)
                last = act.activation(f_out[:, 4 * g * P:(4 * g + n) * P], psum[0:18, 4 + g % 2, 0:n * P], ACT.Copy)
                last.then_inc(flast_copied, 1)

            def ple(i, ahead):
                act.wait_ge(gemm_done, i * 2 + (PR_PLE * 2 + 1))
                act.wait_ge(psum_free[1], i + PR_PLE)
                act.activation(gate_p[:, 0, :].rearrange("p (a t) -> p a t", a=2), acc(0), ACT.Sigmoid).then_inc(psum_free[0], 1)
                if ahead >= 1:
                    hi(PR_PLE, i + 1, 1, PT)
                if ahead >= 2:
                    hi(PR_PLE, i + 2, 0, KD)

            with act.Fori(0, KD - 2) as i:
                ple(i, 2)
            ple(KD - 2, 1)
            ple(KD - 1, 0)
            act.wait_ge(sum_done, KD + 3)
            act.activation(rstd[:].rearrange("p (a t) -> p a t", a=2), psum[:, 6:8, 0:HALF], ACT.Sqrt, bias=eps_c[:]).then_inc(std_ready, 1)
            for b in range(TB):
                rows = TS if b == QB else P
                act.wait_ge(ytr_done, 2 * b + 1)
                if b >= 2:
                    act.wait_ge(y_store[b % 2], 16 * (b // 2))
                act.activation(y_rows[0:rows, b % 2, 0:512], psum[0:rows, 2 * b % 4, :], ACT.Copy).then_inc(ytr_copied[0], 1)

        @block.tensor
        def _(pe):
            pe.wait_ge(cst_in, 16)
            pe.wait_ge(x_in, 16 * TB)
            for k in range(KD):
                s = k % 2
                if k >= 2:
                    pe.wait_ge(x_ready, k - 1)
                for b in range(QB):
                    pe.transpose(psum[:, 2 * s, b * P:(b + 1) * P], xs[:, b, k * P:(k + 1) * P], ident)
                pe.transpose(psum[:, 2 * s + 1, 0:TS], xs[0:TS, QB, k * P:(k + 1) * P], ident[0:TS, 0:TS]).then_inc(xt_done, 1)
            pe.wait_ge(rows_in, 16 * 13)
            pe.transpose(psum[:, 4, 0:ROWS1], rows1[0:ROWS1, :], ident[0:ROWS1, 0:ROWS1]).then_inc(cols_done, 1)
            pe.transpose(psum[:, 5, 0:ROWS2], rows2[0:ROWS2, :], ident[0:ROWS2, 0:ROWS2]).then_inc(cols_done, 1)

            def mean_square(number):
                pe.wait_ge(sq_ready, 2 * KD * (number + 1) - KD)
                for a in range(2):
                    last = pe.matmul(psum[:, 6 + a, 0:HALF], mean_d[:], sq[:, 1, a * HALF:(a + 1) * HALF], start=True, stop=True)
                last.then_inc(sum_done, 1)

            pe.wait_ge(consts_ready, 4)
            for k in range(KD):
                pe.wait_ge(sq_ready, k + 1)
                for a in range(2):
                    last = pe.matmul(psum[:, 6 + a, 0:HALF], mean_d[:], sq[:, k % 2, a * HALF:(a + 1) * HALF],
                                     start=(k == 0), stop=(k == KD - 1))
                last.then_inc(sum_done, 1)

            def chunk(first, i, slot, xhi, xlo, kt):
                pe.wait_ge(hi_ready, (i + first) * 2 + (slot + 1))
                pe.wait_ge(psum_free[slot], i + first)
                for a in range(2):
                    dst, cols = acc(slot)[:, a, :], slice(a * HALF, (a + 1) * HALF)
                    for k in range(kt):
                        pe.matmul(dst, w_hi[:, slot, k, :], xhi[:, k, cols], start=(k == 0), stop=False)
                        pe.matmul(dst, w_hi[:, slot, k, :], xlo[:, k, cols], start=False, stop=False)
                    if a == 0:
                        pe.wait_ge(lo_ready, (i + first) * 2 + (slot + 1))
                    for k in range(kt):
                        last = pe.matmul(dst, w_lo[:, slot, k, :], xhi[:, k, cols], start=False, stop=(k == kt - 1))
                last.then_inc(gemm_done, 1)

            def first_chunks(first, slots, kt, xhi, xlo, arrived, each):
                for slot in slots:
                    pe.wait_ge(lo_ready, first * 2 + slot + 1)
                    if first:
                        pe.wait_ge(psum_free[slot], first)
                for k in range(kt):
                    pe.wait_ge(arrived, each(k))
                    for slot in slots:
                        for a in range(2):
                            dst, cols = acc(slot)[:, a, :], slice(a * HALF, (a + 1) * HALF)
                            pe.matmul(dst, w_hi[:, slot, k, :], xhi[:, k, cols], start=(k == 0), stop=False)
                            pe.matmul(dst, w_hi[:, slot, k, :], xlo[:, k, cols], start=False, stop=False)
                            last = pe.matmul(dst, w_lo[:, slot, k, :], xhi[:, k, cols], start=False, stop=(k == kt - 1))
                        if k == kt - 1:
                            last.then_inc(gemm_done, 1)

            def chunks(first, start, pairs, xs2, kts):
                def one(i):
                    for slot in (0, 1):
                        chunk(first, i, slot, *xs2[slot], kts[slot])

                if pairs - start == 1:
                    one(start)
                else:
                    with pe.Fori(start, pairs) as i:
                        one(i)

            first_chunks(PR_A, (0, 1), KD, a_hi, a_lo, a_ready, lambda k: k + 1)
            pe.wait_ge(ws_ready, 1)
            pe.wait_ge(cols_ready, 2)
            for a in range(2):
                dst, cols = psum[0:96, 4 + a, 0:HALF], slice(a * HALF, (a + 1) * HALF)
                for k in range(KD):
                    pe.matmul(dst, ws_hi[:, k, :], a_hi[:, k, cols], start=(k == 0), stop=False)
                    pe.matmul(dst, ws_hi[:, k, :], a_lo[:, k, cols], start=False, stop=False)
                    last = pe.matmul(dst, ws_lo[:, k, :], a_hi[:, k, cols], start=False, stop=(k == KD - 1))
            last.then_inc(gates_done, 1)
            normed = (a_hi, a_lo)
            chunks(PR_A, 1, 6, (normed, normed), (KD, KD))

            pe.wait_ge(cum_ready, 1)
            for b in range(QB):
                pe.transpose(psum[:, 4, AH * b:AH * b + AH], lsg[0:AH, b * P:(b + 1) * P], ident[0:AH, 0:AH])
            pe.transpose(psum[0:TS, 4, AH * QB:AH * TB], lsg[0:AH, TP:T], ident[0:AH, 0:AH]).then_inc(small_done, 1)
            pe.wait_ge(small_ready, 1)
            pe.wait_ge(psum_free[0], 6)
            pe.wait_ge(psum_free[1], 6)
            for b in range(TB):
                rows = TS if b == QB else P
                for which in range(2):
                    n = 2 * b + which
                    if n >= 4:
                        pe.wait_ge(tok_copied, n - 3)
                    for f in range(WT):
                        last = pe.transpose(psum[0:rows, 4 + n % 4, f * P:(f + 1) * P],
                                            q_a[:, (2 - which) * WT + f, b * P:b * P + rows], ident)
                    last.then_inc(tok_done, 1)
            pe.wait_ge(tok_copied, 2 * TB)

            pe.wait_ge(q_scaled, 1)
            for h in range(AH + 1):
                for i in range(QB + 1):
                    for m in ((0, 1), (2,), (3,), (), ())[i] if h < AH else ():
                        n = 4 * h + m
                        b = QB - 1 - m
                        f, r = h // 2, slice(64 * (h % 2), 64 * (h % 2) + 64)
                        w = P * (b + 1)
                        bank = S_BANKS[m]
                        if n >= 4:
                            pe.wait_ge(exp_done, n - 3)
                        pe.matmul(psum[:, bank, 0:w], q_a[r, f, b * P:b * P + P], q_a[r, WT + f, 0:w], start=True, stop=False)
                        pe.matmul(psum[:, bank, w - P:w], ident, c("future_keys"), start=False, stop=False)
                        pe.matmul(psum[:, bank, 0:w], pick[:, h, :], ncum[:, 0:w], start=False, stop=True).then_inc(scores_done, 1)
                    g = h - 1
                    if g < 0:
                        continue
                    gf, gr = g // 2, slice(64 * (g % 2), 64 * (g % 2) + 64)
                    if i < QB:
                        m = 4 * g + i
                        pe.wait_ge(probs_ready, 4 * (g + 1))
                        if m >= 2:
                            pe.wait_ge(pt_copied, m - 1)
                        for b in range(i, QB):
                            o = P * (b * (b + 1) // 2 + i)
                            last = pe.transpose(psum[:, (6, 2)[m % 2], (b - i) * P:(b - i + 1) * P],
                                                probs[:, g % 2, o:o + P], ident)
                        last.then_inc(pt_done, 1)
                    if i >= 1:
                        m = 4 * g + i - 1
                        pe.wait_ge(pt_copied, m + 1)
                        if gf >= 2 and g % 2 == 0 and i == 1:
                            pe.wait_ge(o_lo, gf - 1)
                        pe.matmul(psum[gr, (7, 3)[gf % 2], P * (i - 1):TP], v_tok[:, i - 1, AD * g:AD * g + AD],
                                  pt[:, m % 2, 0:TP - P * (i - 1)], start=(i == 1), stop=(i == QB)).then_inc(pv_done, 1)
            pe.wait_ge(o_lo, 4)

            pe.wait_ge(qblk_ready, AH + 1)
            for p in range(NBATCH // 2 + 1):
                if p < NBATCH // 2:
                    if p >= 2:
                        pe.wait_ge(s_free, p - 1)
                    for b2 in range(2):
                        b = 2 * p + b2
                        pe.wait_ge(kp_in[b2], 64 * (p + 1))
                        rr = slice(64 * b2, 64 * b2 + 64)
                        for f in range(WT + 1):
                            if f < WT:
                                m = 4 * b + f
                                if m >= 2:
                                    pe.wait_ge(ktr_copied, m - 1)
                                for j in range(PAGES):
                                    last = pe.transpose(psum[:, 4 + m % 2, j * P:(j + 1) * P], kp[b2][:, j, f * P:(f + 1) * P], ident)
                                last.then_inc(ktr_done, 1)
                            if f:
                                g = f - 1
                                pe.wait_ge(ktr_copied, 4 * b + g + 1)
                                pe.matmul(psum[rr, 2 + p % 2, :], q_blk[:, g, b, :], kt_s[:, g, :], start=(g == 0), stop=(g == WT - 1)).then_inc(s_done, 1)
                    pe.wait_ge(lrep_ready, 2 * p + 4)
                    for j in range(PAGES):
                        pe.matmul(psum[:, 0, P * j:TP], lrep[:, j, :], tri[:, 0:TP - P * j], start=(j == 0), stop=(j == PAGES - 1))
                    if p:
                        pe.wait_ge(s_free, p)
                    for j in range(PAGES):
                        pe.matmul(psum[:, 1, 0:TS], lrep[:, j, :], ones[:, 0:TS], start=(j == 0), stop=False)
                    pe.matmul(psum[:, 1, 0:TS], lnew[:], c("seq_tri", TS), start=False, stop=True)
                    for b2 in range(2):
                        for g in range(WT):
                            last = pe.matmul(psum[64 * b2:64 * b2 + 64, 1, 64:64 + TS], q_blk[:, g, 2 * p + b2, :], k_new[:, g, :],
                                             start=(g == 0), stop=(g == WT - 1))
                    last.then_inc(cums_done, 1)
                if p:
                    y = p - 1
                    pe.wait_ge(sprobs, y + 1)
                    if y:
                        pe.wait_ge(so_lo, 2 * y)
                    pe.wait_ge(cums_ready, min(y + 2, NBATCH // 2))
                    for j in range(QB):
                        pe.transpose(psum[:, 6, j * P:(j + 1) * P], ls[:, j * P:(j + 1) * P], ident)
                    pe.transpose(psum[0:TS, 0, 0:P], ls[:, TP:T], ident).then_inc(spt_done, 1)
                    pe.wait_ge(spt_copied, y + 1)
                    for b2 in range(2):
                        pe.wait_ge(vp_in[b2], 64 * (y + 1))
                    for b2 in range(2):
                        rr = slice(64 * b2, 64 * b2 + 64)
                        for j in range(PAGES):
                            pe.matmul(psum[rr, 7, :], pts[:, j, rr], vp[:, b2, j, :], start=(j == 0), stop=False)
                        last = pe.matmul(psum[rr, 7, :], pts[0:TS, QB, rr], v_tok[0:TS, QB, :], start=False, stop=True)
                    last.then_inc(spv_done, 1)
                    pe.wait_ge(so_rows, y + 1)
                    for f in range(WT):
                        last = pe.transpose(psum[:, 6, f * P:(f + 1) * P], o_tok[:, f * P:(f + 1) * P], ident)
                    last.then_inc(sot_done, 1)
            pe.wait_ge(s_free, NBATCH // 2)
            pe.wait_ge(spt_copied, NBATCH // 2)
            pe.wait_ge(so_lo, NBATCH)
            chunks(PR_M, 0, 1, (normed, normed), (KD, KD))
            chunks(PR_M, 1, 6, (normed, normed), (KD, KD))
            pe.wait_ge(mrow_ready, 1)
            for h in range(MH):
                if h >= 2:
                    pe.wait_ge(mb_copied, h - 1)
                pe.matmul(psum[:, 4 + h % 2, :], pick[0:MH, h, :], rows_m[:, 3, 0:TP], start=True, stop=True).then_inc(mb_done, 1)
            for h in range(MH):
                pe.matmul(psum[:, 6, TS * h:TS * h + TS], pick[0:MH, h, :], rows_m[:, 3, TP:T], start=True, stop=True)
                pe.matmul(psum[:, 6, TS * (MH + h):TS * (MH + h) + TS], pick[0:MH, h, :], rows_m[:, 0, TP:T], start=True, stop=True)
                pe.matmul(psum[:, 7, TS * h:TS * h + TS], pick[0:MH, h, :], rows_m[:, 4, 0:TS], start=True, stop=True)
            for b in range(TB):
                rows = TS if b == QB else P
                last = pe.transpose(psum[0:rows, 7, 256 + MH * b:256 + MH * b + MH], rows_m[:, 1, b * P:b * P + rows], ident[0:MH, 0:MH])
            last.then_inc(mside_done, 1)
            pe.wait_ge(psum_free[0], PR_M + 6)
            pe.wait_ge(psum_free[1], PR_M + 6)
            pe.wait_ge(kscaled, 1)
            for b in range(TB):
                rows = TS if b == QB else P
                for which in range(2):
                    n = 2 * b + which
                    if n >= 4:
                        pe.wait_ge(mtok_copied, n - 3)
                    for f in range(WT):
                        last = pe.transpose(psum[0:rows, n % 4, f * P:(f + 1) * P], q_m[:, (2 - which) * WT + f, b * P:b * P + rows], ident)
                    last.then_inc(mtok_done, 1)
            pe.wait_ge(mtok_copied, 2 * TB)
            pe.wait_ge(mside_copied, 1)
            pe.wait_ge(mb_copied, MH)
            for n in range(4 * MH + 1):
                if n < 4 * MH:
                    h, j = n // 4, n % 4
                    if j == 0:
                        if h:
                            pe.wait_ge(em_ready, h)
                        pe.matmul(psum[:, 2, :], pick[0:MH, h, :], rows_m[:, 0, 0:TP], start=True, stop=True).then_inc(em_done, 1)
                    if n >= 2:
                        pe.wait_ge(mw_ready, n - 1)
                    pe.matmul(psum[:, 4 + n % 2, 0:TP - P * j], q_m[:, WT + h, P * j:P * j + P], q_m[:, h, P * j:TP],
                              start=True, stop=True).then_inc(mqk_done, 1)
                if n:
                    m = n - 1
                    h, j = m // 4, m % 4
                    pe.wait_ge(mw_ready, m + 1)
                    if h >= 2 and j == 0:
                        pe.wait_ge(h_ready, h - 1)
                    pe.matmul(psum[:, (6, 0)[h % 2], P * j:TP], vm_tok[:, j, h * MD:(h + 1) * MD], decay[:, m % 3, 0:TP - P * j], start=(j == 0), stop=(j == QB - 1))
                    pe.matmul(psum[:, (7, 1)[h % 2], P * j:TP], ones[:], decay[:, m % 3, 0:TP - P * j], start=(j == 0), stop=(j == QB - 1)).then_inc(mpv_done, 1)
            pe.wait_ge(kw_ready, QB)
            for h in range(MH):
                for b in range(QB):
                    last = pe.matmul(psum[:, 3, h * MD:(h + 1) * MD], vm_tok[:, b, h * MD:(h + 1) * MD], k_tok[:, b, h * MD:(h + 1) * MD],
                                     start=(b == 0), stop=(b == QB - 1))
            last.then_inc(cp_done, 1)
            for b in range(QB):
                last = pe.matmul(psum[0:1, 4, :], ones[:, 0:1], k_tok[:, b, :], start=(b == 0), stop=(b == QB - 1))
            last.then_inc(cp_done, 1)
            pe.wait_ge(n_in, 16)
            for h in range(MH):
                pe.transpose(psum[:, 5, NBATCH * h:NBATCH * h + NBATCH], n0[:, h * MD:(h + 1) * MD], ident[0:NBATCH, 0:NBATCH])
            pe.transpose(psum[0:NBATCH, 5, 64:64 + MH], a_last[:], ident[0:MH, 0:MH]).then_inc(nt_done, 1)
            pe.wait_ge(h_ready, MH)
            for h in range(MH):
                last = pe.matmul(psum[0:TS, 2, TS * h:TS * h + TS], q_m[:, WT + h, TP:T], q_m[:, h, TP:T], start=True, stop=True)
            last.then_inc(sqk_done, 1)
            pe.wait_ge(cp_copied, 2)
            for b in range(NBATCH + 1):
                if b < NBATCH:
                    if b == 0:
                        pe.wait_ge(c_in[0], 16 * EARLY)
                    if b == EARLY:
                        pe.wait_ge(c_in[1], 16 * (NBATCH - EARLY))
                    if b >= 2:
                        pe.wait_ge(ctr_copied, b - 1)
                    for h in range(MH):
                        last = pe.transpose(psum[:, b % 2, h * MD:(h + 1) * MD], c_st[b][:, h, :], ident)
                    last.then_inc(ctr_done, 1)
                    pe.wait_ge(kown_ready, b + 1)
                    if b >= 2:
                        pe.wait_ge(cnew_ready, b - 1)
                    for h in range(MH):
                        last = pe.matmul(psum[:, 3 + b % 2, h * MD:(h + 1) * MD], vm_tok[0:TS, QB, h * MD:(h + 1) * MD], k_own[:, b % 2, h, :], start=True, stop=True)
                    last.then_inc(cadd_done, 1)
                if b:
                    y = b - 1
                    pe.wait_ge(ctr_copied, y + 1)
                    for h in range(MH):
                        last = pe.matmul(psum[:, 6, TS * h + NEW * y:TS * h + NEW * y + NEW], c_t[:, h, :], q_m[:, h, TP + NEW * y:TP + NEW * y + NEW], start=True, stop=True)
                    last.then_inc(inter_done, 1)
            pe.wait_ge(qn_ready, 1)
            pe.wait_ge(sw_ready, 1)
            pe.matmul(psum[:, 7, 0:MH * TS], ones[:], q_m[:, 0:MH, 0:TS], start=True, stop=True)
            for h in range(MH):
                pe.matmul(psum[:, 7, 256 + TS * h:256 + TS * h + TS], ones[0:TS, :], w_s[:, h, :], start=True, stop=True)
                pe.matmul(psum[:, 6, 256 + TS * h:256 + TS * h + TS], vm_tok[0:TS, QB, h * MD:(h + 1) * MD], w_s[:, h, :], start=True, stop=True)
            for h in range(MH):
                last = pe.matmul(psum[0:NBATCH, 5, h * MD:(h + 1) * MD], wl_s[:, h, :], k_tok[0:TS, QB, h * MD:(h + 1) * MD], start=True, stop=True)
            last.then_inc(ssum_done, 1)
            pe.wait_ge(cnew_ready, NBATCH)
            for pair in range(2):
                chunks(PR_O, pair, pair + 1, (normed, normed), (KD, KD))
                pe.wait_ge(hsq_ready, 1)
                if pair:
                    pe.wait_ge(hstd_ready, 1)
                for n in range(4):
                    h, a = 2 * pair + n // 2, n % 2
                    last = pe.matmul(psum[:, 4 + n, 0:HALF], mean_h[:], h_sq[:, h, a * HALF:(a + 1) * HALF], start=True, stop=True)
                last.then_inc(hmean_done, 1)
            pe.wait_ge(hstd_ready, 2)
            chunks(PR_C, 0, 4, (normed, normed), (KD, KD))
            pe.wait_ge(conv_rows_in, 16)
            for f in range(WT):
                last = pe.transpose(psum[:, 4, 16 * f:16 * f + 16], c_rows[:, f * P:(f + 1) * P], ident[0:16, 0:16])
            last.then_inc(ctr2_done, 1)
            chunks(PR_C, 4, 6, (normed, normed), (KD, KD))
            pe.wait_ge(ym_ready, 1)
            with pe.Fori(0, KD) as i:
                for b, branch in enumerate(((ya_hi, ya_lo), (ym_hi, ym_lo), (yc_hi, yc_lo))):
                    chunk(PR_MIX + b, i * 3, 0, *normed, KD)
                    if b == 2:
                        pe.wait_ge(yc_ready, 1)
                    chunk(PR_MIX + b, i * 3, 1, *branch, WT)
            for f in range(WT):
                last = pe.transpose(psum[0:18, 5, f * P:(f + 1) * P], c_last[:, f, :], ident)
            last.then_inc(clast_done, 1)
            mixed = (mg_hi, mg_lo)
            first_chunks(PR_WO, (0, 1), KD, mg_hi, mg_lo, mix_step, lambda k: 4 * (k + 1))
            chunks(PR_WO, 1, 4, (mixed, mixed), (KD, KD))
            mean_square(1)

            pe.wait_ge(f_rows_in, 16)
            for t in range(FT):
                last = pe.transpose(psum[:, 4, 16 * t:16 * t + 16], f_rows[:, t * P:(t + 1) * P], ident[0:16, 0:16])
            last.then_inc(fcols_done, 1)
            first_chunks(PR_FFN, (0, 1), KD, a_hi, a_lo, a_ready, lambda k: KD + k + 1)
            hidden = (hid_hi, hid_lo)
            for f in range(2):
                chunks(PR_FFN + f * PR_PART, 1 - f, FH, (normed, normed), (KD, KD))
                first_chunks(PR_FFN + f * PR_PART + FH, (0, 1), FH, hid_hi, hid_lo, hid_ready, lambda k: f * FH + k + 1)
                chunks(PR_FFN + f * PR_PART + FH, 1, 4, (hidden, hidden), (FH, FH))
            mean_square(2)
            pe.wait_ge(p_rows_in, 16 * TB)
            pe.wait_ge(std_ready, 3)
            for k in range(PT):
                for b in range(QB):
                    pe.transpose(psum[:, 5 + 2 * k, b * P:(b + 1) * P], p_rows[:, b, k * P:(k + 1) * P], ident)
                pe.transpose(psum[:, 4 + 2 * k, 0:TS], p_rows[0:TS, QB, k * P:(k + 1) * P], ident[0:TS, 0:TS]).then_inc(p_done, 1)
            first_chunks(PR_PLE, (0,), KD, a_hi, a_lo, a_ready, lambda k: 2 * KD + k + 1)
            pe.wait_ge(p_ready, PT)
            chunk(PR_PLE, 0, 1, p_hi, p_lo, PT)
            for g in range(6):
                if g >= 2:
                    pe.wait_ge(flast_copied, g - 1)
                for t in range(4 * g, min(4 * g + 4, FT)):
                    last = pe.transpose(psum[0:18, 4 + g % 2, (t - 4 * g) * P:(t - 4 * g + 1) * P], f_last[:, t, :], ident)
                last.then_inc(flast_done, 1)
            chunks(PR_PLE, 1, 8, (normed, (p_hi, p_lo)), (KD, PT))
            mean_square(3)
            pe.wait_ge(psum_free[0], PR_END)
            pe.wait_ge(psum_free[1], PR_END)
            for n in range(2 * TB):
                b, half = n // 2, n % 2
                rows = TS if b == QB else P
                pe.wait_ge(yt_ready, 4 * half + 4)
                if n >= 4:
                    pe.wait_ge(ytr_copied[half], b - 1)
                for f in range(4):
                    last = pe.transpose(psum[0:rows, n % 4, f * P:(f + 1) * P], y_t[:, 4 * half + f, b * P:b * P + rows], ident)
                last.then_inc(ytr_done, 1)

        @block.vector
        def _(dve):
            steps = [0]

            def link(ins):
                steps[0] += 1
                ins.then_inc(dve_step, 1)
                dve.wait_ge(dve_step, steps[0])

            dve.memset(gbias[:], 0.0).then_inc(gzero, 1)
            dve.wait_ge(cols_done, 1)
            dve.tensor_copy(cols1[:], psum[:, 4, 0:ROWS1]).then_inc(cols_ready, 1)
            dve.wait_ge(cols_done, 2)
            dve.tensor_copy(cols2[:], psum[:, 5, 0:ROWS2]).then_inc(cols_ready, 1)
            dve.wait_ge(cols_ready, 2)

            def add_square(number, k, xk):
                dve.tensor_tensor(sq[:, 0:1, :], xk, xk, ALU.mult).then_inc(sq_ready, 1)
                dve.wait_ge(sq_ready, k * 2 + (2 * KD * number - KD + 1))
                dve.tensor_tensor(sq[:, 1, :], sq[:, 1, :], sq[:, 0, :], ALU.add).then_inc(sq_ready, 1)
                dve.wait_ge(sq_ready, k * 2 + (2 * KD * number - KD + 2))

            def norm(number, gain, last=False):
                dve.wait_ge(std_ready, number + 1)
                link(dve.reciprocal(rstd[:], rstd[:]))
                if last:
                    for k in range(KD):
                        dve.scalar_tensor_tensor(y_t[:, k, :], xT[:, k, :], cols1[:, gain + k:gain + k + 1], rstd[:],
                                                 ALU.mult, ALU.mult).then_inc(yt_ready, 1)
                    return
                for k in range(KD):
                    if k >= 2 or number:
                        dve.wait_ge(a_ready, KD * number + k - 1)
                    dve.scalar_tensor_tensor(hn[:, k % 2, :], xT[:, k, :], cols1[:, gain + k:gain + k + 1], rstd[:],
                                             ALU.mult, ALU.mult).then_inc(hn_ready, 1)

            for k in range(KD):
                dve.wait_ge(x_ready, k + 1)
                if k >= 2:
                    dve.wait_ge(sum_done, k - 1)
                dve.tensor_tensor(sq[:, k % 2, :], xT[:, k, :], xT[:, k, :], ALU.mult).then_inc(sq_ready, 1)
            norm(0, GMIX)
            dve.wait_ge(psum_free[0], 2)
            dve.wait_ge(psum_free[1], 2)
            dve.tensor_scalar(q_a[:, 0:WT, :], q_a[:, 0:WT, :], AD ** -0.5, None, ALU.mult).then_inc(q_scaled, 1)
            dve.wait_ge(gln_ready, 1)
            link(dve.scalar_tensor_tensor(lsg[:], gs[:], 0.0, ge[:], ALU.min, ALU.subtract))
            link(dve.tensor_tensor_scan(ncum[:], c("keep", AH), lsg[0:AH, :], 0.0, ALU.mult, ALU.add))
            dve.tensor_scalar(ncum[:], ncum[:], -1.0, None, ALU.mult).then_inc(cum_ready, 1)

            for n in range(4 * AH + 1):
                if n < 4 * AH:
                    i = n % 4
                    dve.wait_ge(scores_done, n + 1)
                    if n >= 4:
                        dve.wait_ge(exp_done, n - 3)
                    dve.tensor_reduce(nmax[:, i:i + 1], psum[:, S_BANKS[i], 0:P * (QB - i)], AX_X, ALU.max, negate=True).then_inc(nmax_ready, 1)
                if n:
                    m = n - 1
                    dve.wait_ge(exp_done, m + 1)
                    if m >= 4:
                        dve.wait_ge(probs_ready, m - 3)
                    dve.reciprocal(rinv[:, m % 4:m % 4 + 1], rsum[:, m % 4:m % 4 + 1]).then_inc(rinv_ready, 1)
                if n >= 12 and (n - 12) % 8 == 0 or n == 4 * AH:
                    f = (n - 12) // 8 if n < 4 * AH else 3
                    dve.wait_ge(o_hi, f + 1)
                    dve.tensor_tensor(ya_lo[:, f, 0:TP], psum[:, (7, 3)[f % 2], :], ya_hi[:, f, 0:TP].bitcast(F32), ALU.subtract).then_inc(o_lo, 1)

            for y in range(NBATCH // 2):
                dve.wait_ge(cums_ready, y + 1)
                dve.wait_ge(s_done, 8 * (y + 1))
                link(dve.tensor_tensor(tmp64[:], cums[:, TP:T], c("own_key")[:, TS * y:TS * (y + 1)], ALU.mult))
                link(dve.tensor_reduce(rinv[:, 1:2], tmp64[:], AX_X, ALU.add))
                if y:
                    dve.wait_ge(spt_done, y)
                dve.scalar_tensor_tensor(ls[:, 0:TP], psum[:, 2 + y % 2, :], rinv[:, 1:2], cums[:, 0:TP], ALU.add, ALU.subtract)
                link(dve.scalar_tensor_tensor(ls[:, TP:T], psum[:, 1, 64:64 + TS], rinv[:, 1:2], cums[:, TP:T],
                                              ALU.add, ALU.subtract))
                dve.tensor_tensor(ls[:, TP:T], ls[:, TP:T], c("new_keys")[:, TS * y:TS * (y + 1)], ALU.add).then_inc(s_free, 1)
                dve.wait_ge(s_free, y + 1)
                dve.tensor_reduce(nmax[:, 0:1], ls[:], AX_X, ALU.max, negate=True).then_inc(snmax, 1)
                dve.wait_ge(sexp, y + 1)
                link(dve.reciprocal(rinv[:, 0:1], rsum[:, 0:1]))
                dve.tensor_scalar(ls[:], ls[:], rinv[:, 0:1], None, ALU.mult).then_inc(sprobs, 1)
                for hh in range(2):
                    r = slice(64 * hh, 64 * hh + 64)
                    dve.wait_ge(so_hi, 2 * y + hh + 1)
                    dve.tensor_tensor(ya_lo[r, :, TP + 16 * y:TP + 16 * y + 16].rearrange("p f (b q) -> p f b q", b=2),
                                      own_heads(r, hh),
                                      ya_hi[r, :, TP + 16 * y:TP + 16 * y + 16].rearrange("p f (b q) -> p f b q", b=2).bitcast(F32),
                                      ALU.subtract).then_inc(so_lo, 1)
            link(dve.tensor_copy(rows_m[:, 0, :], lsg[64:64 + MH, :]))
            link(dve.tensor_copy(rows_m[:, 1, :], gs[32:32 + MH, :]))
            dve.engine_nop().then_inc(rows_ready, 1)
            link(dve.tensor_tensor_scan(rows_m[:, 2, :], c("keep", MH), rows_m[:, 0, :], 0.0, ALU.mult, ALU.add))
            link(dve.tensor_tensor(rows_m[:, 1, :], rows_m[:, 1, :], rows_m[:, 2, :], ALU.subtract))
            link(dve.tensor_copy(rows_m[:, 4, :], rows_m[:, 1, :]))
            dve.wait_ge(m0_in, 16)
            link(dve.tensor_scalar(rows_m[:, 4, 0:1], rows_m[:, 4, 0:1], 0.0, None, ALU.max))
            link(dve.tensor_tensor(rows_m[:, 4, TP:T:NEW], rows_m[:, 4, TP:T:NEW], m0[:], ALU.max))
            link(dve.tensor_tensor_scan(rows_m[:, 3, :], c("restart", MH), rows_m[:, 4, :], -BIG, ALU.add, ALU.max))
            link(dve.tensor_tensor(rows_m[:, 0, :], rows_m[:, 2, :], rows_m[:, 3, :], ALU.add))
            dve.tensor_tensor(rows_m[:, 4, 0:TS].rearrange("p (b t) -> p b t", b=NBATCH), m0[:].unsqueeze(2).broadcast_to([MH, NBATCH, NEW]),
                              rows_m[:, 3, TP:T].rearrange("p (b t) -> p b t", b=NBATCH), ALU.subtract).then_inc(mrow_ready, 1)
            dve.wait_ge(psum_free[0], PR_M + 4)
            dve.wait_ge(psum_free[1], PR_M + 4)
            dve.tensor_scalar(q_m[:, WT:2 * WT, :], q_m[:, WT:2 * WT, :], MD ** -0.5, None, ALU.mult).then_inc(kscaled, 1)
            dve.wait_ge(mside_copied, 1)
            dve.tensor_tensor(wl_p[:], g_col[:, 0:QB, :], m_all[:, :, TP - 1].unsqueeze(1).broadcast_to([P, QB, MH]), ALU.subtract).then_inc(wl_sub, 1)
            link(dve.tensor_tensor(wl_s[:], g_col[0:TS, QB, :].unsqueeze(2).broadcast_to([TS, MH, NBATCH]), m_all[0:TS, :, TP + NEW - 1:T:NEW], ALU.subtract))
            link(dve.tensor_scalar(wl_s[:], wl_s[:], 0.0, None, ALU.min))
            dve.tensor_tensor(wl_s[:], wl_s[:], c("not_seq", TS).unsqueeze(1).broadcast_to([TS, MH, NBATCH]), ALU.add).then_inc(wl_sub, 1)

            def decays(n):
                h, j = n // 4, n % 4
                w = TP - P * j
                if n >= 3:
                    dve.wait_ge(mpv_done, n - 2)
                link(dve.tensor_scalar(decay[:, n % 3, 0:w], m_all[:, h, P * j:TP], g_col[:, j, h:h + 1], 0.0, ALU.subtract, ALU.max))
                dve.tensor_tensor(decay[:, n % 3, 0:P], decay[:, n % 3, 0:P], c("past_rows"), ALU.add).then_inc(mdec_ready, 1)

            def finish_head(h):
                dve.wait_ge(mpv_done, 4 * (h + 1))
                dve.wait_ge(em_ready, h + 1)
                e = e_m[:, h % 2, :]
                link(dve.scalar_tensor_tensor(e, psum[:, (7, 1)[h % 2], :], -1.0, e, ALU.mult, ALU.max))
                link(dve.tensor_tensor(e, psum[:, (7, 1)[h % 2], :], e, ALU.max))
                link(dve.reciprocal(e, e))
                dve.tensor_tensor(h_t[:, h, 0:TP], psum[:, (6, 0)[h % 2], :], e, ALU.mult).then_inc(h_ready, 1)

            dve.wait_ge(mtok_done, 2 * TB)
            decays(0)
            for n in range(4 * MH):
                if n + 1 < 4 * MH:
                    decays(n + 1)
                w = TP - P * (n % 4)
                dve.wait_ge(mexp_done, n + 1)
                dve.wait_ge(mqk_done, n + 1)
                dve.tensor_tensor(decay[:, n % 3, 0:w], psum[:, 4 + n % 2, 0:w], decay[:, n % 3, 0:w], ALU.mult).then_inc(mw_ready, 1)
                if n % 4 == 1 and n > 4:
                    finish_head(n // 4 - 1)
            finish_head(MH - 1)

            gc_s = g_col[0:TS, QB, :].unsqueeze(2).broadcast_to([TS, MH, TS])
            link(dve.tensor_tensor(w_s[:], m_all[0:TS, :, TP:T], gc_s, ALU.subtract))
            link(dve.tensor_scalar(w_s[:], w_s[:], 0.0, None, ALU.max))
            dve.tensor_tensor(w_s[:], w_s[:], c("seq_past", TS).unsqueeze(1).broadcast_to([TS, MH, TS]), ALU.add).then_inc(sdec_ready, 1)
            dve.wait_ge(nt_copied, 1)
            q_s = q_m[:, 0:MH, TP:T].rearrange("p h (b t) -> p h b t", b=NBATCH)
            for h in range(MH):
                last = dve.tensor_tensor(q_m[:, h, 0:TS].rearrange("p (b t) -> p b t", b=NBATCH), q_s[:, h],
                                         n_t[:, h, :].unsqueeze(2).broadcast_to([P, NBATCH, NEW]), ALU.mult)
            last.then_inc(qn_ready, 1)
            dve.wait_ge(sdexp_done, 1)
            dve.wait_ge(sqk_done, 1)
            dve.tensor_tensor(w_s[:], psum[0:TS, 2, 0:MH * TS].rearrange("p (h t) -> p h t", h=MH), w_s[:], ALU.mult).then_inc(sw_ready, 1)
            for b in range(NBATCH):
                dve.wait_ge(ctr_done, b + 1)
                cb = c_st[b][:]
                link(dve.tensor_tensor(cb, cb, a_s[:, :, NEW * b + NEW - 1:NEW * b + NEW].broadcast_to([P, MH, MD]), ALU.mult))
                dve.wait_ge(cadd_done, b + 1)
                dve.tensor_tensor(cb, psum[:, 3 + b % 2, :].rearrange("p (h e) -> p h e", h=MH), cb, ALU.add).then_inc(cnew_ready, 1)
            n_v = n0[:].rearrange("p (h e) -> p h e", h=MH)
            link(dve.tensor_tensor(n_v, n_v, a_last_t[:].unsqueeze(2).broadcast_to([NBATCH, MH, MD]), ALU.mult))
            dve.wait_ge(ssum_done, 1)
            dve.tensor_tensor(n0[:], psum[0:NBATCH, 5, :], n0[:], ALU.add).then_inc(n_new_ready, 1)
            dve.wait_ge(inter_done, NBATCH)

            def quad(bank, o):
                return psum[:, bank, o:o + MH * TS].rearrange("p (h t) -> p h t", h=MH)

            num, den = q_m[:, 0:MH, TS:2 * TS], q_m[:, 0:MH, 2 * TS:3 * TS]
            link(dve.tensor_tensor(num, quad(6, 0), a_s[:], ALU.mult))
            link(dve.tensor_tensor(num, quad(6, 256), num, ALU.add))
            link(dve.tensor_tensor(den, quad(7, 0), a_s[:], ALU.mult))
            link(dve.tensor_tensor(den, quad(7, 256), den, ALU.add))
            link(dve.scalar_tensor_tensor(e_ms[:], den, -1.0, e_ms[:], ALU.mult, ALU.max))
            link(dve.tensor_tensor(den, den, e_ms[:], ALU.max))
            link(dve.reciprocal(den, den))
            link(dve.tensor_tensor(h_t[:, :, TP:T], num, den, ALU.mult))
            dve.tensor_tensor(h_sq[:], h_t[:], h_t[:], ALU.mult).then_inc(hsq_ready, 1)
            dve.wait_ge(hstd_ready, 2)
            link(dve.reciprocal(h_sq[:], h_sq[:]))
            link(dve.tensor_tensor(h_t[:], h_t[:], h_sq[:], ALU.mult))
            dve.wait_ge(psum_free[0], PR_O + 2)
            dve.wait_ge(psum_free[1], PR_O + 2)
            for h in range(MH):
                last = dve.scalar_tensor_tensor(h_t[:, h, :], h_t[:, h, :], cols1[:, GMH + h:GMH + h + 1], sig_o[:, h, :], ALU.mult, ALU.mult)
            last.then_inc(ym_full, 1)
            dve.wait_ge(ymhi_ready, 1)
            dve.tensor_tensor(ym_lo[:], h_t[:], ym_hi[:].bitcast(F32), ALU.subtract).then_inc(ym_ready, 1)
            link(dve.memset(u_c[:, :, 0:2], 0.0))
            dve.wait_ge(ctr2_done, 1)

            def seqs(x):
                return x.rearrange("p (b t) -> p b t", b=NBATCH)

            def seqs4(x):
                return x.rearrange("p f (b t) -> p f b t", b=NBATCH)

            us = seqs4(u_c[:, :, 2 + TP:UW])
            dve.tensor_copy(us[:, :, :, 0:2], psum[:, 4, 0:16 * WT].rearrange("p (f b r) -> p f b r", f=WT, b=NBATCH))
            for g in range(2):
                for slot in (0, 1):
                    dve.wait_ge(psum_free[slot], PR_C + 5 + g)
                fs2 = slice(2 * g, 2 * g + 2)
                b_in, c_in2, x_in2 = (c_buf[:, WT * n + 2 * g:WT * n + 2 * g + 2, :] for n in range(3))
                dve.tensor_tensor(u_c[:, fs2, 2:2 + TP], c_in2[:, :, 0:TP], x_in2[:, :, 0:TP], ALU.mult)
                link(dve.tensor_tensor(us[:, fs2, :, 2:2 + NEW], seqs4(c_in2[:, :, TP:T]), seqs4(x_in2[:, :, TP:T]), ALU.mult))
                dve.tensor_copy(c_last[:, fs2, 0:2], u_c[:, fs2, TP:TP + 2])
                dve.tensor_copy(c_last[:, fs2, 2:18].rearrange("p f (b r) -> p f b r", b=NBATCH), us[:, fs2, :, NEW:NEW + 2])
                for j in (2, 1, 0):
                    for f in (2 * g, 2 * g + 1):
                        w = cols1[:, WSC + WT * j + f:WSC + WT * j + f + 1]
                        y = c_buf[:, WT + f, :]
                        if j == 2:
                            dve.tensor_scalar(y[:, 0:TP], u_c[:, f, 2:2 + TP], w, None, ALU.mult)
                            last = dve.tensor_scalar(seqs(y[:, TP:T]), us[:, f, :, 2:2 + NEW], w, None, ALU.mult)
                        else:
                            dve.scalar_tensor_tensor(y[:, 0:TP], u_c[:, f, j:j + TP], w, y[:, 0:TP], ALU.mult, ALU.add)
                            last = dve.scalar_tensor_tensor(seqs(y[:, TP:T]), us[:, f, :, j:j + NEW], w, seqs(y[:, TP:T]), ALU.mult, ALU.add)
                    link(last)
                dve.tensor_tensor(c_in2, c_in2, b_in, ALU.mult).then_inc(yc_full, 1)
            for g in range(2):
                fs2 = slice(2 * g, 2 * g + 2)
                dve.wait_ge(ychi_ready, g + 1)
                last = dve.tensor_tensor(yc_lo[:, fs2, :], c_buf[:, WT + 2 * g:WT + 2 * g + 2, :], yc_hi[:, fs2, :].bitcast(F32), ALU.subtract)
            last.then_inc(yc_ready, 1)

            def halves(x):
                return x.rearrange("p (a t) -> p a t", a=2)

            with dve.Fori(0, KD) as i:
                for b in range(3):
                    dve.wait_ge(gemm_done, i * 6 + ((PR_MIX + b) * 2 + 2))
                    dve.wait_ge(psum_free[0], i * 3 + (PR_MIX + b + 1))
                    dve.tensor_tensor(halves(mix[:, min(b, 1), :]), acc(1), halves(gate[:, b, :]), ALU.mult).then_inc(psum_free[1], 1)
                    dve.wait_ge(psum_free[1], i * 3 + (PR_MIX + b + 1))
                    if b:
                        dve.tensor_tensor(mix[:, 0, :], mix[:, 0, :], mix[:, 1, :], ALU.add).then_inc(mix_step, 1)
                        dve.wait_ge(mix_step, i * 4 + b)
                whole = mix[:, 0:1, :]
                dve.tensor_copy(mg_hi[:, bass.ds(i, 1), :], whole).then_inc(mix_step, 1)
                dve.wait_ge(mix_step, i * 4 + 3)
                dve.tensor_tensor(mg_lo[:, bass.ds(i, 1), :], whole, mg_hi[:, bass.ds(i, 1), :].bitcast(F32), ALU.subtract).then_inc(mix_step, 1)
                dve.wait_ge(mix_step, i * 4 + 4)

            def add_to_stream(first, pairs, number):
                if number:
                    link(dve.memset(sq[:, 1, :], 0.0))
                with dve.Fori(0, pairs) as i:
                    for slot in (0, 1):
                        dve.wait_ge(gemm_done, i * 2 + (first * 2 + slot + 1))
                        xk = xT[:, bass.ds(i * 2 + slot, 1), :].rearrange("p o (a t) -> p (o a) t", a=2)
                        dve.tensor_tensor(xk, acc(slot), xk, ALU.add).then_inc(psum_free[slot], 1)
                        if number:
                            dve.wait_ge(psum_free[slot], i + (first + 1))
                            add_square(number, i * 2 + slot, xT[:, bass.ds(i * 2 + slot, 1), :])

            add_to_stream(PR_WO, 4, 1)
            norm(1, GFFN)
            dve.wait_ge(fcols_done, 1)
            dve.tensor_copy(f_cols[:], psum[:, 4, 0:16 * FT].rearrange("p (t r) -> p t r", t=FT)).then_inc(fcols_ready, 1)

            dve.memset(u_f[:, 0:2], 0.0).then_inc(fconv_done, 1)
            fs = seqs(u_f[:, 2 + TP:UW])
            for f in range(2):
                first = PR_FFN + f * PR_PART
                with dve.Fori(0, FH) as i:
                    t0 = f * FH

                    def col(j):
                        return cols2[:, bass.ds(i + (j * FT + t0), 1)]

                    dve.wait_ge(psum_free[0], i + (first + 1))
                    lt = f_last[:, bass.ds(i + t0, 1), :]
                    dve.tensor_copy(lt[:, :, 0:2], u_f[:, TP:TP + 2].unsqueeze(1))
                    dve.tensor_copy(lt[:, :, 2:18].rearrange("p o (b r) -> p (o b) r", b=NBATCH), fs[:, :, NEW:NEW + 2])
                    dve.tensor_scalar(y_f[:, 0:TP], u_f[:, 2:2 + TP], col(2), col(3), ALU.mult, ALU.add)
                    dve.tensor_scalar(seqs(y_f[:, TP:T]), fs[:, :, 2:2 + NEW], col(2), col(3), ALU.mult, ALU.add).then_inc(fstep, 1)
                    dve.wait_ge(fstep, i * 4 + (4 * t0 + 1))
                    for j in (1, 0):
                        dve.scalar_tensor_tensor(y_f[:, 0:TP], u_f[:, j:j + TP], col(j), y_f[:, 0:TP], ALU.mult, ALU.add)
                        last = dve.scalar_tensor_tensor(seqs(y_f[:, TP:T]), fs[:, :, j:j + NEW], col(j), seqs(y_f[:, TP:T]), ALU.mult, ALU.add)
                        if j:
                            last.then_inc(fstep, 1)
                            dve.wait_ge(fstep, i * 4 + (4 * t0 + 2))
                        else:
                            last.then_inc(fconv_done, 1)
                    dve.wait_ge(fsig_done, i + (t0 + 1))
                    dve.tensor_tensor(y_f[:], y_f[:], s_f[:], ALU.mult).then_inc(fstep, 1)
                    dve.wait_ge(fstep, i * 4 + (4 * t0 + 3))
                    dve.wait_ge(gemm_done, i * 2 + (first * 2 + 2))
                    dve.tensor_tensor(halves(y_f[:]), acc(1), halves(y_f[:]), ALU.mult).then_inc(psum_free[1], 1)
                    dve.wait_ge(psum_free[1], i + (first + 1))
                    dve.tensor_copy(hid_hi[:, bass.ds(i, 1), :], y_f[:].unsqueeze(1)).then_inc(fstep, 1)
                    dve.wait_ge(fstep, i * 4 + (4 * t0 + 4))
                    dve.tensor_tensor(hid_lo[:, bass.ds(i, 1), :], y_f[:].unsqueeze(1), hid_hi[:, bass.ds(i, 1), :].bitcast(F32), ALU.subtract).then_inc(hid_ready, 1)
                    dve.wait_ge(hid_ready, i + (t0 + 1))
                add_to_stream(first + FH, 4, 2 * f)
            norm(2, GPLE)
            for k in range(PT):
                dve.wait_ge(phi_ready, k + 1)
                dve.tensor_tensor(p_lo[:, k, 0:TP], psum[:, 5 + 2 * k, :], p_hi[:, k, 0:TP].bitcast(F32), ALU.subtract)
                dve.tensor_tensor(p_lo[:, k, TP:T], psum[:, 4 + 2 * k, 0:TS], p_hi[:, k, TP:T].bitcast(F32), ALU.subtract).then_inc(p_ready, 1)
            link(dve.memset(sq[:, 1, :], 0.0))
            with dve.Fori(0, KD) as i:
                dve.wait_ge(psum_free[0], i + (PR_PLE + 1))
                dve.wait_ge(gemm_done, i * 2 + (PR_PLE * 2 + 2))
                dve.tensor_tensor(halves(emb[:]), acc(1), halves(gate_p[:, 0, :]), ALU.mult).then_inc(psum_free[1], 1)
                dve.wait_ge(psum_free[1], i + (PR_PLE + 1))
                xk = xT[:, bass.ds(i, 1), :]
                dve.tensor_tensor(xk, xk, emb[:].unsqueeze(1), ALU.add).then_inc(xple_ready, 1)
                dve.wait_ge(xple_ready, i + 1)
                add_square(3, i, xk)
            norm(3, GFIN, last=True)

            for b in range(TB):
                rows = TS if b == QB else P
                dve.wait_ge(ytr_done, 2 * b + 2)
                if b >= 2:
                    dve.wait_ge(y_store[b % 2], 16 * (b // 2))
                dve.tensor_copy(y_rows[0:rows, b % 2, 512:1024], psum[0:rows, (2 * b + 1) % 4, :]).then_inc(ytr_copied[1], 1)


_INS = ["x_prompt", "x_sample", "cache_k", "cache_v", "cache_logf", "state_mlstm_C", "state_mlstm_n", "state_mlstm_m",
        "state_conv", "state_ffn_conv", "page_table", "p_prompt", "p_sample", "w_in", "b_in", "g_mix", "g_mhead",
        "w_sconv", "w_oa", "w_om", "w_oc", "w_o", "g_ffn", "w_up", "w_fconv", "b_fconv", "w_down", "g_ple",
        "w_ple_gate", "w_ple", "g_final"]
_OUTS = [("y_prompt", (1, 512, 1024)), ("y_sample", (8, 8, 1024)),
         ("k_p", (1, 512, 1, 8, 64)), ("v_p", (1, 512, 1, 8, 64)), ("logf_p", (1, 512, 1, 8)),
         ("C_p", (1, 1, 4, 128, 128)), ("n_p", (1, 1, 4, 128)), ("m_p", (1, 1, 4)),
         ("conv_p", (1, 1, 2, 512)), ("ffn_p", (1, 1, 2, 2816)),
         ("k_s", (8, 8, 1, 8, 64)), ("v_s", (8, 8, 1, 8, 64)), ("logf_s", (8, 8, 1, 8)),
         ("C_s", (8, 1, 4, 128, 128)), ("n_s", (8, 1, 4, 128)), ("m_s", (8, 1, 4)),
         ("conv_s", (8, 1, 2, 512)), ("ffn_s", (8, 1, 2, 2816))]


def kernel(**inputs):
    import numpy as _np
    import concourse.bacc as _bacc
    from concourse import mybir as _mybir
    from concourse.bass_utils import run_bass_kernel_spmd as _run

    nc = _bacc.Bacc("TRN2", target_bir_lowering=False, num_devices=1)
    arrays, d = {}, {}
    for name in _INS:
        a = _np.ascontiguousarray(inputs[name])
        arrays[f"in_{name}"] = a
        d[name] = nc.dram_tensor(f"in_{name}", a.shape, _mybir.dt.from_np(a.dtype), kind="ExternalInput").ap()
    parts = tables()
    at, ncst = layout(parts)
    arrays["in_cst"] = _np.concatenate([_np.asarray(a, _np.float32) for a in parts.values()], 1)
    d["cst"] = nc.dram_tensor("in_cst", (P, ncst), F32, kind="ExternalInput").ap()
    for name, shape in _OUTS:
        d[name] = nc.dram_tensor(f"out_{name}", shape, F32, kind="ExternalOutput").ap()
    build(nc, d, at, ncst)
    r = _run(nc, [arrays], core_ids=[0])
    return tuple(r.results[0][f"out_{name}"] for name, _ in _OUTS)
```
